# Optimizing a Trainium2 kernel written in Bass

```python
import math, functools
import jax, jax.numpy as jnp
from jax import lax
import numpy as np

D_MODEL = 1024
BATCH = 1
SEQ = 512
DEPTH = 1
DEC_BATCH = 8
DEC_SEQ = 4
PAST_LEN = 4096
PAGE_SIZE = 128

GLA_HEADS = 4
GLA_DV = D_MODEL // (2 * GLA_HEADS)
GLA_DK = GLA_DV // 2
GLA_RANK = 16
GLA_TAU = 16.0
GLA_CHUNK = 64
GLA_WIDTH = GLA_HEADS * GLA_DV
NSA_HEADS = 8
NSA_KV_HEADS = 2
NSA_GROUP = NSA_HEADS // NSA_KV_HEADS
NSA_HEAD_DIM = D_MODEL // (2 * NSA_HEADS)
NSA_WIDTH = NSA_HEADS * NSA_HEAD_DIM
CMP_BLK = 32
CMP_STRIDE = 16
CMP_HIDDEN = 2 * NSA_HEAD_DIM
SLC_BLK = 64
SLC_TOP_N = 16
WINDOW = 512
NSA_QBLK = 64
FORCE_BONUS = 1e4
NEG = -1e30
MIX_WIDTH = GLA_WIDTH + NSA_WIDTH
D_FF = -(-8 * D_MODEL // (3 * 256)) * 256
ALPHA = (2 * DEPTH) ** 0.25
BETA = (8 * DEPTH) ** -0.25
KV_W = 2 * NSA_KV_HEADS * NSA_HEAD_DIM
IN_SIZES = (GLA_HEADS * GLA_DK, GLA_HEADS * GLA_DK, GLA_WIDTH, GLA_RANK, GLA_WIDTH,
            NSA_WIDTH, KV_W, KV_W, KV_W, 3 * NSA_HEADS)
IN_WIDTH = sum(IN_SIZES)
IN_SPLITS = tuple(int(v) for v in np.cumsum(IN_SIZES)[:-1])

kernel_name = 'hybrid_gla_nsa_deepnorm_adaln_step'

def layer_norm(x, g, b, eps=1e-5):
    xf = x.astype(jnp.float32)
    mu = jnp.mean(xf, axis=-1, keepdims=True)
    xc = xf - mu
    var = jnp.mean(xc * xc, axis=-1, keepdims=True)
    return (xc * lax.rsqrt(var + eps) * g.astype(jnp.float32) + b.astype(jnp.float32)).astype(x.dtype)

def masked_softmax(s, mask):
    s = jnp.where(mask, s.astype(jnp.float32), NEG)
    e = jnp.where(mask, jnp.exp(s - jnp.max(s, axis=-1, keepdims=True)), 0.0)
    return e / jnp.maximum(jnp.sum(e, axis=-1, keepdims=True), 1e-30)

def gla_chunked(q, k, v, log_a, s0):
    f32 = jnp.float32
    B, L, H, _ = q.shape
    c = min(GLA_CHUNK, L)
    pad = (-L) % c

    def prep(t):
        t = jnp.pad(t.astype(f32), ((0, 0), (0, pad), (0, 0), (0, 0)))
        return t.reshape(B, -1, c, H, t.shape[-1]).transpose(1, 0, 3, 2, 4)

    qs, ks, vs, gs = prep(q), prep(k), prep(v), prep(log_a)
    causal = jnp.tril(jnp.ones((c, c), bool))[:, :, None]

    def step(S, inp):
        qc, kc, vc, gc = inp
        b = jnp.cumsum(gc, axis=2)
        o_inter = jnp.einsum('bhcd,bhde->bhce', qc * jnp.exp(b), S)
        diff = jnp.where(causal, b[:, :, :, None, :] - b[:, :, None, :, :], -jnp.inf)
        att = jnp.einsum('bhid,bhjd,bhijd->bhij', qc, kc, jnp.exp(diff))
        o = o_inter + jnp.einsum('bhij,bhje->bhie', att, vc)
        b_last = b[:, :, -1:, :]
        S = jnp.exp(b_last[:, :, 0, :])[..., None] * S + jnp.einsum('bhcd,bhce->bhde', kc * jnp.exp(b_last - b), vc)
        return S, o

    S, o = lax.scan(step, s0.astype(f32), (qs, ks, vs, gs))
    o = o.transpose(1, 0, 3, 2, 4).reshape(B, -1, H, o.shape[-1])[:, :L]
    return o, S

def compress_blocks(kv, pe, w1, b1, w2):
    B, T = kv.shape[:2]
    n_seg = T // CMP_STRIDE
    r = CMP_BLK // CMP_STRIDE
    nc = n_seg - r + 1
    seg = kv[:, :n_seg * CMP_STRIDE].reshape(B, n_seg, CMP_STRIDE, 2, NSA_KV_HEADS, NSA_HEAD_DIM)
    w1r = w1.reshape(2, r, CMP_STRIDE, NSA_HEAD_DIM, CMP_HIDDEN)
    proj = jnp.einsum('bnscgd,cmsdh->mbncgh', seg, w1r)
    pe_bias = jnp.einsum('pcd,cpdh->ch', pe, w1.reshape(2, CMP_BLK, NSA_HEAD_DIM, CMP_HIDDEN))
    h = sum(proj[m][:, m:m + nc] for m in range(r)) + (pe_bias + b1)[None, None, :, None, :]
    out = jnp.einsum('bncgh,chd->bncgd', jax.nn.gelu(h), w2)
    t_end = jnp.arange(nc, dtype=jnp.int32) * CMP_STRIDE + CMP_BLK - 1
    return out[:, :, 0], out[:, :, 1], t_end

def to_blocks(k):
    B, T = k.shape[:2]
    k = jnp.pad(k, ((0, 0), (0, (-T) % SLC_BLK), (0, 0), (0, 0)))
    return k.reshape(B, -1, SLC_BLK, NSA_KV_HEADS, NSA_HEAD_DIM).transpose(0, 3, 1, 2, 4)

def overlap_matrix(nc, nb):
    i = jnp.arange(nc)[:, None] * CMP_STRIDE
    j = jnp.arange(nb)[None, :] * SLC_BLK
    return ((i < j + SLC_BLK) & (i + CMP_BLK > j)).astype(jnp.float32)

def nsa_core(qg, tq, kc, vc, tc_end, kb, vb, kw, vw, tw, gates):
    f32 = jnp.float32
    B, Q, G, R, D = qg.shape
    nb = kb.shape[2]
    s_c = jnp.einsum('bqgrd,bngd->bqgrn', qg, kc.astype(f32))
    p_c = masked_softmax(s_c, (tc_end[None, :] <= tq[:, None])[None, :, None, None, :])
    o_c = jnp.einsum('bqgrn,bngd->bqgrd', p_c, vc.astype(f32))
    imp = jnp.einsum('bqgn,nj->bqgj', p_c.sum(axis=3), overlap_matrix(kc.shape[1], nb))
    j = jnp.arange(nb)[None, :]
    cur = (tq // SLC_BLK)[:, None]
    valid = j * SLC_BLK <= tq[:, None]
    forced = (j == 0) | (j == cur) | (j == cur - 1)
    score = jnp.where(valid[None, :, None, :], imp + FORCE_BONUS * forced[None, :, None, :].astype(f32), -jnp.inf)
    _, idx = lax.top_k(score, min(SLC_TOP_N, nb))
    take = jax.vmap(jax.vmap(lambda blocks, ids: blocks[ids]))
    idx_t = idx.transpose(0, 2, 1, 3)
    ks = take(kb, idx_t)
    vs = take(vb, idx_t)
    s_s = jnp.einsum('bqgrd,bgqnkd->bqgrnk', qg, ks.astype(f32))
    pos = idx[..., None] * SLC_BLK + jnp.arange(SLC_BLK)
    m_s = (pos <= tq[None, :, None, None, None]).reshape(B, Q, G, 1, -1)
    p_s = masked_softmax(s_s.reshape(B, Q, G, R, -1), m_s).reshape(s_s.shape)
    o_s = jnp.einsum('bqgrnk,bgqnkd->bqgrd', p_s, vs.astype(f32))
    s_w = jnp.einsum('bqgrd,bwgd->bqgrw', qg, kw.astype(f32))
    m_w = (tw[None, :] <= tq[:, None]) & (tw[None, :] > tq[:, None] - WINDOW) & (tw[None, :] >= 0)
    p_w = masked_softmax(s_w, m_w[None, :, None, None, :])
    o_w = jnp.einsum('bqgrw,bwgd->bqgrd', p_w, vw.astype(f32))
    g = gates.reshape(B, Q, G, R, 3)
    o = g[..., 0:1] * o_c + g[..., 1:2] * o_s + g[..., 2:3] * o_w
    return o.reshape(B, Q, G * R * D)

def nsa_prompt(q, kv_c, kv_s, kv_w, gates, pe, w1, b1, w2):
    B, L = q.shape[:2]
    qg = q.reshape(B, L, NSA_KV_HEADS, NSA_GROUP, NSA_HEAD_DIM).astype(jnp.float32) * NSA_HEAD_DIM ** -0.5
    kc, vc, tc_end = compress_blocks(kv_c, pe, w1, b1, w2)
    kb, vb = to_blocks(kv_s[:, :, 0]), to_blocks(kv_s[:, :, 1])
    kw_pad = jnp.pad(kv_w, ((0, 0), (WINDOW, 0), (0, 0), (0, 0), (0, 0)))
    qb = min(NSA_QBLK, L)

    def block(i):
        s0 = i * qb
        tq = s0 + jnp.arange(qb, dtype=jnp.int32)
        tw = s0 - WINDOW + jnp.arange(WINDOW + qb, dtype=jnp.int32)
        qi = lax.dynamic_slice_in_dim(qg, s0, qb, axis=1)
        gi = lax.dynamic_slice_in_dim(gates, s0, qb, axis=1)
        wi = lax.dynamic_slice_in_dim(kw_pad, s0, WINDOW + qb, axis=1)
        return nsa_core(qi, tq, kc, vc, tc_end, kb, vb, wi[:, :, 0], wi[:, :, 1], tw, gi)

    o = lax.map(block, jnp.arange(L // qb, dtype=jnp.int32))
    o = o.transpose(1, 0, 2, 3).reshape(B, L, NSA_WIDTH)
    return o, kv_w[:, L - min(WINDOW, L):]

def nsa_sample(cmp_past, slc_past, win_past, q, kv_c, kv_s, kv_w, gates, pe, w1, b1, w2):
    B, S = q.shape[:2]
    past_len = cmp_past.shape[1]
    qg = q.reshape(B, S, NSA_KV_HEADS, NSA_GROUP, NSA_HEAD_DIM).astype(jnp.float32) * NSA_HEAD_DIM ** -0.5
    kc, vc, tc_end = compress_blocks(jnp.concatenate([cmp_past, kv_c], axis=1), pe, w1, b1, w2)
    slc_all = jnp.concatenate([slc_past, kv_s], axis=1)
    kb, vb = to_blocks(slc_all[:, :, 0]), to_blocks(slc_all[:, :, 1])
    win_all = jnp.concatenate([win_past, kv_w], axis=1)
    wb = win_past.shape[1]
    tw = past_len - wb + jnp.arange(wb + S, dtype=jnp.int32)
    tq = past_len + jnp.arange(S, dtype=jnp.int32)
    o = nsa_core(qg, tq, kc, vc, tc_end, kb, vb, win_all[:, :, 0], win_all[:, :, 1], tw, gates)
    return o, win_all[:, S:]

def decoder_layer(x, c, s0, nsa_fn, w_ada, b_ada, w_in, gla_w_a2, gla_b_a, gla_norm_g, cmp_pe, cmp_w1, cmp_b1,
                  cmp_w2, w_o, ln1_g, ln1_b, w_ffn_in, w_ffn_out, ln2_g, ln2_b):
    f32 = jnp.float32
    B, L, _ = x.shape
    mod = jnp.einsum('bd,dm->bm', jax.nn.silu(c), w_ada) + b_ada
    sh1, sc1, ga1, sh2, sc2, ga2 = [m[:, None, :] for m in jnp.split(mod, 6, axis=-1)]
    u = x * (1 + sc1) + sh1
    z = jnp.einsum('bld,dp->blp', u, w_in)
    q_g, k_g, v_g, a_g, r_g, q_n, kv_c, kv_s, kv_w, g_n = jnp.split(z, IN_SPLITS, axis=-1)
    log_a = jax.nn.log_sigmoid((jnp.einsum('blr,rk->blk', a_g, gla_w_a2) + gla_b_a).astype(f32)) / GLA_TAU
    hs = (B, L, GLA_HEADS, -1)
    o_g, s_new = gla_chunked(q_g.reshape(hs) * GLA_DK ** -0.5, k_g.reshape(hs), v_g.reshape(hs), log_a.reshape(hs), s0)
    o_g = o_g * lax.rsqrt(jnp.mean(o_g * o_g, axis=-1, keepdims=True) + 1e-6) * gla_norm_g.astype(f32)
    o_g = o_g.reshape(B, L, GLA_WIDTH) * jax.nn.silu(r_g.astype(f32))
    kvs = (B, L, 2, NSA_KV_HEADS, NSA_HEAD_DIM)
    kv_c, kv_s, kv_w = kv_c.reshape(kvs), kv_s.reshape(kvs), kv_w.reshape(kvs)
    gates = jax.nn.sigmoid(g_n.astype(f32))
    o_n, win_new = nsa_fn(q_n.reshape(B, L, NSA_HEADS, NSA_HEAD_DIM), kv_c, kv_s, kv_w, gates,
                          cmp_pe, cmp_w1, cmp_b1, cmp_w2)
    mix = jnp.einsum('blm,md->bld', jnp.concatenate([o_g, o_n], axis=-1).astype(x.dtype), w_o)
    x = layer_norm(ALPHA * x + ga1 * mix, ln1_g, ln1_b)
    u2 = x * (1 + sc2) + sh2
    gate, up = jnp.split(jnp.einsum('bld,df->blf', u2, w_ffn_in), 2, axis=-1)
    ffn = jnp.einsum('blf,fd->bld', jax.nn.silu(gate) * up, w_ffn_out)
    x = layer_norm(ALPHA * x + ga2 * ffn, ln2_g, ln2_b)
    return x, s_new, kv_c, kv_s, win_new

def setup_inputs(seed: int = 0) -> dict:
    key = jax.random.key(seed)
    ks = jax.random.split(key, 32)
    f32 = jnp.float32

    def nrm(k, shape, s):
        return jax.random.normal(k, shape, f32) * s

    n_pages = PAST_LEN // PAGE_SIZE
    n_used = DEC_BATCH * n_pages
    n_pool = n_used + n_used // 4
    win_buf = min(WINDOW, PAST_LEN)
    kvt = (2, NSA_KV_HEADS, NSA_HEAD_DIM)
    perm = jax.random.permutation(ks[0], n_pool)
    page_table = perm[:n_used].reshape(DEC_BATCH, n_pages).astype(jnp.int32)
    return {
        'x_prompt': nrm(ks[1], (BATCH, SEQ, D_MODEL), 1.0),
        'x_sample': nrm(ks[2], (DEC_BATCH, DEC_SEQ, D_MODEL), 1.0),
        'state_gla': nrm(ks[3], (DEPTH, DEC_BATCH, GLA_HEADS, GLA_DK, GLA_DV), 1.0),
        'cache_cmp_kv': nrm(ks[4], (DEPTH, n_pool, PAGE_SIZE) + kvt, 1.0),
        'cache_slc_kv': nrm(ks[5], (DEPTH, n_pool, PAGE_SIZE) + kvt, 1.0),
        'cache_win_kv': nrm(ks[6], (DEPTH, DEC_BATCH, win_buf) + kvt, 1.0),
        'page_table': page_table,
        'c_prompt': nrm(ks[7], (BATCH, D_MODEL), 1.0),
        'c_sample': nrm(ks[8], (DEC_BATCH, D_MODEL), 1.0),
        'ln_in_g': 1.0 + nrm(ks[9], (D_MODEL,), 0.02),
        'ln_in_b': nrm(ks[10], (D_MODEL,), 0.02),
        'w_ada': nrm(ks[11], (DEPTH, D_MODEL, 6 * D_MODEL), D_MODEL ** -0.5),
        'b_ada': nrm(ks[12], (DEPTH, 6 * D_MODEL), 0.01),
        'w_in': nrm(ks[13], (DEPTH, D_MODEL, IN_WIDTH), D_MODEL ** -0.5),
        'gla_w_a2': nrm(ks[14], (DEPTH, GLA_RANK, GLA_HEADS * GLA_DK), GLA_RANK ** -0.5),
        'gla_b_a': nrm(ks[15], (DEPTH, GLA_HEADS * GLA_DK), 0.1),
        'gla_norm_g': 1.0 + nrm(ks[16], (DEPTH, GLA_DV), 0.02),
        'cmp_pe': nrm(ks[17], (DEPTH, CMP_BLK, 2, NSA_HEAD_DIM), 0.1),
        'cmp_w1': nrm(ks[18], (DEPTH, 2, CMP_BLK * NSA_HEAD_DIM, CMP_HIDDEN), (CMP_BLK * NSA_HEAD_DIM) ** -0.5),
        'cmp_b1': nrm(ks[19], (DEPTH, 2, CMP_HIDDEN), 0.01),
        'cmp_w2': nrm(ks[20], (DEPTH, 2, CMP_HIDDEN, NSA_HEAD_DIM), CMP_HIDDEN ** -0.5),
        'w_o': nrm(ks[21], (DEPTH, MIX_WIDTH, D_MODEL), BETA * MIX_WIDTH ** -0.5),
        'ln1_g': 1.0 + nrm(ks[22], (DEPTH, D_MODEL), 0.02),
        'ln1_b': nrm(ks[23], (DEPTH, D_MODEL), 0.02),
        'w_ffn_in': nrm(ks[24], (DEPTH, D_MODEL, 2 * D_FF), D_MODEL ** -0.5),
        'w_ffn_out': nrm(ks[25], (DEPTH, D_FF, D_MODEL), BETA * D_FF ** -0.5),
        'ln2_g': 1.0 + nrm(ks[26], (DEPTH, D_MODEL), 0.02),
        'ln2_b': nrm(ks[27], (DEPTH, D_MODEL), 0.02),
    }

def reference(x_prompt, x_sample, state_gla, cache_cmp_kv, cache_slc_kv, cache_win_kv, page_table, c_prompt,
              c_sample, ln_in_g, ln_in_b, w_ada, b_ada, w_in, gla_w_a2, gla_b_a, gla_norm_g, cmp_pe, cmp_w1,
              cmp_b1, cmp_w2, w_o, ln1_g, ln1_b, w_ffn_in, w_ffn_out, ln2_g, ln2_b):
    xp = layer_norm(x_prompt, ln_in_g, ln_in_b)
    xs = layer_norm(x_sample, ln_in_g, ln_in_b)
    db, n_pages = page_table.shape
    kvt = (2, NSA_KV_HEADS, NSA_HEAD_DIM)
    g_p, g_s, c_p, c_s, s_p, s_s, w_p, w_s = [], [], [], [], [], [], [], []
    for l in range(DEPTH):
        lw = (w_ada[l], b_ada[l], w_in[l], gla_w_a2[l], gla_b_a[l], gla_norm_g[l], cmp_pe[l], cmp_w1[l],
              cmp_b1[l], cmp_w2[l], w_o[l], ln1_g[l], ln1_b[l], w_ffn_in[l], w_ffn_out[l], ln2_g[l], ln2_b[l])
        s0 = jnp.zeros((xp.shape[0], GLA_HEADS, GLA_DK, GLA_DV), jnp.float32)
        xp, gp, cp, sp, wp = decoder_layer(xp, c_prompt, s0, nsa_prompt, *lw)
        cmp_past = cache_cmp_kv[l][page_table].reshape((db, n_pages * PAGE_SIZE) + kvt)
        slc_past = cache_slc_kv[l][page_table].reshape((db, n_pages * PAGE_SIZE) + kvt)
        fn = functools.partial(nsa_sample, cmp_past, slc_past, cache_win_kv[l])
        xs, gs, cs, ss, ws = decoder_layer(xs, c_sample, state_gla[l], fn, *lw)
        g_p.append(gp); g_s.append(gs); c_p.append(cp); c_s.append(cs)
        s_p.append(sp); s_s.append(ss); w_p.append(wp); w_s.append(ws)
    return (xp, xs, jnp.stack(g_p), jnp.stack(g_s), jnp.stack(c_p), jnp.stack(c_s), jnp.stack(s_p),
            jnp.stack(s_s), jnp.stack(w_p), jnp.stack(w_s))


_drawn_inputs = setup_inputs


def setup_inputs(seed=0):
    import zlib

    import numpy as np

    out = dict(_drawn_inputs(seed))
    spreads = {}
    factors = {'cache_cmp_kv': 5.926,
     'cache_slc_kv': 6.168,
     'gla_norm_g': 22.883,
     'cmp_pe': 8.0,
     'cmp_b1': 24.057,
     'ln1_g': 2.773,
     'ln1_b': 2.833,
     'ln2_g': 22.711,
     'ln2_b': 24.917}
    for name, (base, spread) in spreads.items():
        noise = np.random.default_rng([zlib.crc32(name.encode()), seed]).standard_normal(out[name].shape)
        drawn = base * np.exp(spread * noise) if base else spread * noise
        out[name] = __import__('jax').numpy.asarray(drawn.astype(out[name].dtype))
    for name, factor in factors.items():
        out[name] = (out[name] * factor).astype(out[name].dtype)
    return out
```

```python
from contextlib import ExitStack

import concourse.bass as bass
from concourse import mybir

ALU = mybir.AluOpType
ACT = mybir.ActivationFunctionType
F32 = mybir.dt.float32
I32 = mybir.dt.int32
U32 = mybir.dt.uint32
AX = mybir.AxisListType

P = 128
D = 1024
KD = D // P
LP = 512
TT = LP // P
DB, DS = 8, 4
LS = DB * DS
NT = LP + LS
NC = 1 + DB
FF = 2816
KF = FF // P
ALPHA = 2.0 ** 0.25

GH, DK, DV = 4, 64, 128
RANK, TAU = 16, 16.0
CH = 32
NCH = LP // CH
NH, G, R, HD = 8, 2, 4, 64
ROWS = G * R * DS
KVW = 2 * G * HD
PAGES, PSZ = 32, 128
PAST = PAGES * PSZ
WIN = 512
SPAN = PAST // P
SEG = 16
NSEG = PAST // SEG
NCS = NSEG - 1
NSEGP = LP // SEG
NCP = NSEGP - 1
HID = 128
JP = SEG // 2
NB = PAST // 64 + 1
NEG = -1e30
GELU_A, GELU_C = 0.7978845608028654, 0.044715

ZQG, ZKG, ZVG, ZRG, ZQN, ZKV = 0, 2, 4, 8, 12, 16
ZT = 22
MISC = RANK + 3 * NH

C_WIN, C_XW, C_XS, C_SLC, C_CMP = 0, WIN, WIN + DS, WIN + 2 * DS, WIN + 2 * DS + PAST
C_ALL = C_CMP + NCS + 1
NPT = 4 + 1 + SPAN + 2

RING, SLOT = 4, 2 * P * KD
N_ADA1, N_IN, N_ADA2, N_O, N_F1, N_F2 = 8, 12, 16, 4, 22, 16
S_IN = N_ADA1
S_ADA2 = S_IN + N_IN
S_O = S_ADA2 + N_ADA2
S_F1 = S_O + N_O
S_F2 = S_F1 + N_F1
S_END = S_F2 + N_F2


def build(nc, a, out):
    (y_t, gla_p, gla_s, cmp_p, cmp_s, slc_p, slc_s, win_p, win_s) = out
    gate_scr = nc.dram_tensor("gate_scr", (LS, R, G, 3), F32, kind="Internal").ap()

    with ExitStack() as ctx:
        def sb(name, shape, dt=F32):
            return ctx.enter_context(nc.sbuf_tensor(name, shape, dt))

        sems = {}

        def sem(name):
            if name not in sems:
                sems[name] = ctx.enter_context(nc.semaphore(name))
            return sems[name]

        RX = sb("trunk", [P, KD * NT])
        RM = sb("mixreg", [P, KD * NT])
        RZ = sb("zreg", [P, ZT * NT])
        W1 = sb("w1", [P, 2, 2, JP, HID])
        RR = sb("ringreg", [P, RING * SLOT])
        RC = sb("creg", [P, SPAN * KVW])
        RS = sb("sreg", [P, SPAN * KVW + 4 * KVW])

        X = RX[:, :].rearrange("p (k t) -> p k t", k=KD)
        XC = RM[:, :].rearrange("p (k t) -> p k t", k=KD)
        MIXT = XC
        U = RC[:, 0:KD * NT].rearrange("p (k t) -> p k t", k=KD)
        SQ = RS[:, 0:KD * NT].rearrange("p (k t) -> p k t", k=KD)
        Z = RZ[:, :].rearrange("p (k t) -> p k t", k=ZT)
        HT = Z
        ring = [RR[:, s * SLOT:(s + 1) * SLOT] for s in range(RING)]
        wslot = [r.rearrange("p (k c) -> p k c", k=KD) for r in ring]
        wslot1 = [r.rearrange("p (k h c) -> p k h c", k=KD, h=2) for r in ring]
        wslot2 = [r[:, 0:KF // 2 * P].rearrange("p (k c) -> p k c", c=P) for r in ring]

        ident = sb("ident", [P, P])
        ones = sb("ones", [P, P])
        pen = sb("pen", [P, LP])
        mod = sb("mod", [P, 6, KD, NC])
        cs = sb("cs", [P, KD, NC])
        cth = sb("cth", [P, KD, NC])
        bada = sb("bada", [P, 6, KD])
        lnv = sb("lnv", [P, 6, KD])
        rstd = sb("rstd", [P, NT])
        w2 = sb("w2", [P, 2, HD])
        pe_t = sb("pe_t", [P, 2, 2, JP])
        cb1 = sb("cb1", [P, 2])
        cbias = sb("cbias", [P, 2])
        wa2 = sb("wa2", [RANK, GH * DK])
        ba = sb("ba", [P, 2])
        gng = sb("gng", [P, 1])
        zM = sb("zM", [MISC, NT])
        GT = sb("GT", [P, TT + 1, MISC])
        zS = sb("zS", [P, 8, LS])
        grow = sb("grow", [ROWS, DB, 3])
        ptab = sb("ptab", [P, DB], I32)
        idx = sb("idx", [P, DB], U32)
        pidx = sb("pidx", [P, 1], I32)
        pmod = sb("pmod", [P, 1], I32)
        pmodf = sb("pmodf", [P, 1])
        qbd = sb("qbd", [P, G, R, DS])
        knew = sb("knew", [P, 2, DS])
        gcur = sb("gcur", [ROWS, 3])
        VX = sb("VX", [2 * DS, P])
        bpen = sb("bpen", [ROWS, NB])
        spen = sb("spen", [ROWS, NB])
        rsum = sb("rsum", [ROWS, ROWS])
        impA = sb("impA", [ROWS, 4 * (NB + 1)])
        score = sb("score", [ROWS, 3, NB])
        top8 = sb("top8", [ROWS, 2, 8])
        smx = sb("smx", [ROWS, 4, 3])
        gdec = sb("gdec", [P, 2, NCH + DB])
        gares = sb("gares", [P, 2, NC])
        wpen = sb("wpen", [ROWS, WIN + 2 * DS])

        PS = ctx.enter_context(nc.psum_tensor("PS", [P, 8, 512], F32))
        PF = PS[:, :, :].rearrange("p b c -> p (b c)")
        dense = [PF[:, (4 + 2 * b) * 512:(4 + 2 * b) * 512 + NT] for b in range(2)]
        stat = [PF[:, 2 * b * 512:2 * b * 512 + NT] for b in range(2)]
        pmods = PS[:, 4, 0:KD * NC].rearrange("p (k c) -> p k c", k=KD)

        VW = DV * GH + 3 * KVW
        VT = RS[:, 0:(TT + 1) * VW].rearrange("p (t c) -> p t c", t=TT + 1)
        S1 = RS[:, (TT + 1) * VW:(TT + 1) * VW + (NCH + 1) * P].rearrange("p (c v) -> p c v", c=NCH + 1)
        GW = 2 * NT
        LA, BC, DM, DL = (RR[:, i * GW:(i + 1) * GW].rearrange("p (h t) -> p h t", h=2) for i in range(4))
        ATT = RR[:, 2 * GW:2 * GW + 16 * P].rearrange("p (h t i) -> p h t i", h=GH, t=TT)
        SQG = RR[:, 0:GH * NT].rearrange("p (h t) -> p h t", h=GH)
        S0 = RR[:, 4 * GW:4 * GW + 2 * DB * P].rearrange("p (h b v) -> p h b v", h=2, b=DB)
        KE = RR[:, 6400:6400 + (TT + 1) * 256].rearrange("p (t c) -> p t c", t=TT + 1)
        ATTS = RR[0:LS, 7680:7680 + GH * LS].rearrange("p (h i) -> p h i", h=GH)
        E = [RC[:, i * GW:(i + 1) * GW].rearrange("p (h t) -> p h t", h=2) for i in range(4)]
        TH = RC[:, 0:GH * NT].rearrange("p (h t) -> p h t", h=GH)
        S0P = RC[:, 4 * GW:4 * GW + (NCH + 1) * P].rearrange("p (c v) -> p c v", c=NCH + 1)
        SST = [S0P, S1]
        VMB = RC[0:LS, 6528:6528 + DB * P].rearrange("p (b v) -> p b v", b=DB)
        rmask = RC[:, 7552:7552 + NT]
        gmask = sb("gmask", [P, CH])
        smask = sb("smask", [LS, LS])
        bmask = sb("bmask", [LS, DB])

        CP = RC[0:NSEGP, 0:SEG * KVW]
        CPV = CP.rearrange("p (c g j x) -> p c g j x", c=2, g=G, j=JP)
        XTP = RC[:, 4096:4096 + 16 * 64].rearrange("p (u g n) -> p u g n", u=16, g=G)
        HX = RC[:, 5120:5120 + 62 * 2].rearrange("p (c g n) -> p c g n", c=2, g=G)
        HG = RC[:, 5244:5244 + 62 * 2].rearrange("p (c g n) -> p c g n", c=2, g=G)
        kcTp = RC[:, 5376:5376 + NCP]
        vcp = RC[0:NCP, 5408:5408 + P]
        pcp = RC[:, 5540:5540 + TT * NCP].rearrange("p (t n) -> p t n", t=TT)
        mcp = RC[:, 5670:5670 + TT * NCP].rearrange("p (t n) -> p t n", t=TT)
        PB = [RR[:, b * 1056:(b + 1) * 1056] for b in range(2)]
        PTB = [RR[:, 2112 + b * 1152:2112 + (b + 1) * 1152] for b in range(2)]
        qcur = RR[:, 4416:4416 + LP]
        pst = RR[:, 4928:4928 + 2 * 12].rearrange("p (b k j) -> p b k j", b=2, k=4)
        gpc = RR[:, 4952:4952 + TT * 6].rearrange("p (t c) -> p t c", t=TT)

        CB = RC[:, :].rearrange("p (e s c x) -> p e s c x", e=2, s=SEG, c=2)
        SBF = RS[:, 0:SPAN * KVW]
        SBV = SBF.rearrange("p (t c x) -> p t c x", t=SPAN, c=2)
        WBF = RS[:, SPAN * KVW:SPAN * KVW + 4 * KVW]
        WBV = WBF.rearrange("p (t c x) -> p t c x", t=4, c=2)
        XTS = RR[:, :].rearrange("p (u g n) -> p u g n", u=16, g=G)
        KT = RZ[:, 0:SPAN * P]
        KTW = RZ[:, 4096:4096 + WIN]
        PSC = RZ[0:ROWS, 4608:4608 + C_ALL]
        PTS = RZ[:, 4608 + C_ALL:4608 + C_ALL + NPT * ROWS].rearrange("p (n r) -> p n r", r=ROWS)
        o_ = 4608 + C_ALL + NPT * ROWS
        kcT = RZ[:, o_:o_ + NSEG]
        vc = sb("vc", [P, 2, P])
        hgx = RZ[:, o_ + NSEG:o_ + NSEG + 2 * NCS]
        assert o_ + NSEG + 2 * NCS <= ZT * NT
        HXS = sb("hxs", [P, 2 * NCS])

        def seg_src(u, h, g):
            return PS[g * HD:(g + 1) * HD, u % 2, h * 2 * P:(h + 1) * 2 * P].rearrange("p (e n) -> p e n", e=2)

        def seg_dst(u, h, g):
            return XTS[h * HD:(h + 1) * HD, u, g, :].rearrange("p (n e) -> p e n", e=2)

        def matmul(o, lhsT, rhs, start, stop, **kw):
            return nc.tensor.matmul(o, lhsT, rhs, start=start, stop=stop, **kw)

        block = ctx.enter_context(nc.Block())

        @block.sync
        def _(sp):
            sp.dma_start(X, a["x_t"]).then_inc(sem("x_in"), 16)

            def stretch(src, base, count, views):
                full = count // RING
                with sp.Fori(0, full) as i:
                    for k in range(RING):
                        sp.wait_ge(sem("weights_used"), i * (2 * RING) + 2 * (base + k - RING + 1))
                        s = (base + k) % RING
                        sp.dma_start(views[s], src[bass.ds(i * RING + k, 1)].rearrange("o p x -> p (o x)")
                                     ).then_inc(sem(f"ring_full{s}"), 16)
                for n in range(base + full * RING, base + count):
                    sp.wait_ge(sem("weights_used"), 2 * (n - RING + 1))
                    sp.dma_start(views[n % RING], src[n - base]).then_inc(sem(f"ring_full{n % RING}"), 16)

            for n in range(RING):
                sp.dma_start(ring[n], a["w_ada"][n]).then_inc(sem(f"ring_full{n}"), 16)
            for n in range(RING, N_ADA1):
                sp.wait_ge(sem("weights_used"), 2 * (n - RING + 1))
                sp.dma_start(ring[n % RING], a["w_ada"][n]).then_inc(sem(f"ring_full{n % RING}"), 16)
            stretch(a["w_in"], S_IN, N_IN - 1, ring)
            n = S_IN + N_IN - 1
            sp.wait_ge(sem("weights_used"), 2 * (n - RING + 1))
            sp.dma_start(ring[n % RING][:, 0:KD * MISC], a["w_misc"]).then_inc(sem(f"ring_full{n % RING}"), 16)
            stretch(a["w_ada"][N_ADA1:], S_ADA2, N_ADA2, ring)

            sp.wait_ge(sem("weights_used"), 2 * S_O)
            sp.dma_start(S0, a["state"]).then_inc(sem("s0_in"), 16)
            sp.wait_ge(sem("rows_ready"), 3 * (TT + 1))
            for o, c in ((cmp_p, 512), (slc_p, 768), (win_p, 1024)):
                sp.dma_start(o.rearrange("(t p) c -> p t c", p=P), VT[:, 0:TT, c:c + KVW]).then_inc(sem("kv_out"), 16)
            for o, c in ((cmp_s, 512), (slc_s, 768)):
                sp.dma_start(o, VT[0:LS, TT, c:c + KVW]).then_inc(sem("kv_out"), 16)
            for b in range(DB):
                sp.dma_start(win_s[b, WIN - DS:WIN, :],
                             VT[b * DS:(b + 1) * DS, TT, 1024:1280]).then_inc(sem("kv_out"), 16)
            sp.dma_start(win_s[:, 0:WIN - DS, :], a["win"][:, DS:WIN, :]).then_inc(sem("winc_out"), 16)
            sp.wait_ge(sem("gates_ready"), 1)
            sp.dma_start(gate_scr.rearrange("t r g j -> t (r g j)"), GT[0:LS, TT, RANK:MISC]).then_inc(sem("gate_out"), 16)
            sp.wait_ge(sem("gate_out"), 16)
            for g in range(G):
                for r in range(R):
                    sp.dma_start(grow[(g * R + r) * DS:(g * R + r + 1) * DS, :, :],
                                 gate_scr[:, r, g, :].rearrange("(b q) j -> q b j", q=DS)).then_inc(sem("grow_in"), 16)
            sp.wait_ge(sem("gla_scan"), 2 * NCH)
            for h in range(2):
                sp.dma_start(gla_p[2 * h:2 * h + 2].rearrange("h k v -> (h k) v"),
                             SST[h][:, NCH, :]).then_inc(sem("gla_out"), 16)
            for h in range(2):
                sp.wait_ge(sem("gla_snew"), h + 1)
                sp.dma_start(gla_s[:, 2 * h:2 * h + 2].rearrange("b h k v -> (h k) b v"),
                             S0[:, h]).then_inc(sem("gla_out"), 16)
            sp.wait_ge(sem("kv_out"), 16 * (5 + DB))
            sp.wait_ge(sem("gla_done"), GH)
            sp.wait_ge(sem("gla_out"), 64)
            for c in range(2):
                for g in range(G):
                    o = (c * G + g) * HD
                    sp.dma_start(CP[:, o * SEG:(o + HD) * SEG].rearrange("p (s d) -> p s d", s=SEG),
                                 cmp_p.rearrange("(n s) x -> n s x", s=SEG)[:, :, o:o + HD]).then_inc(sem("segp_in"), 16)

            def batch(b, waited):
                if waited:
                    sp.wait_ge(sem("pv_done"), b)
                else:
                    sp.wait_ge(sem("zs"), 6)
                sp.dma_start(WBF, a["win"][bass.ds(b, 1)].rearrange("o (p t) c -> p (o t c)", p=P)).then_inc(sem("win_in"), 16)
                sp.dma_start(VX[0:DS, :], win_s[bass.ds(b, 1), WIN - DS:WIN, P:KVW].rearrange("o q c -> (o q) c")).then_inc(sem("win_in"), 16)
                sp.dma_start(VX[DS:2 * DS, :], slc_s.rearrange("(b q) c -> b q c", q=DS)[bass.ds(b, 1), :, P:KVW].rearrange("o q c -> (o q) c")).then_inc(sem("win_in"), 16)

            batch(0, False)
            with sp.Fori(1, DB) as b:
                batch(b, True)
            sp.wait_ge(sem("cmp_mm"), 16 * DB)
            stretch(a["w_o"], S_O, N_O, ring)
            stretch(a["w_f1"], S_F1, N_F1, ring)
            stretch(a["w_f2"], S_F2, N_F2, [r[:, 0:KF // 2 * P] for r in ring])
            sp.wait_ge(sem("ln_x"), 3 * KD)
            sp.dma_start(y_t, X).then_inc(sem("y_out"), 16)
            sp.wait_ge(sem("y_out"), 16)
            sp.wait_ge(sem("winc_out"), 16)

        @block.gpsimd
        def _(pool):
            small = ((lnv, a["lnv"]), (cs, a["c_t"]), (bada, a["b_ada"]), (pe_t, a["pe"]), (cb1, a["b1"]), (w2, a["w2"]),
                     (wa2, a["wa2"]), (ba, a["ba"]), (gng, a["gng"]), (W1, a["w1"]))
            for dst, src in small:
                pool.dma_start(dst[:], src).then_inc(sem("consts_in"), 16)
            pool.dma_start(ptab[:, :], a["ptab"].unsqueeze(1).to_broadcast([PAGES, 4, DB])).then_inc(sem("ptab_in"), 16)

            nset = [0]

            def fill(t, v):
                nset[0] += 1
                nc.gpsimd.memset(t, v).then_inc(sem("pool_set"), 1)
                pool.wait_ge(sem("pool_set"), nset[0])
            fill(ident[:, :], 0.0)
            fill(ones[:, :], 1.0 / D)
            fill(pen[:, :], 0.0)
            fill(gmask[:, :], 1.0)
            fill(smask[:, :], 1.0)
            fill(bmask[:, :], 1.0)
            fill(rsum[:, :], 0.0)
            fill(wpen[:, :], 0.0)
            fill(bpen[:, :], 0.0)
            fill(impA[:, :], 0.0)
            fill(qbd[:, :, :, :], 0.0)

            nsel = [0]

            def sel(t, op, base, pattern, cm, fillv):
                nsel[0] += 1
                nc.gpsimd.affine_select(out=t, in_=t, compare_op=op, fill=fillv, base=base, pattern=pattern,
                                        channel_multiplier=cm).then_inc(sem("pool_sel"), 1)
                pool.wait_ge(sem("pool_sel"), nsel[0])

            sel(ident[:, :], ALU.not_equal, 0, [[-1, P]], 1, 1.0)
            sel(pen[:, LP - P:LP], ALU.is_ge, 0, [[-1, P]], 1, NEG)
            for c in range(4):
                sel(gmask[32 * c:32 * c + 32, :], ALU.is_ge, 0, [[1, CH]], -1, 0.0)
            sel(smask[:, :], ALU.is_ge, 0, [[1, LS]], -1, 0.0)
            sel(bmask[:, :], ALU.is_ge, 0, [[-DS, DB]], 1, 0.0)
            for d in range(-(R - 1), R):
                sel(rsum[:, :], ALU.not_equal, DS * d, [[-1, ROWS]], 1, 1.0)
                sel(bmask[:, :], ALU.is_ge, DS - 1, [[DS, DB]], -1, 0.0)
            sel(bpen[:, :], ALU.not_equal, 0, [[1, NB]], 0, 1e4)
            sel(bpen[:, :], ALU.not_equal, -(NB - 1), [[1, NB]], 0, 1e4)
            sel(bpen[:, :], ALU.not_equal, -(NB - 2), [[1, NB]], 0, 1e4)
            nc.gpsimd.iota(pidx[:, :], pattern=[[0, 1]], base=0, channel_multiplier=1).then_inc(sem("pidx"), 1)
            pool.wait_ge(sem("pidx"), 1)
            sel(rsum[0:ROWS, 0:ROWS // 2], ALU.is_ge, ROWS // 2 - 1, [[0, ROWS // 2]], -1, 0.0)
            sel(rsum[0:ROWS, ROWS // 2:ROWS], ALU.is_ge, -(ROWS // 2), [[0, ROWS // 2]], 1, 0.0)
            pool.wait_ge(sem("pool_sel"), nsel[0])
            nc.gpsimd.memset(top8[:, :, :], 0.0).then_inc(sem("pool_consts"), 1)
            pool.wait_ge(sem("pool_consts"), 1)
            nc.gpsimd.memset(rmask, 1.0).then_inc(sem("rmask0"), 1)
            pool.wait_ge(sem("rmask0"), 1)
            nc.gpsimd.memset(rmask[:, 0:LP].rearrange("p (c i) -> p c i", i=CH)[:, :, 0:1], 0.0).then_inc(sem("rmask"), 1)
            pool.wait_ge(sem("rmask"), 1)
            nc.gpsimd.memset(rmask[:, LP:NT].rearrange("p (c i) -> p c i", i=DS)[:, :, 0:1], 0.0).then_inc(sem("rmask"), 1)

            pool.wait_ge(sem("gla_done"), GH)
            pool.wait_ge(sem("gla_out"), 64)
            nc.gpsimd.memset(pcp, 0.0).then_inc(sem("pcp0"), 1)
            pool.wait_ge(sem("pcp0"), 1)
            nc.gpsimd.memset(mcp, 1.0).then_inc(sem("pcp0"), 1)
            pool.wait_ge(sem("pcp0"), 2)
            for t, v in ((pcp, NEG), (mcp, 0.0)):
                nc.gpsimd.affine_select(out=t, in_=t, compare_op=ALU.is_ge, fill=v, base=-(2 * SEG - 1),
                                        pattern=[[P, TT], [-SEG, NCP]], channel_multiplier=1).then_inc(sem("pcp"), 1)
                pool.wait_ge(sem("pcp"), 1 if t is pcp else 2)

            pool.wait_ge(sem("zs"), 6)
            pool.wait_ge(sem("idx"), 1)
            for b in range(DB):
                if b:
                    pool.wait_ge(sem("seg_t"), 16 * b)
                    pool.wait_ge(sem("slc_in"), 16 * b)
                nc.gpsimd.indirect_dma_start(out=RC[:, :], out_offset=None, in_=a["cmp"],
                                             in_offset=bass.IndirectOffsetOnAxis(ap=idx[:, b:b + 1], axis=0)
                                             ).then_inc(sem("cmp_in"), 16)
                pool.wait_ge(sem("cmp_in"), 16 * (b + 1))
                if b:
                    pool.wait_ge(sem("pv_done"), b)
                nc.gpsimd.indirect_dma_start(out=SBF, out_offset=None, in_=a["slc"],
                                             in_offset=bass.IndirectOffsetOnAxis(ap=idx[:, b:b + 1], axis=0)
                                             ).then_inc(sem("slc_in"), 16)

        @block.tensor
        def _(pe):
            def ln_mean(base):
                for k in range(KD):
                    matmul(stat[0][:, 0:LP], ones[:, :], X[:, k, 0:LP], k == 0, k == KD - 1)
                    last = matmul(stat[0][:, LP:NT], ones[:, :], X[:, k, LP:NT], k == 0, k == KD - 1)
                last.then_inc(sem("ln_mean"), 1)

            def ln_var(nth):
                for k in range(KD):
                    pe.wait_ge(sem("ln_sq"), nth * KD + k + 1)
                    matmul(stat[1][:, 0:LP], ones[:, :], SQ[:, k, 0:LP], k == 0, k == KD - 1)
                    last = matmul(stat[1][:, LP:NT], ones[:, :], SQ[:, k, LP:NT], k == 0, k == KD - 1)
                last.then_inc(sem("ln_var"), 1)

            def slot_ready(base, i, k):
                pe.wait_ge(sem(f"ring_full{(base + k) % RING}"), i * 16 + 16 * ((base + k) // RING + 1))

            def ada(base, i, nth):
                pe.wait_ge(sem("mod_free"), nth)
                for k in range(RING):
                    slot_ready(base, i, k)
                    for f in range(2):
                        for c in range(KD):
                            last = matmul(pmods[:, 2 * k + f, :], wslot[(base + k) % RING][:, c, f * P:(f + 1) * P],
                                          cs[:, c, :], c == 0, c == KD - 1)
                        last.then_inc(sem("weights_used"), 1)

            def project(w, b, src, m=P):
                for k in range(KD):
                    matmul(dense[b][0:m, 0:LP], w(k), src[:, k, 0:LP], k == 0, k == KD - 1)
                    last = matmul(dense[b][0:m, LP:NT], w(k), src[:, k, LP:NT], k == 0, k == KD - 1)
                return last

            pe.wait_ge(sem("pool_consts"), 1)
            pe.wait_ge(sem("x_in"), 16)
            ln_mean(0)
            pe.wait_ge(sem("silu_c"), 1)
            ada(0, 0, 1)
            ln_var(0)
            ada(RING, 0, 2)

            pe.wait_ge(sem("ln_u"), KD + 1)
            full = (N_IN - 1) // RING

            def in_tiles(i, slots):
                for k in slots:
                    slot_ready(S_IN, i, k)
                    for f in range(2):
                        pe.wait_ge(sem("dense_free"), i * 8 + 2 * k + f + 1)
                        project(lambda c: wslot[(S_IN + k) % RING][:, c, f * P:(f + 1) * P], f, U
                                ).then_inc(sem("weights_used"), 1)
            with pe.Fori(0, full) as i:
                in_tiles(i, range(RING))
            in_tiles(full, range(N_IN - 1 - full * RING))
            n = S_IN + N_IN - 1
            slot_ready(n, 0, 0)
            pe.wait_ge(sem("dense_free"), ZT + 1)
            wm = ring[n % RING][:, 0:KD * MISC].rearrange("p (k c) -> p k c", k=KD)
            project(lambda c: wm[:, c, :], 0, U, MISC).then_inc(sem("weights_used"), 2)

            pe.wait_ge(sem("dense_free"), ZT + 1 + 2)
            with pe.Fori(0, N_ADA2 // RING) as i:
                ada(S_ADA2, i, i + 3)
            pe.wait_ge(sem("mod_free"), 7)

            src = [ZVG + i for i in range(4)] + [ZKV + i for i in range(6)]
            for t in range(TT + 1):
                n = P if t < TT else LS
                cols = slice(t * P, t * P + n)
                if t >= 2:
                    pe.wait_ge(sem("rows_ready"), 3 * (t - 1))
                bank = 4 * (t % 2)
                for q, z in enumerate(src):
                    last = nc.tensor.transpose(PS[0:n, bank + q // 4, (q % 4) * P:(q % 4 + 1) * P], Z[:, z, cols], ident[:, :])
                    if q == 3 or q == 7:
                        last.then_inc(sem("rows_t"), 1)
                nc.tensor.transpose(PS[0:n, bank + 2, 256:256 + MISC], zM[:, cols], ident[0:MISC, 0:MISC]).then_inc(sem("rows_t"), 1)

            pe.wait_ge(sem("rows_ready"), 3 * (TT + 1))
            for c in range(2):
                for n in range(2 * JP):
                    last = matmul(PS[:, 6, c:c + 1], W1[:, c, n // JP, n % JP, :], pe_t[:, c, n // JP, n % JP:n % JP + 1],
                                  n == 0, n == 2 * JP - 1)
            last.then_inc(sem("pe_bias"), 1)

            for h in range(2):
                matmul(stat[h][:, 0:LP], wa2[:, h * P:(h + 1) * P], zM[0:RANK, 0:LP], True, True)
                matmul(stat[h][:, LP:NT], wa2[:, h * P:(h + 1) * P], zM[0:RANK, LP:NT], True, True).then_inc(sem("decay_x"), 1)
            pe.wait_ge(sem("gla_q"), 4)
            for h in range(GH):
                hp, lo = h // 2, (h % 2) * DK
                for t in range(TT):
                    for c in range(4):
                        cols = slice(t * P + c * CH, t * P + (c + 1) * CH)
                        matmul(PS[c * CH:(c + 1) * CH, h % 2, (hp * TT + t) * CH:(hp * TT + t + 1) * CH],
                               E[1][lo:lo + DK, hp, cols], E[0][lo:lo + DK, hp, cols], True, True)
                last = matmul(PS[0:LS, h % 2, 256 + hp * LS:256 + (hp + 1) * LS],
                              E[1][lo:lo + DK, hp, LP:NT], E[0][lo:lo + DK, hp, LP:NT], True, True)
            last.then_inc(sem("gla_att"), 1)
            for h in range(2):
                for t in range(TT + 1):
                    n = P if t < TT else LS
                    last = nc.tensor.transpose(PS[0:n, 4 + t // 2, ((t % 2) * 2 + h) * P:((t % 2) * 2 + h + 1) * P],
                                               E[3][:, h, t * P:t * P + n], ident[:, :])
            last.then_inc(sem("gla_ket"), 1)
            pe.wait_ge(sem("gla_ke"), 3)
            for hp in range(2):
                if hp == 1:
                    pe.wait_ge(sem("gla_attm"), 10)
                for c in range(4):
                    for t in range(TT):
                        for lo in range(2):
                            h = 2 * hp + lo
                            last = matmul(PS[lo * DK:(lo + 1) * DK, 4 - 4 * hp + c, t * P:(t + 1) * P],
                                          KE[c * CH:(c + 1) * CH, t, h * DK:(h + 1) * DK],
                                          VT[c * CH:(c + 1) * CH, t, h * DV:(h + 1) * DV], True, True)
                last.then_inc(sem("gla_u"), 1)
            pe.wait_ge(sem("gla_scan"), 2 * NCH)
            pe.wait_ge(sem("s0_in"), 16)
            for h in range(GH):
                hp, lo = h // 2, (h % 2) * DK
                matmul(PS[:, 4 + h % 2, h * LS:(h + 1) * LS], VT[0:LS, TT, h * DV:(h + 1) * DV], ATTS[:, h, :], True, False, skip_group_check=True)
                for b in range(DB):
                    c = slice(LP + b * DS, LP + (b + 1) * DS)
                    last = matmul(PS[:, 4 + h % 2, h * LS + b * DS:h * LS + (b + 1) * DS], S0[lo:lo + DK, hp, b, :],
                                  E[2][lo:lo + DK, hp, c], False, b == DB - 1, skip_group_check=True)
            last.then_inc(sem("gla_os"), 1)
            for h in range(GH):
                hp, lo = h // 2, (h % 2) * DK
                for t in range(TT):
                    matmul(PS[:, h, t * P:(t + 1) * P], VT[:, t, h * DV:(h + 1) * DV], ATT[:, h, t, :], True, False, skip_group_check=True)
                    for c in range(4):
                        cc = slice(t * P + c * CH, t * P + (c + 1) * CH)
                        last = matmul(PS[:, h, cc], SST[hp][lo:lo + DK, t * 4 + c, :], E[2][lo:lo + DK, hp, cc], False, c == 3, skip_group_check=True)
                last.then_inc(sem("gla_o"), 1)
            for h in range(GH):
                pe.wait_ge(sem("gla_vm"), h + 1)
                if h == 2:
                    pe.wait_ge(sem("gla_snew"), 1)
                for s in range(2):
                    last = matmul(PS[(h % 2) * DK:(h % 2 + 1) * DK, 6 + s, :], KE[0:LS, TT, h * DK:(h + 1) * DK],
                                  VMB[:, 4 * s:4 * s + 4, :], True, True)
                last.then_inc(sem("gla_us"), 1)
            for h in range(GH):
                pe.wait_ge(sem("gla_sq"), h + 1)
                if h == 0:
                    pe.wait_ge(sem("gla_snew"), 2)
                if h >= 2:
                    pe.wait_ge(sem("gla_ms_used"), h - 1)
                matmul(dense[h % 2][:, 0:LP], ones[:, :], SQG[:, h, 0:LP], True, True)
                matmul(dense[h % 2][:, LP:NT], ones[:, :], SQG[:, h, LP:NT], True, True).then_inc(sem("gla_ms"), 1)

            def segments(u):
                c, j = u // JP, u % JP
                for n in range(4):
                    last = nc.tensor.transpose(PS[:, u % 2, n * P:(n + 1) * P], CB[:, n % 2, 2 * j + n // 2, c, :], ident[:, :])
                last.then_inc(sem("seg_t"), 1)

            def compress(b, u, xt, n):
                c, j = u // JP, u % JP
                for m in range(2):
                    last = matmul(PS[:, 2 + c, 0:2 * n].rearrange("p (g n) -> p g n", g=2), W1[:, c, m, j, :],
                                  xt[:, u, :, m:m + n], j == 0 and m == 0, j == JP - 1 and m == 1)
                last.then_inc(sem("cmp_mm"), 1)

            pe.wait_ge(sem("segp_in"), 64)
            pe.wait_ge(sem("gla_done"), GH)
            for u in range(18):
                if u < 16:
                    if u >= 2:
                        pe.wait_ge(sem("segp_ev"), u - 1)
                    c, j = u // JP, u % JP
                    for g in range(G):
                        last = nc.tensor.transpose(PS[:, u % 2, g * NSEGP:(g + 1) * NSEGP], CPV[:, c, g, j, :],
                                                   ident[0:NSEGP, 0:NSEGP])
                    last.then_inc(sem("segp_t"), 1)
                if u >= 2:
                    v = u - 2
                    c, j = v // JP, v % JP
                    pe.wait_ge(sem("segp_ev"), v + 1)
                    for m in range(2):
                        last = matmul(PS[:, 2 + c, 0:2 * NCP].rearrange("p (g n) -> p g n", g=2), W1[:, c, m, j, :],
                                      XTP[:, v, :, m:m + NCP], j == 0 and m == 0, j == JP - 1 and m == 1)
                    last.then_inc(sem("cmpp_mm"), 1)
            pe.wait_ge(sem("cmpp_g"), 2)
            for g in range(G):
                last = matmul(PS[g * HD:(g + 1) * HD, 4, 0:NCP], w2[:, 0, :], HG[:, 0, g, :], True, True)
            last.then_inc(sem("cmpp_kv"), 1)
            for g in range(G):
                last = matmul(PS[0:NCP, 5, g * HD:(g + 1) * HD], HG[:, 1, g, :], w2[:, 1, :], True, True)
            last.then_inc(sem("cmpp_kv"), 1)

            def scores(r, s):
                i, g = s // 2, s % 2
                lo, w = g * HD, (i + 1) * P
                q = qcur[lo:lo + HD, i * P:(i + 1) * P]
                pe.wait_ge(sem("nsa_sc_used"), r * 8 + s + 1)
                matmul(PS[:, 2 * g, 0:w], q, Z[lo:lo + HD, ZKV + 2, 0:w], True, True)
                matmul(PS[:, 2 * g + 1, 0:w], q, Z[lo:lo + HD, ZKV + 4, 0:w], True, True)
                matmul(PS[:, 4 + g, 0:NCP], q, kcTp[lo:lo + HD, :], True, True).then_inc(sem("nsa_sc"), 1)

            def values(r, s):
                i, g = s // 2, s % 2
                pb, pt = PB[g], PTB[g]
                pe.wait_ge(sem("nsa_p"), r * 24 + 3 * (s + 1))
                nc.tensor.transpose(PS[0:NCP, 4 + g, P:2 * P], pb[:, 0:NCP], ident[:, :]).then_inc(sem("nsa_pt"), 1)
                pe.wait_ge(sem("nsa_ptev"), r * 24 + 3 * s + 1)
                for q in range(2):
                    for t in range(i + 1):
                        last = nc.tensor.transpose(PS[:, 6 + q, t * P:(t + 1) * P],
                                                   pb[:, 32 + q * LP + t * P:32 + q * LP + (t + 1) * P], ident[:, :])
                    last.then_inc(sem("nsa_pt"), 1)
                pe.wait_ge(sem("nsa_ptev"), r * 24 + 3 * s + 4)
                o = PS[g * HD:(g + 1) * HD, 4 + g, 2 * P:3 * P]
                matmul(o, vcp[:, g * HD:(g + 1) * HD], pt[0:NCP, 0:P], True, False)
                for q, c in ((0, 768 + P), (1, 1024 + P)):
                    for t in range(i + 1):
                        last = matmul(o, VT[:, t, c + g * HD:c + (g + 1) * HD], pt[:, (1 + 4 * q + t) * P:(2 + 4 * q + t) * P],
                                      False, q == 1 and t == i)
                last.then_inc(sem("nsa_pv"), 1)

            pe.wait_ge(sem("cmpp_ev"), 2)
            with pe.Fori(0, R) as r:
                pe.wait_ge(sem("nsa_q"), r + 1)
                scores(r, 0)
                for s in range(8):
                    if s + 1 < 8:
                        scores(r, s + 1)
                    values(r, s)

            def seg_step(b, u):
                if u >= 2:
                    pe.wait_ge(sem("seg_ev"), b * 32 + 2 * u - 2)
                    pe.wait_ge(sem("seg_dve"), b * 32 + 2 * u - 2)
                segments(u)

            def cmp_step(b, u):
                pe.wait_ge(sem("seg_ev"), b * 32 + 2 * u + 2)
                pe.wait_ge(sem("seg_dve"), b * 32 + 2 * u + 2)
                compress(b, u, XTS, NCS)

            def tail(b):
                cols = [(C_WIN + t * P, P) for t in range(4)] + [(C_XW, 2 * DS)] + \
                       [(C_SLC + t * P, P) for t in range(SPAN)] + [(C_CMP, P), (C_CMP + P, NCS - P)]
                for n, (c, w) in enumerate(cols):
                    last = nc.tensor.transpose(PS[0:w, 4 + n // 16, (n % 16) * ROWS:(n % 16 + 1) * ROWS], PSC[:, c:c + w],
                                               ident[0:ROWS, 0:ROWS])
                    if n % 16 == 15 or n == NPT - 1:
                        last.then_inc(sem("pt_t"), 1)
                pe.wait_ge(sem("pt_ev"), 3 * (b + 1) if isinstance(b, int) else b * 3 + 3)
                vals = [WBV[:, t, 1, :] for t in range(4)] + [VX[:, :]] + [SBV[:, t, 1, :] for t in range(SPAN)] + \
                       [vc[:, 0, :], vc[0:NCS - P, 1, :]]
                for n, v in enumerate(vals):
                    w = cols[n][1]
                    last = matmul(PS[:, 7, 0:ROWS], v, PTS[0:w, n, :], n == 0, n == NPT - 1)
                last.then_inc(sem("pv_done"), 1)

            def batch(b, waited):
                if not waited:
                    pe.wait_ge(sem("zs"), 6)
                pe.wait_ge(sem("cmp_in"), b * 16 + 16)
                if waited:
                    pe.wait_ge(sem("sc_ev"), b * 11)
                seg_step(b, 0)
                seg_step(b, 1)
                for u in range(16):
                    if u == 7 and waited:
                        pe.wait_ge(sem("p_ready"), b)
                    cmp_step(b, u)
                    if u + 2 < 16:
                        seg_step(b, u + 2)
                    if u == 7 and waited:
                        tail(b - 1)
                    if u == 11:
                        pe.wait_ge(sem("cmp_g"), b * 2 + 1)
                        if waited:
                            pe.wait_ge(sem("o_ev"), b * 2)
                        for g in range(G):
                            last = matmul(PS[g * HD:(g + 1) * HD, 4, 0:NCS], w2[:, 0, :], hgx[:, g * NCS:(g + 1) * NCS], True, True)
                        last.then_inc(sem("cmp_k"), 1)
                    if u == 13:
                        pe.wait_ge(sem("cmp_kev"), b + 1)
                        pe.wait_ge(sem("batch_q"), b * 3 + 3)
                        matmul(PS[0:ROWS, 6, 0:NCS], qbd[:, :, :, :].rearrange("p g r q -> p (g r q)"), kcT[:, 0:NCS], True, True
                               ).then_inc(sem("sc_done"), 1)
                pe.wait_ge(sem("slc_in"), b * 16 + 16)
                pe.wait_ge(sem("win_in"), b * 48 + 48)
                for n in range(9):
                    if n >= 2:
                        pe.wait_ge(sem("kt_ev"), b * 9 + n - 1)
                    if n == 8:
                        pe.wait_ge(sem("pc_ready"), b + 1)
                    for t in range(4):
                        src = SBV[:, 4 * n + t, 0, :] if n < 8 else WBV[:, t, 0, :]
                        last = nc.tensor.transpose(PS[:, n % 2, t * P:(t + 1) * P], src, ident[:, :])
                    last.then_inc(sem("kt_t"), 1)
                matmul(PS[0:ROWS, 5, 0:NCS], rsum[:, :], PSC[:, C_CMP:C_CMP + NCS], True, True).then_inc(sem("imp"), 1)
                pe.wait_ge(sem("cmp_g"), b * 2 + 2)
                for g in range(G):
                    for s in range(2):
                        n = P if s == 0 else NCS - P
                        last = matmul(PS[0:n, 4, s * P + g * HD:s * P + (g + 1) * HD],
                                      hgx[:, g * NCS + s * P:g * NCS + s * P + n], w2[:, 1, :], True, True)
                last.then_inc(sem("cmp_v"), 1)
                q = qbd[:, :, :, :].rearrange("p g r q -> p (g r q)")
                pe.wait_ge(sem("kt_ev"), b * 9 + 9)
                pe.wait_ge(sem("cmp_hx"), b * 2 + 2)
                for n in range(10):
                    if n >= 2:
                        pe.wait_ge(sem("sc_ev"), b * 11 + n)
                    if n == 0:
                        last = matmul(PS[0:ROWS, 2, 0:WIN], q, KTW, True, True)
                    elif n == 1:
                        last = matmul(PS[0:ROWS, 3, 0:2 * DS], q, knew[:, :, :].rearrange("p a q -> p (a q)"), True, True)
                    else:
                        last = matmul(PS[0:ROWS, 2 + n % 2, 0:512], q, KT[:, (n - 2) * 512:(n - 1) * 512], True, True)
                    last.then_inc(sem("sc_done"), 1)

            batch(0, False)
            with pe.Fori(1, DB) as b:
                batch(b, True)
            pe.wait_ge(sem("p_ready"), DB)
            tail(DB - 1)

            pe.wait_ge(sem("o_ev"), 2 * DB)
            for k in range(N_O):
                slot_ready(S_O, 0, k)
                for f in range(2):
                    pe.wait_ge(sem("res_free"), 2 * k + f + 1)
                    project(lambda c: wslot[(S_O + k) % RING][:, c, f * P:(f + 1) * P], f, MIXT).then_inc(sem("weights_used"), 1)
            pe.wait_ge(sem("x_res"), KD)
            ln_mean(1)
            ln_var(1)
            pe.wait_ge(sem("ln_u"), 2 * (KD + 1))

            def ffn_in(i, slots):
                for k in slots:
                    slot_ready(S_F1, i, k)
                    for f in range(2):
                        pe.wait_ge(sem("h_ready" if f else "gate_free"), i * RING + k + (2 if f else 1))
                        project(lambda c: wslot1[(S_F1 + k) % RING][:, c, f, :], f, U).then_inc(sem("weights_used"), 1)
            full = N_F1 // RING
            with pe.Fori(0, full) as i:
                ffn_in(i, range(RING))
            ffn_in(full, range(N_F1 - full * RING))
            pe.wait_ge(sem("h_ready"), N_F1 + 2)
            with pe.Fori(0, N_F2 // RING) as i:
                for k in range(RING):
                    f = k // 2
                    slot_ready(S_F2, i, k)
                    if k % 2 == 0:
                        pe.wait_ge(sem("res_free"), i * 2 + KD + f + 1)
                    w = wslot2[(S_F2 + k) % RING]
                    for c in range(KF // 2):
                        h = (k % 2) * (KF // 2) + c
                        matmul(dense[f][:, 0:LP], w[:, c, :], HT[:, h, 0:LP], h == 0, h == KF - 1)
                        last = matmul(dense[f][:, LP:NT], w[:, c, :], HT[:, h, LP:NT], h == 0, h == KF - 1)
                    last.then_inc(sem("weights_used"), 2)
            pe.wait_ge(sem("x_res"), 2 * KD)
            ln_mean(2)
            ln_var(2)

        @block.scalar
        def _(act):
            step = [0]

            def link(ins):
                step[0] += 1
                ins.then_inc(sem("act_step"), 1)
                act.wait_ge(sem("act_step"), step[0])

            def ln_act(nth, g, last=False):
                for k in range(KD):
                    act.wait_ge(sem("ln_cent"), nth * KD + k + 1)
                    nc.scalar.activation(SQ[:, k, :], XC[:, k, :], ACT.Square).then_inc(sem("ln_sq"), 1)
                act.wait_ge(sem("ln_rec"), nth + 1)
                nc.scalar.activation(rstd[:, :], rstd[:, :], ACT.Sqrt).then_inc(sem("ln_rstd"), 1)
                for k in range(KD):
                    act.wait_ge(sem("ln_h"), nth * KD + k + 1)
                    nc.scalar.activation(X[:, k, :], XC[:, k, :], ACT.Identity, bias=lnv[:, 2 * nth + 1, k:k + 1],
                                         scale=lnv[:, 2 * nth, k:k + 1]).then_inc(sem("ln_x"), 1)

            act.wait_ge(sem("consts_in"), 160)
            nc.scalar.activation(cth[:, :, :], cs[:, :, :], ACT.Tanh, scale=0.5).then_inc(sem("c_tanh"), 1)
            ln_act(0, 0)

            def copy_tiles(i, n):
                for t in range(n):
                    act.wait_ge(sem("weights_used"), i * 8 + 2 * S_IN + t + 1)
                    nc.scalar.activation(Z[:, bass.ds(i * 8 + t, 1), :].rearrange("p o t -> p (o t)"), dense[t % 2], ACT.Copy).then_inc(sem("dense_free"), 1)
            full = (N_IN - 1) // RING
            with act.Fori(0, full) as i:
                copy_tiles(i, 8)
            copy_tiles(full, ZT - 8 * full)
            act.wait_ge(sem("weights_used"), 2 * S_ADA2)
            nc.scalar.activation(zM[:, :], dense[0][0:MISC, :], ACT.Copy).then_inc(sem("dense_free"), 1)

            for t in range(TT + 1):
                n = P if t < TT else LS
                bank = 4 * (t % 2)
                for q, w in ((0, 512), (1, 512), (2, 256)):
                    act.wait_ge(sem("rows_t"), 3 * t + q + 1)
                    if q == 2:
                        nc.scalar.activation(GT[0:n, t, :], PS[0:n, bank + 2, 256:256 + MISC], ACT.Copy).then_inc(sem("gt"), 1)
                    nc.scalar.activation(VT[0:n, t, q * 512:q * 512 + w], PS[0:n, bank + q, 0:w], ACT.Copy).then_inc(sem("rows_ready"), 1)
            act.wait_ge(sem("gt"), TT + 1)
            nc.scalar.activation(GT[:, 0:TT, RANK:MISC], GT[:, 0:TT, RANK:MISC], ACT.Tanh, scale=0.5).then_inc(sem("gates_tanh"), 1)
            nc.scalar.activation(GT[0:LS, TT, RANK:MISC], GT[0:LS, TT, RANK:MISC], ACT.Tanh, scale=0.5).then_inc(sem("gates_tanh"), 1)

            for h in range(2):
                act.wait_ge(sem("decay_x"), h + 1)
                link(nc.scalar.activation(DM[:, h, :], stat[h], ACT.Abs, bias=ba[:, h:h + 1]))
            link(nc.scalar.activation(DL[:, :, :], DM[:, :, :], ACT.Exp, scale=-1.0))
            nc.scalar.activation(DM[:, :, :], DL[:, :, :], ACT.Ln, bias=1.0).then_inc(sem("decay_ln"), 1)
            act.wait_ge(sem("gla_sums"), 5)
            for n, (src, s) in enumerate(((DM, 1.0), (DM, -1.0), (BC, 1.0), (DL, 1.0))):
                nc.scalar.activation(E[n][:, :, :], src[:, :, :], ACT.Exp, scale=s / TAU).then_inc(sem("gla_exp"), 1)
            act.wait_ge(sem("gla_ket"), 1)
            for q in range(2):
                nc.scalar.activation(KE[:, 2 * q:2 * q + 2, :].rearrange("p t c -> p (t c)"), PS[:, 4 + q, :], ACT.Copy).then_inc(sem("gla_ke"), 1)
            nc.scalar.activation(KE[0:LS, TT, :], PS[0:LS, 6, 0:256], ACT.Copy).then_inc(sem("gla_ke"), 1)
            act.wait_ge(sem("gla_os"), 1)
            for h in range(GH):
                nc.scalar.activation(MIXT[:, h, LP:NT], PS[:, 4 + h % 2, h * LS:(h + 1) * LS], ACT.Copy).then_inc(sem("gla_cp"), 1)
            act.wait_ge(sem("gla_q"), 4)
            for h in range(GH):
                act.wait_ge(sem("gla_o"), h + 1)
                nc.scalar.activation(MIXT[:, h, 0:LP], PS[:, h, :], ACT.Copy).then_inc(sem("gla_cp"), 1)
            act.wait_ge(sem("gla_cp"), 2 * GH)
            act.wait_ge(sem("gla_o"), GH)
            for h in range(GH):
                nc.scalar.activation(SQG[:, h, :], MIXT[:, h, :], ACT.Square).then_inc(sem("gla_sq"), 1)
            nc.scalar.activation(TH, Z[:, ZRG:ZRG + GH, :], ACT.Tanh, scale=0.5).then_inc(sem("gla_th"), 1)
            for h in range(GH):
                act.wait_ge(sem("gla_rec"), h + 1)
                nc.scalar.activation(SQG[:, h, :], SQG[:, h, :], ACT.Sqrt).then_inc(sem("gla_rstd"), 1)

            for u in range(16):
                act.wait_ge(sem("segp_t"), u + 1)
                nc.scalar.activation(XTP[:, u, :, :].rearrange("p g n -> p (g n)"), PS[:, u % 2, 0:2 * NSEGP], ACT.Copy).then_inc(sem("segp_ev"), 1)
            act.wait_ge(sem("cbias"), 1)
            for c in range(2):
                act.wait_ge(sem("cmpp_mm"), 8 * (c + 1))
                nc.scalar.activation(HX[:, c, :, :].rearrange("p g n -> p (g n)"), PS[:, 2 + c, 0:2 * NCP], ACT.Identity,
                                     bias=cbias[:, c:c + 1]).then_inc(sem("cmpp_hx"), 1)
            act.wait_ge(sem("cmpp_poly"), 1)
            nc.scalar.activation(HG, HG, ACT.Tanh, scale=GELU_A).then_inc(sem("cmpp_tanh"), 1)

            with act.Fori(0, R) as r:
                act.wait_ge(sem("nsa_sc_used"), r * 8 + 2)
                nc.scalar.activation(qcur, Z[:, bass.ds(r + ZQN, 1), 0:LP].rearrange("p o t -> p (o t)"), ACT.Copy,
                                     scale=HD ** -0.5).then_inc(sem("nsa_q"), 1)
                for s in range(8):
                    i, g = s // 2, s % 2
                    w = (i + 1) * P
                    act.wait_ge(sem("nsa_max"), r * 8 + s + 1)
                    nc.scalar.activation(PB[g][:, 0:NCP], PB[g][:, 0:NCP], ACT.Exp, bias=pst[:, g, 1, 0:1]).then_inc(sem("nsa_exp"), 1)
                    for q in range(2):
                        v = PB[g][:, 32 + q * LP:32 + q * LP + w]
                        nc.scalar.activation(v, v, ACT.Exp, bias=pst[:, g, 1, q + 1:q + 2],
                                             accum_out=pst[:, g, 2, q + 1:q + 2]).then_inc(sem("nsa_exp"), 1)
                    act.wait_ge(sem("nsa_pt"), r * 24 + 3 * s + 1)
                    nc.scalar.activation(PTB[g][0:NCP, 0:P], PS[0:NCP, 4 + g, P:2 * P], ACT.Copy).then_inc(sem("nsa_ptev"), 1)
                    for q in range(2):
                        act.wait_ge(sem("nsa_pt"), r * 24 + 3 * s + 2 + q)
                        nc.scalar.activation(PTB[g][:, (1 + 4 * q) * P:(1 + 4 * q) * P + w], PS[:, 6 + q, 0:w], ACT.Copy).then_inc(sem("nsa_ptev"), 1)

            def exp_tail(b):
                for q, (c0, w) in enumerate(((C_WIN, WIN + DS), (C_XS, DS + PAST))):
                    act.wait_ge(sem("sc_max"), b * 3 + 2 + q)
                    nc.scalar.activation(PSC[:, c0:c0 + w], PSC[:, c0:c0 + w], ACT.Exp, bias=smx[:, 1, q:q + 1],
                                         accum_out=smx[:, 2, q:q + 1]).then_inc(sem("sc_exp"), 1)

            def seg_copy(b, u):
                act.wait_ge(sem("seg_t"), b * 16 + u + 1)
                for h in range(2):
                    nc.scalar.activation(seg_dst(u, h, 0), seg_src(u, h, 0), ACT.Copy).then_inc(sem("seg_ev"), 1)

            def batch(b, waited):
                if waited:
                    act.wait_ge(sem("sc_done"), b * 11)
                for g in range(G):
                    nc.scalar.activation(qbd[g * HD:(g + 1) * HD, g, :, :], zS[g * HD:(g + 1) * HD, 0:R, bass.ds(b * DS, DS)],
                                         ACT.Copy).then_inc(sem("batch_q"), 1)
                nc.scalar.activation(knew[:, :, :], zS[:, 4:6, bass.ds(b * DS, DS)], ACT.Copy).then_inc(sem("batch_q"), 1)
                for u in range(10):
                    seg_copy(b, u)
                act.wait_ge(sem("cmp_mm"), b * 16 + 8)
                if waited:
                    act.wait_ge(sem("cmp_g"), b * 2)
                nc.scalar.activation(HXS[:, :], PS[:, 2, 0:2 * NCS], ACT.Identity, bias=cbias[:, 0:1]).then_inc(sem("cmp_hx"), 1)
                if waited:
                    act.wait_ge(sem("p_ready"), b)
                nc.scalar.activation(gcur[:, :], grow[:, bass.ds(b, 1), :].rearrange("p o j -> p (o j)"), ACT.Copy).then_inc(sem("batch_g"), 1)
                seg_copy(b, 10)
                seg_copy(b, 11)
                act.wait_ge(sem("cmp_poly"), b * 2 + 1)
                nc.scalar.activation(hgx[:, :], hgx[:, :], ACT.Tanh, scale=GELU_A).then_inc(sem("cmp_tanh"), 1)
                seg_copy(b, 12)
                seg_copy(b, 13)
                act.wait_ge(sem("cmp_k"), b + 1)
                nc.scalar.activation(kcT[:, 0:NCS], PS[:, 4, 0:NCS], ACT.Copy, scale=0.5).then_inc(sem("cmp_kev"), 1)
                seg_copy(b, 14)
                seg_copy(b, 15)
                act.wait_ge(sem("sc_max"), b * 3 + 1)
                nc.scalar.activation(PSC[:, C_CMP:C_CMP + NCS], PSC[:, C_CMP:C_CMP + NCS], ACT.Exp, bias=smx[:, 1, 2:3],
                                     accum_out=smx[:, 2, 2:3]).then_inc(sem("sc_exp"), 1)
                act.wait_ge(sem("cmp_mm"), b * 16 + 16)
                nc.scalar.activation(HXS[:, :], PS[:, 3, 0:2 * NCS], ACT.Identity, bias=cbias[:, 1:2]).then_inc(sem("cmp_hx"), 1)
                if waited:
                    act.wait_ge(sem("sc_done"), b * 11)
                for n in range(9):
                    act.wait_ge(sem("kt_t"), b * 9 + n + 1)
                    dst = KT[:, n * 512:(n + 1) * 512] if n < 8 else KTW
                    nc.scalar.activation(dst, PS[:, n % 2, :], ACT.Copy).then_inc(sem("kt_ev"), 1)
                    if n == 2:
                        act.wait_ge(sem("cmp_poly"), b * 2 + 2)
                        nc.scalar.activation(hgx[:, :], hgx[:, :], ACT.Tanh, scale=GELU_A).then_inc(sem("cmp_tanh"), 1)
                exp_tail(b)

            act.wait_ge(sem("zs"), 6)
            act.wait_ge(sem("grow_in"), 16 * NH)
            batch(0, False)
            with act.Fori(1, DB) as b:
                batch(b, True)

            for k in range(KD):
                nc.scalar.activation(X[:, k, :], X[:, k, :], ACT.Copy, scale=ALPHA).then_inc(sem("x_alpha"), 1)
            ln_act(1, 2)
            act.wait_ge(sem("ln_u"), 2 * (KD + 1))
            for k in range(KD):
                nc.scalar.activation(X[:, k, :], X[:, k, :], ACT.Copy, scale=ALPHA).then_inc(sem("x_alpha"), 1)

            def gate(i, n):
                for k in range(n):
                    act.wait_ge(sem("weights_used"), i * 8 + 2 * S_F1 + 2 * k + 1)
                    act.wait_ge(sem("h_ready"), i * RING + k + 1)
                    nc.scalar.activation(SQ[:, k % 2, :], dense[0], ACT.Tanh, scale=0.5).then_inc(sem("gate_th"), 1)
            full = N_F1 // RING
            with act.Fori(0, full) as i:
                gate(i, RING)
            gate(full, N_F1 - full * RING)
            ln_act(2, 4)

        @block.vector
        def _(dve):
            step = [0]

            def link(ins):
                step[0] += 1
                ins.then_inc(sem("dve_step"), 1)
                dve.wait_ge(sem("dve_step"), step[0])

            def ln_dve(nth, chunk):
                dve.wait_ge(sem("ln_mean"), nth + 1)
                for k in range(KD):
                    nc.vector.tensor_tensor(XC[:, k, :], X[:, k, :], stat[0], ALU.subtract).then_inc(sem("ln_cent"), 1)
                dve.wait_ge(sem("ln_var"), nth + 1)
                link(nc.vector.tensor_scalar(rstd[:, :], stat[1], 1e-5, None, ALU.add))
                nc.vector.reciprocal(rstd[:, :], rstd[:, :]).then_inc(sem("ln_rec"), 1)
                dve.wait_ge(sem("ln_rstd"), nth + 1)
                for k in range(KD):
                    nc.vector.tensor_tensor(XC[:, k, :], XC[:, k, :], rstd[:, :], ALU.mult).then_inc(sem("ln_h"), 1)
                if chunk is None:
                    return
                for k in range(KD):
                    dve.wait_ge(sem("ln_x"), nth * KD + k + 1)
                    nc.vector.tensor_scalar(U[:, k, 0:LP], X[:, k, 0:LP], mod[:, chunk + 1, k, 0:1], mod[:, chunk, k, 0:1],
                                            ALU.mult, ALU.add).then_inc(sem("ln_u"), 1)
                us = U[:, :, LP:NT].rearrange("p k (b q) -> p k b q", q=DS)
                xs = X[:, :, LP:NT].rearrange("p k (b q) -> p k b q", q=DS)
                shp = [P, KD, DB, DS]
                link(nc.vector.tensor_tensor(us, xs, mod[:, chunk + 1, :, 1:NC].unsqueeze(3).to_broadcast(shp), ALU.mult))
                nc.vector.tensor_tensor(us, us, mod[:, chunk, :, 1:NC].unsqueeze(3).to_broadcast(shp), ALU.add).then_inc(sem("ln_u"), 1)

            def mod_copy(i, base, c):
                dve.wait_ge(sem("weights_used"), i * 8 + base)
                nc.vector.tensor_tensor(mod[:, bass.ds(c, 1), :, :].rearrange("p o k c -> p (o k) c"), pmods,
                                        bada[:, bass.ds(c, 1), :].rearrange("p o k -> p (o k)").unsqueeze(2).to_broadcast([P, KD, NC]),
                                        ALU.add).then_inc(sem("mod_free"), 1)

            dve.sem_inc(sem("mod_free"), 1)
            dve.sem_inc(sem("dense_free"), 2)
            dve.wait_ge(sem("c_tanh"), 1)
            link(nc.vector.scalar_tensor_tensor(out=cth[:, :, :], in0=cth[:, :, :], scalar=1.0, in1=cs[:, :, :], op0=ALU.add, op1=ALU.mult))
            nc.vector.tensor_scalar(cs[:, :, :], cth[:, :, :], 0.5, None, ALU.mult).then_inc(sem("silu_c"), 1)
            dve.wait_ge(sem("pidx"), 1)
            dve.wait_ge(sem("ptab_in"), 16)
            link(nc.vector.tensor_single_scalar(pmod[:, :], pidx[:, :], 3, op=ALU.bitwise_and))
            link(nc.vector.tensor_copy(pmodf[:, :], pmod[:, :]))
            nc.vector.tensor_scalar(idx[:, :], ptab[:, :], 4.0, None, ALU.mult).then_inc(sem("idx4"), 1)
            dve.wait_ge(sem("idx4"), 1)
            nc.vector.tensor_scalar(idx[:, :], idx[:, :], pmodf[:, 0:1], None, ALU.add).then_inc(sem("idx"), 1)
            dve.wait_ge(sem("pool_consts"), 1)
            for q in range(DS):
                link(nc.vector.tensor_scalar(smx[:, 0, 0:1], pmodf[0:ROWS, 0:1], float(q), NEG, ALU.is_ge, ALU.mult))
                link(nc.vector.tensor_copy(wpen[:, q * P:q * P + 1], smx[:, 0, 0:1]))
                link(nc.vector.tensor_scalar(smx[:, 0, 1:2], pmodf[0:ROWS, 0:1], float(q), NEG, ALU.is_lt, ALU.mult))
                link(nc.vector.tensor_copy(wpen[:, WIN + q:WIN + q + 1], smx[:, 0, 1:2]))
                link(nc.vector.tensor_copy(wpen[:, WIN + DS + q:WIN + DS + q + 1], smx[:, 0, 1:2]))
            link(nc.vector.tensor_copy(VMB[:, :, 0:DS], bmask[:, :].unsqueeze(2).to_broadcast([LS, DB, DS])))
            link(nc.vector.tensor_tensor(smask[:, :].rearrange("p (b q) -> p b q", q=DS), smask[:, :].rearrange("p (b q) -> p b q", q=DS),
                                         VMB[:, :, 0:DS], ALU.mult))

            dve.wait_ge(sem("ln_mean"), 1)
            for k in range(KD):
                nc.vector.tensor_tensor(XC[:, k, :], X[:, k, :], stat[0], ALU.subtract).then_inc(sem("ln_cent"), 1)
            mod_copy(0, 8, 0)
            dve.wait_ge(sem("ln_var"), 1)
            link(nc.vector.tensor_scalar(rstd[:, :], stat[1], 1e-5, None, ALU.add))
            nc.vector.reciprocal(rstd[:, :], rstd[:, :]).then_inc(sem("ln_rec"), 1)
            dve.wait_ge(sem("ln_rstd"), 1)
            for k in range(KD):
                nc.vector.tensor_tensor(XC[:, k, :], XC[:, k, :], rstd[:, :], ALU.mult).then_inc(sem("ln_h"), 1)
            mod_copy(0, 16, 1)
            dve.wait_ge(sem("mod_free"), 3)
            link(nc.vector.tensor_scalar(mod[:, 1, :, :], mod[:, 1, :, :], 1.0, None, ALU.add))
            for k in range(KD):
                dve.wait_ge(sem("ln_x"), k + 1)
                nc.vector.tensor_scalar(U[:, k, 0:LP], X[:, k, 0:LP], mod[:, 1, k, 0:1], mod[:, 0, k, 0:1],
                                        ALU.mult, ALU.add).then_inc(sem("ln_u"), 1)
            us = U[:, :, LP:NT].rearrange("p k (b q) -> p k b q", q=DS)
            xs = X[:, :, LP:NT].rearrange("p k (b q) -> p k b q", q=DS)
            shp = [P, KD, DB, DS]
            link(nc.vector.tensor_tensor(us, xs, mod[:, 1, :, 1:NC].unsqueeze(3).to_broadcast(shp), ALU.mult))
            nc.vector.tensor_tensor(us, us, mod[:, 0, :, 1:NC].unsqueeze(3).to_broadcast(shp), ALU.add).then_inc(sem("ln_u"), 1)

            with dve.Fori(0, N_ADA2 // RING) as i:
                mod_copy(i, 2 * S_ADA2 + 8, i + 2)
            dve.wait_ge(sem("mod_free"), 7)
            link(nc.vector.tensor_scalar(mod[:, 4, :, :], mod[:, 4, :, :], 1.0, None, ALU.add))

            dve.wait_ge(sem("gates_tanh"), 2)
            link(nc.vector.tensor_scalar(GT[:, 0:TT, RANK:MISC], GT[:, 0:TT, RANK:MISC], 0.5, 0.5, ALU.mult, ALU.add))
            nc.vector.tensor_scalar(GT[0:LS, TT, RANK:MISC], GT[0:LS, TT, RANK:MISC], 0.5, 0.5, ALU.mult, ALU.add).then_inc(sem("gates_ready"), 1)
            dve.wait_ge(sem("pe_bias"), 1)
            nc.vector.tensor_tensor(cbias[:, :], PS[:, 6, 0:2], cb1[:, :], ALU.add).then_inc(sem("cbias"), 1)

            dve.wait_ge(sem("decay_ln"), 1)
            for h in range(2):
                link(nc.vector.tensor_scalar(LA[:, h, :], stat[h], ba[:, h:h + 1], 0.0, ALU.add, ALU.min))
            link(nc.vector.tensor_tensor(LA[:, :, :], LA[:, :, :], DM[:, :, :], ALU.subtract))
            dve.wait_ge(sem("rmask"), 2)
            for h in range(2):
                link(nc.vector.tensor_tensor_scan(BC[:, h, :], rmask, LA[:, h, :], 0.0, ALU.mult, ALU.add))
            nc.vector.memset(S0P[:, 0, :], 0.0).then_inc(sem("gla_sums"), 1)
            nc.vector.memset(S1[:, 0, :], 0.0)
            for lo, hi, n, w in ((0, LP, NCH, CH), (LP, NT, DB, DS)):
                b4 = BC[:, :, lo:hi].rearrange("p h (c i) -> p h c i", i=w)
                shp4 = [P, 2, n, w]
                nc.vector.tensor_tensor(DM[:, :, lo:hi].rearrange("p h (c i) -> p h c i", i=w), b4,
                                        b4[:, :, :, w // 2 - 1:w // 2].to_broadcast(shp4), ALU.subtract).then_inc(sem("gla_sums"), 1)
                nc.vector.tensor_tensor(DL[:, :, lo:hi].rearrange("p h (c i) -> p h c i", i=w),
                                        b4[:, :, :, w - 1:w].to_broadcast(shp4), b4, ALU.subtract).then_inc(sem("gla_sums"), 1)
            dve.wait_ge(sem("gla_exp"), 4)
            dec = gdec[:, :, 0:NCH]
            decs = gdec[:, :, NCH:NCH + DB]
            nc.vector.tensor_copy(dec, E[2][:, :, CH - 1:LP:CH]).then_inc(sem("gla_dec"), 1)
            nc.vector.tensor_copy(decs, E[2][:, :, LP + DS - 1:NT:DS]).then_inc(sem("gla_dec"), 1)
            dve.wait_ge(sem("gla_dec"), 2)
            for n, z in ((0, ZQG), (1, ZKG), (2, ZQG), (3, ZKG)):
                nc.vector.scalar_tensor_tensor(out=E[n][:, :, :], in0=E[n][:, :, :], scalar=DK ** -0.5 if z == ZQG else 1.0,
                                               in1=Z[:, z:z + 2, :], op0=ALU.mult, op1=ALU.mult).then_inc(sem("gla_q"), 1)
            nc.vector.memset(ATT, 0.0).then_inc(sem("att_zero"), 1)
            dve.wait_ge(sem("gla_att"), 1)
            dve.wait_ge(sem("att_zero"), 1)
            for h2 in range(2):
                for c in range(4):
                    rows = slice(c * CH, (c + 1) * CH)
                    nc.vector.tensor_tensor(
                        RR[rows, 2 * GW:2 * GW + 16 * P].rearrange("p (a b t i) -> p a b t i", a=2, b=2, t=TT)[:, :, h2, :, rows],
                        PS[rows, h2, 0:256].rearrange("p (a t i) -> p a t i", a=2, t=TT),
                        gmask[rows, :].unsqueeze(1).unsqueeze(1).to_broadcast([CH, 2, TT, CH]), ALU.mult).then_inc(sem("gla_attm"), 1)
                nc.vector.tensor_tensor(ATTS.rearrange("p (a b) i -> p a b i", b=2)[:, :, h2, :],
                                        PS[0:LS, h2, 256:256 + 2 * LS].rearrange("p (a i) -> p a i", a=2),
                                        smask[:, :].unsqueeze(1).to_broadcast([LS, 2, LS]), ALU.mult).then_inc(sem("gla_attm"), 1)
            for h in range(2):
                dve.wait_ge(sem("gla_u"), h + 1)
                for c in range(NCH):
                    nc.vector.scalar_tensor_tensor(out=SST[h][:, c + 1, :], in0=SST[h][:, c, :], scalar=dec[:, h, c:c + 1],
                                                   in1=PS[:, 4 - 4 * h + c % 4, (c // 4) * P:(c // 4 + 1) * P],
                                                   op0=ALU.mult, op1=ALU.add).then_inc(sem("gla_scan"), 1)
                    dve.wait_ge(sem("gla_scan"), h * NCH + c + 1)
            for h in range(GH):
                if h >= 1:
                    dve.wait_ge(sem("gla_us"), h)
                nc.vector.tensor_tensor(VMB, VT[0:LS, TT, h * DV:(h + 1) * DV].unsqueeze(1).to_broadcast([LS, DB, DV]),
                                        bmask[:, :].unsqueeze(2).to_broadcast([LS, DB, DV]), ALU.mult).then_inc(sem("gla_vm"), 1)
                if h % 2 == 1:
                    dve.wait_ge(sem("gla_us"), h + 1)
                    dve.wait_ge(sem("gla_os"), 1)
                    hp = h // 2
                    for b in range(DB):
                        last = nc.vector.scalar_tensor_tensor(out=S0[:, hp, b, :], in0=S0[:, hp, b, :], scalar=decs[:, hp, b:b + 1],
                                                              in1=PS[:, 6 + b // 4, (b % 4) * P:(b % 4 + 1) * P], op0=ALU.mult, op1=ALU.add)
                    last.then_inc(sem("gla_snew"), 1)
            dve.wait_ge(sem("gla_th"), 1)
            link(nc.vector.scalar_tensor_tensor(out=TH, in0=TH, scalar=1.0, in1=Z[:, ZRG:ZRG + GH, :], op0=ALU.add, op1=ALU.mult))
            for h in range(GH):
                dve.wait_ge(sem("gla_ms"), h + 1)
                nc.vector.tensor_scalar(SQG[:, h, :], dense[h % 2], float(D // DV), 1e-6, ALU.mult, ALU.add).then_inc(sem("gla_ms_used"), 1)
                dve.wait_ge(sem("gla_ms_used"), h + 1)
                nc.vector.reciprocal(SQG[:, h, :], SQG[:, h, :]).then_inc(sem("gla_rec"), 1)
            for h in range(GH):
                dve.wait_ge(sem("gla_rstd"), h + 1)
                link(nc.vector.scalar_tensor_tensor(out=MIXT[:, h, :], in0=MIXT[:, h, :], scalar=gng[:, 0:1], in1=SQG[:, h, :], op0=ALU.mult, op1=ALU.mult))
                nc.vector.scalar_tensor_tensor(out=MIXT[:, h, :], in0=MIXT[:, h, :], scalar=0.5, in1=TH[:, h, :], op0=ALU.mult, op1=ALU.mult).then_inc(sem("gla_done"), 1)

            dve.wait_ge(sem("cmpp_hx"), 2)
            link(nc.vector.tensor_tensor(HG, HX, HX, ALU.mult))
            link(nc.vector.tensor_scalar(HG, HG, GELU_C, 1.0, ALU.mult, ALU.add))
            nc.vector.tensor_tensor(HG, HG, HX, ALU.mult).then_inc(sem("cmpp_poly"), 1)
            dve.wait_ge(sem("cmpp_tanh"), 1)
            nc.vector.scalar_tensor_tensor(out=HG.rearrange("p c g n -> p (c g n)"), in0=HG.rearrange("p c g n -> p (c g n)"), scalar=1.0,
                                           in1=HX.rearrange("p c g n -> p (c g n)"), op0=ALU.add, op1=ALU.mult).then_inc(sem("cmpp_g"), 2)
            dve.wait_ge(sem("cmpp_kv"), 2)
            nc.vector.tensor_scalar(kcTp, PS[:, 4, 0:NCP], 0.5, None, ALU.mult).then_inc(sem("cmpp_ev"), 1)
            nc.vector.tensor_scalar(vcp, PS[0:NCP, 5, 0:P], 0.5, None, ALU.mult).then_inc(sem("cmpp_ev"), 1)

            dve.wait_ge(sem("pcp"), 2)
            dve.sem_inc(sem("nsa_sc_used"), 2)
            dve.sem_inc(sem("nsa_ptev"), 1)
            base = step[0]
            PER = 1 + 8 * 7
            with dve.Fori(0, R) as r:
                count = [0]

                def lk(ins):
                    count[0] += 1
                    ins.then_inc(sem("dve_step"), 1)
                    dve.wait_ge(sem("dve_step"), r * PER + base + count[0])
                lk(nc.vector.tensor_copy(gpc, GT[:, 0:TT, bass.ds(r * 6 + RANK, 6)]))

                def prepare(s):
                    i, g = s // 2, s % 2
                    w = (i + 1) * P
                    pb, st = PB[g], pst[:, g]
                    pv = pb[:, 32:32 + 2 * LP].rearrange("p (q c) -> p q c", q=2)[:, :, 0:w]
                    dve.wait_ge(sem("nsa_sc"), r * 8 + s + 1)
                    dve.wait_ge(sem("nsa_pv"), r * 8 + s - 1) if s >= 2 else None
                    nc.vector.tensor_tensor(pv, PS[:, 2 * g:2 * g + 2, 0:w], pen[:, LP - w:LP].unsqueeze(1).to_broadcast([P, 2, w]), ALU.add)
                    lk(nc.vector.tensor_tensor(pb[:, 0:NCP], PS[:, 4 + g, 0:NCP], pcp[:, i, :], ALU.add))
                    nc.vector.tensor_reduce(st[:, 0, 1:3], pv, AX.X, ALU.max)
                    lk(nc.vector.tensor_reduce(st[:, 0, 0:1], pb[:, 0:NCP], AX.X, ALU.max))
                    nc.vector.tensor_scalar(st[:, 1, :], st[:, 0, :], -1.0, None, ALU.mult).then_inc(sem("nsa_max"), 1)

                def finish(s):
                    i, g = s // 2, s % 2
                    w = (i + 1) * P
                    pb, st = PB[g], pst[:, g]
                    dve.wait_ge(sem("nsa_exp"), r * 24 + 3 * (s + 1))
                    lk(nc.vector.tensor_tensor(pb[:, 0:NCP], pb[:, 0:NCP], mcp[:, i, :], ALU.mult))
                    lk(nc.vector.tensor_reduce(st[:, 2, 0:1], pb[:, 0:NCP], AX.X, ALU.add))
                    lk(nc.vector.tensor_scalar(st[:, 2, :], st[:, 2, :], 1e-30, None, ALU.max))
                    lk(nc.vector.reciprocal(st[:, 2, :], st[:, 2, :]))
                    lk(nc.vector.tensor_tensor(st[:, 3, :], st[:, 2, :], gpc[:, i, g * 3:g * 3 + 3], ALU.mult))
                    nc.vector.tensor_scalar(pb[:, 0:NCP], pb[:, 0:NCP], st[:, 3, 0:1], None, ALU.mult).then_inc(sem("nsa_p"), 1)
                    for q in range(2):
                        v = pb[:, 32 + q * LP:32 + q * LP + w]
                        nc.vector.tensor_scalar(v, v, st[:, 3, q + 1:q + 2], None, ALU.mult).then_inc(sem("nsa_p"), 1)

                def output(s):
                    i, g = s // 2, s % 2
                    dve.wait_ge(sem("nsa_pv"), r * 8 + s + 1)
                    o = nc.vector.tensor_copy(MIXT[g * HD:(g + 1) * HD, bass.ds(r + 4, 1), i * P:(i + 1) * P].rearrange("p o t -> p (o t)"),
                                              PS[g * HD:(g + 1) * HD, 4 + g, 2 * P:3 * P])
                    o.then_inc(sem("nsa_sc_used"), 1)

                prepare(0)
                for s in range(8):
                    finish(s)
                    if s + 1 < 8:
                        prepare(s + 1)
                    output(s)
                assert count[0] == PER, count[0]
            step[0] += PER * R
            dve.wait_ge(sem("nsa_sc_used"), 8 * R + 2)
            for r in range(R):
                nc.vector.tensor_scalar(zS[:, r, :], Z[:, ZQN + r, LP:NT], HD ** -0.5, None, ALU.mult).then_inc(sem("zs"), 1)
            nc.vector.tensor_copy(zS[:, 4, :], Z[:, ZKV + 4, LP:NT]).then_inc(sem("zs"), 1)
            nc.vector.tensor_copy(zS[:, 5, :], Z[:, ZKV + 2, LP:NT]).then_inc(sem("zs"), 1)
            dve.wait_ge(sem("zs"), 6)

            sbase = step[0]
            SPER = 20

            def tail(b):
                for q in range(3):
                    n = min(16, NPT - 16 * q)
                    dve.wait_ge(sem("pt_t"), b * 3 + q + 1)
                    if q == 0:
                        nc.vector.tensor_copy(PTS[:, 0:4, :], PS[:, 4, 0:4 * ROWS].rearrange("p (n r) -> p n r", r=ROWS))
                        nc.vector.tensor_copy(PTS[0:2 * DS, 4, :], PS[0:2 * DS, 4, 4 * ROWS:5 * ROWS])
                        last = nc.vector.tensor_copy(PTS[:, 5:16, :], PS[:, 4, 5 * ROWS:16 * ROWS].rearrange("p (n r) -> p n r", r=ROWS))
                    elif q == 1:
                        last = nc.vector.tensor_copy(PTS[:, 16:32, :], PS[:, 5, :].rearrange("p (n r) -> p n r", r=ROWS))
                    else:
                        nc.vector.tensor_copy(PTS[:, 32:NPT - 1, :], PS[:, 6, 0:(NPT - 33) * ROWS].rearrange("p (n r) -> p n r", r=ROWS))
                        last = nc.vector.tensor_copy(PTS[0:NCS - P, NPT - 1, :], PS[0:NCS - P, 6, (NPT - 33) * ROWS:(NPT - 32) * ROWS])
                    last.then_inc(sem("pt_ev"), 1)
                dve.wait_ge(sem("pv_done"), b + 1)
                for g in range(G):
                    rows = slice(g * HD, (g + 1) * HD)
                    nc.vector.tensor_copy(MIXT[rows, R:2 * R, bass.ds(b * DS + LP, DS)],
                                          PS[rows, 7, g * R * DS:(g + 1) * R * DS].rearrange("p (r q) -> p r q", r=R)).then_inc(sem("o_ev"), 1)

            def batch(b, waited):
                count = [0]

                def lk(ins):
                    count[0] += 1
                    ins.then_inc(sem("dve_step"), 1)
                    dve.wait_ge(sem("dve_step"), b * SPER + sbase + count[0])

                def seg_copy(u):
                    dve.wait_ge(sem("seg_t"), b * 16 + u + 1)
                    for h in range(2):
                        nc.vector.tensor_copy(seg_dst(u, h, 1), seg_src(u, h, 1)).then_inc(sem("seg_dve"), 1)

                def gelu_poly(c):
                    dve.wait_ge(sem("cmp_hx"), b * 2 + c + 1)
                    if c == 1:
                        dve.wait_ge(sem("cmp_k"), b + 1)
                    elif waited:
                        dve.wait_ge(sem("cmp_v"), b)
                    lk(nc.vector.tensor_tensor(hgx[:, :], HXS[:, :], HXS[:, :], ALU.mult))
                    lk(nc.vector.tensor_scalar(hgx[:, :], hgx[:, :], GELU_C, 1.0, ALU.mult, ALU.add))
                    nc.vector.tensor_tensor(hgx[:, :], hgx[:, :], HXS[:, :], ALU.mult).then_inc(sem("cmp_poly"), 1)

                def gelu_last(c):
                    dve.wait_ge(sem("cmp_tanh"), b * 2 + c + 1)
                    nc.vector.scalar_tensor_tensor(out=hgx[:, :], in0=hgx[:, :], scalar=1.0, in1=HXS[:, :], op0=ALU.add, op1=ALU.mult
                                                   ).then_inc(sem("cmp_g"), 1)

                def maximum(c0, w, q):
                    lk(nc.vector.tensor_reduce(smx[:, 0, q:q + 1], PSC[:, c0:c0 + w], AX.X, ALU.max))
                    nc.vector.tensor_scalar(smx[:, 1, q:q + 1], smx[:, 0, q:q + 1], -1.0, None, ALU.mult).then_inc(sem("sc_max"), 1)

                for u in range(10):
                    seg_copy(u)
                if waited:
                    tail(b - 1)
                seg_copy(10)
                gelu_poly(0)
                for u in (11, 12, 13):
                    seg_copy(u)
                gelu_last(0)
                seg_copy(14)
                seg_copy(15)
                dve.wait_ge(sem("sc_done"), b * 11 + 1)
                nc.vector.tensor_copy(PSC[:, C_CMP:C_CMP + NCS], PS[0:ROWS, 6, 0:NCS]).then_inc(sem("sc_ev"), 1)
                dve.wait_ge(sem("sc_ev"), b * 11 + 1)
                maximum(C_CMP, NCS, 2)
                dve.wait_ge(sem("sc_exp"), b * 3 + 1)
                lk(nc.vector.reciprocal(smx[:, 3, 2:3], smx[:, 2, 2:3]))
                nc.vector.tensor_scalar(PSC[:, C_CMP:C_CMP + NCS], PSC[:, C_CMP:C_CMP + NCS], smx[:, 3, 2:3], None, ALU.mult).then_inc(sem("pc_ready"), 1)
                gelu_poly(1)
                gelu_last(1)
                dve.wait_ge(sem("imp"), b + 1)
                lk(nc.vector.tensor_copy(impA[:, 4:4 + NCS], PS[0:ROWS, 5, 0:NCS]))
                lk(nc.vector.tensor_reduce(score[:, 0, :], impA[:, 4:4 + 4 * NB].rearrange("p (j n) -> p j n", n=4), AX.X, ALU.add))
                lk(nc.vector.tensor_tensor(score[:, 0, :], score[:, 0, :], impA[:, 3:3 + 4 * NB:4], ALU.add))
                lk(nc.vector.tensor_tensor(score[:, 0, :], score[:, 0, :], bpen[:, :], ALU.add))

                def pause():
                    nc.vector.tensor_copy(smx[:, 3, 0:1], smx[:, 3, 2:3])

                for n in range(2):
                    pause()
                    lk(nc.vector.max(top8[:, n, :], score[:, n, :]))
                    pause()
                    lk(nc.vector.match_replace(score[:, n + 1, :], top8[:, n, :], score[:, n, :], -3e38))
                lk(nc.vector.tensor_scalar(spen[:, :], score[:, 2, :], -1e38, NEG, ALU.is_gt, ALU.mult))
                dve.wait_ge(sem("cmp_v"), b + 1)
                nc.vector.tensor_scalar(vc[:, 0, :], PS[:, 4, 0:P], 0.5, None, ALU.mult)
                lk(nc.vector.tensor_scalar(vc[0:NCS - P, 1, :], PS[0:NCS - P, 4, P:2 * P], 0.5, None, ALU.mult))
                dve.wait_ge(sem("batch_g"), b + 1)
                for n in range(10):
                    dve.wait_ge(sem("sc_done"), b * 11 + 2 + n)
                    if n == 0:
                        last = nc.vector.tensor_tensor(PSC[:, 0:WIN], PS[0:ROWS, 2, :], wpen[:, 0:WIN], ALU.add)
                    elif n == 1:
                        last = nc.vector.tensor_tensor(PSC[:, C_XW:C_XW + 2 * DS], PS[0:ROWS, 3, 0:2 * DS], wpen[:, WIN:WIN + 2 * DS], ALU.add)
                    else:
                        last = nc.vector.tensor_tensor(
                            PSC[:, C_SLC + (n - 2) * 512:C_SLC + (n - 1) * 512].rearrange("p (t j e) -> p t j e", t=4, e=2),
                            PS[0:ROWS, 2 + n % 2, :].rearrange("p (t j e) -> p t j e", t=4, e=2),
                            spen[:, 0:NB - 1].unsqueeze(1).unsqueeze(3).to_broadcast([ROWS, 4, NB - 1, 2]), ALU.add)
                    last.then_inc(sem("sc_ev"), 1)
                    if n == 1:
                        dve.wait_ge(sem("sc_ev"), b * 11 + 3)
                        maximum(C_WIN, WIN + DS, 0)
                dve.wait_ge(sem("sc_ev"), b * 11 + 11)
                maximum(C_XS, DS + PAST, 1)
                dve.wait_ge(sem("sc_exp"), b * 3 + 3)
                lk(nc.vector.reciprocal(smx[:, 3, 0:2], smx[:, 2, 0:2]))
                nc.vector.tensor_tensor(smx[:, 3, 0:1], smx[:, 3, 0:1], gcur[:, 2:3], ALU.mult)
                lk(nc.vector.tensor_tensor(smx[:, 3, 1:2], smx[:, 3, 1:2], gcur[:, 1:2], ALU.mult))
                nc.vector.tensor_scalar(PSC[:, C_CMP:C_CMP + NCS], PSC[:, C_CMP:C_CMP + NCS], gcur[:, 0:1], None, ALU.mult)
                nc.vector.tensor_scalar(PSC[:, C_WIN:C_WIN + WIN + DS], PSC[:, C_WIN:C_WIN + WIN + DS], smx[:, 3, 0:1], None, ALU.mult)
                nc.vector.tensor_scalar(PSC[:, C_XS:C_XS + DS + PAST], PSC[:, C_XS:C_XS + DS + PAST], smx[:, 3, 1:2], None, ALU.mult).then_inc(sem("p_ready"), 1)
                assert count[0] == SPER, count[0]

            batch(0, False)
            with dve.Fori(1, DB) as b:
                batch(b, True)
            step[0] += SPER * DB
            tail(DB - 1)

            dve.sem_inc(sem("res_free"), 2)
            dve.wait_ge(sem("x_alpha"), KD)
            for f in range(KD):
                dve.wait_ge(sem("weights_used"), 2 * S_O + f + 1)
                if f:
                    dve.wait_ge(sem("x_res"), f)
                ga = mod[:, 2, f, :]
                x = X[:, f, :]
                nc.vector.scalar_tensor_tensor(out=x[:, 0:LP], in0=dense[f % 2][:, 0:LP], scalar=ga[:, 0:1], in1=x[:, 0:LP],
                                               op0=ALU.mult, op1=ALU.add)
                t = rstd[:, 0:LS].rearrange("p (b q) -> p b q", q=DS)
                nc.vector.tensor_tensor(t, dense[f % 2][:, LP:NT].rearrange("p (b q) -> p b q", q=DS),
                                        ga[:, 1:NC].unsqueeze(2).to_broadcast([P, DB, DS]), ALU.mult).then_inc(sem("res_free"), 1)
                dve.wait_ge(sem("res_free"), f + 3)
                nc.vector.tensor_tensor(x[:, LP:NT], x[:, LP:NT], rstd[:, 0:LS], ALU.add).then_inc(sem("x_res"), 1)
            dve.wait_ge(sem("x_res"), KD)
            ln_dve(1, 3)

            dve.sem_inc(sem("gate_free"), 1)
            dve.sem_inc(sem("h_ready"), 2)

            def hidden(i, n):
                for k in range(n):
                    dve.wait_ge(sem("gate_th"), i * RING + k + 1)
                    th = SQ[:, k % 2, :]
                    nc.vector.scalar_tensor_tensor(out=th, in0=th, scalar=1.0, in1=dense[0], op0=ALU.add, op1=ALU.mult).then_inc(sem("gate_free"), 1)
                    dve.wait_ge(sem("gate_free"), i * RING + k + 2)
                    dve.wait_ge(sem("weights_used"), i * 8 + 2 * S_F1 + 2 * k + 2)
                    nc.vector.scalar_tensor_tensor(out=HT[:, bass.ds(i * RING + k, 1), :].rearrange("p o t -> p (o t)"), in0=dense[1],
                                                   scalar=0.5, in1=th, op0=ALU.mult, op1=ALU.mult).then_inc(sem("h_ready"), 1)
            full = N_F1 // RING
            with dve.Fori(0, full) as i:
                hidden(i, RING)
            hidden(full, N_F1 - full * RING)

            dve.wait_ge(sem("x_alpha"), 2 * KD)
            with dve.Fori(0, KD // 2) as i:
                for f in range(2):
                    nc.vector.tensor_copy(gares[:, f, :], mod[:, 5, bass.ds(i * 2 + f, 1), :].rearrange("p o c -> p (o c)")).then_inc(sem("gares"), 1)
                    dve.wait_ge(sem("gares"), i * 2 + f + 1)
                    ga = gares[:, f, :]
                    dve.wait_ge(sem("weights_used"), i * 8 + 2 * S_F2 + 4 * (f + 1))
                    dve.wait_ge(sem("x_res"), i * 2 + KD + f)
                    x = X[:, bass.ds(i * 2 + f, 1), :].rearrange("p o t -> p (o t)")
                    nc.vector.scalar_tensor_tensor(out=x[:, 0:LP], in0=dense[f][:, 0:LP], scalar=ga[:, 0:1], in1=x[:, 0:LP],
                                                   op0=ALU.mult, op1=ALU.add)
                    t = rstd[:, 0:LS].rearrange("p (b q) -> p b q", q=DS)
                    nc.vector.tensor_tensor(t, dense[f][:, LP:NT].rearrange("p (b q) -> p b q", q=DS),
                                            ga[:, 1:NC].unsqueeze(2).to_broadcast([P, DB, DS]), ALU.mult).then_inc(sem("res_free"), 1)
                    dve.wait_ge(sem("res_free"), i * 2 + KD + f + 3)
                    nc.vector.tensor_tensor(x[:, LP:NT], x[:, LP:NT], rstd[:, 0:LS], ALU.add).then_inc(sem("x_res"), 1)
            dve.wait_ge(sem("x_res"), 2 * KD)
            ln_dve(2, None)


_OUTS = [(P, KD, NT), (GH, DK, DV), (DB, GH, DK, DV), (LP, KVW), (LS, KVW), (LP, KVW), (LS, KVW), (LP, KVW), (DB, WIN, KVW)]


def kernel(**inputs):
    import numpy as np
    import concourse.bacc as bacc
    from concourse import mybir as mb
    from concourse.bass_utils import run_bass_kernel_spmd

    v = {k: np.asarray(x) for k, x in inputs.items()}

    def rows(m):
        return m.reshape(-1, KD, P).transpose(2, 1, 0)

    def tiles(w, per):
        k, f = w.shape
        return w.reshape(k // P, P, f // (P * per), per * P).transpose(2, 1, 0, 3).reshape(f // (P * per), P, -1)

    def vec(x):
        return x.reshape(-1, P).T

    w_in = v["w_in"][0]
    cut = np.cumsum([256, 256, 512, RANK, 512, 512, KVW, KVW, KVW])
    q_g, k_g, v_g, a_g, r_g, q_n, kc, ks, kw, g_n = np.split(w_in, cut, axis=1)
    q_n = q_n.reshape(D, G, R, HD).transpose(0, 2, 1, 3).reshape(D, -1)
    g_n = g_n.reshape(D, G, R, 3).transpose(0, 2, 1, 3).reshape(D, -1)
    w_main = np.concatenate([q_g, k_g, v_g, r_g, q_n, kc, ks, kw], axis=1)
    w_misc = np.concatenate([a_g, g_n], axis=1)
    w_o = v["w_o"][0]
    w_o = np.concatenate([w_o[:GH * DV], w_o[GH * DV:].reshape(G, R, HD, D).transpose(1, 0, 2, 3).reshape(-1, D)])
    f1 = v["w_ffn_in"][0].reshape(KD, P, 2, KF, P).transpose(3, 1, 0, 2, 4).reshape(KF, P, -1)
    f2 = v["w_ffn_out"][0].reshape(2, KF // 2, P, KD, P).transpose(3, 0, 2, 1, 4).reshape(2 * KD, P, -1)
    ins = {
        "x_t": rows(np.concatenate([v["x_prompt"].reshape(LP, D), v["x_sample"].reshape(LS, D)])),
        "c_t": rows(np.concatenate([v["c_prompt"], v["c_sample"]])),
        "w_ada": tiles(v["w_ada"][0], 2), "b_ada": vec(v["b_ada"][0]).reshape(P, 6, KD),
        "lnv": np.stack([vec(v[n].reshape(-1)) for n in ("ln_in_g", "ln_in_b", "ln1_g", "ln1_b", "ln2_g", "ln2_b")], 1),
        "w_in": tiles(w_main, 2), "w_misc": w_misc.reshape(KD, P, MISC).transpose(1, 0, 2).reshape(P, -1),
        "wa2": v["gla_w_a2"][0], "ba": vec(v["gla_b_a"][0]), "gng": v["gla_norm_g"][0].reshape(P, 1),
        "pe": v["cmp_pe"][0].reshape(2, JP, 2, 2, HD).transpose(2, 4, 3, 0, 1).reshape(P, 2, 2, JP),
        "w1": v["cmp_w1"][0].reshape(2, 2, JP, P, HID).transpose(3, 0, 1, 2, 4),
        "b1": v["cmp_b1"][0].T, "w2": v["cmp_w2"][0].transpose(1, 0, 2),
        "w_o": tiles(w_o, 2), "w_f1": f1, "w_f2": f2,
        "state": v["state_gla"][0].reshape(DB, 2, 2 * DK, DV).transpose(2, 1, 0, 3),
        "ptab": v["page_table"].T,
        "cmp": v["cache_cmp_kv"][0].reshape(-1, SPAN * KVW), "slc": v["cache_slc_kv"][0].reshape(-1, SPAN * KVW),
        "win": v["cache_win_kv"][0].reshape(DB, WIN, KVW),
    }
    nc = bacc.Bacc("TRN2", target_bir_lowering=False, num_devices=1, dynamic_dma_scratch_size=4096)
    arrays, aps = {}, {}
    for name, x in ins.items():
        x = np.ascontiguousarray(x)
        arrays[f"in_{name}_dram"] = x
        aps[name] = nc.dram_tensor(f"in_{name}_dram", x.shape, mb.dt.from_np(x.dtype), kind="ExternalInput").ap()
    outs = [nc.dram_tensor(f"out_{i}_dram", s, F32, kind="ExternalOutput").ap() for i, s in enumerate(_OUTS)]
    build(nc, aps, outs)
    res = run_bass_kernel_spmd(nc, [arrays], core_ids=[0]).results[0]
    y, gp, gs, cp, c_s, slp, sls, wp, ws = (res[f"out_{i}_dram"] for i in range(len(_OUTS)))
    y = y.transpose(2, 1, 0).reshape(NT, D)
    kv = (2, G, HD)
    return (y[:LP].reshape(1, LP, D), y[LP:].reshape(DB, DS, D), gp.reshape(1, 1, GH, DK, DV), gs.reshape(1, DB, GH, DK, DV),
            cp.reshape(1, 1, LP, *kv), c_s.reshape(1, DB, DS, *kv), slp.reshape(1, 1, LP, *kv), sls.reshape(1, DB, DS, *kv),
            wp.reshape(1, 1, LP, *kv), ws.reshape(1, DB, WIN, *kv))
```

```python
from contextlib import ExitStack

import concourse.bass as bass
from concourse import mybir

ALU = mybir.AluOpType
ACT = mybir.ActivationFunctionType
F32 = mybir.dt.float32
I32 = mybir.dt.int32
U32 = mybir.dt.uint32
AX = mybir.AxisListType

P = 128
D = 1024
KD = D // P
LP = 512
TT = LP // P
DB, DS = 8, 4
LS = DB * DS
NT = LP + LS
NC = 1 + DB
FF = 2816
KF = FF // P
ALPHA = 2.0 ** 0.25

GH, DK, DV = 4, 64, 128
RANK, TAU = 16, 16.0
CH = 32
NCH = LP // CH
NH, G, R, HD = 8, 2, 4, 64
ROWS = G * R * DS
KVW = 2 * G * HD
PAGES, PSZ = 32, 128
PAST = PAGES * PSZ
WIN = 512
SPAN = PAST // P
SEG = 16
NSEG = PAST // SEG
NCS = NSEG - 1
NSEGP = LP // SEG
NCP = NSEGP - 1
HID = 128
JP = SEG // 2
NB = PAST // 64 + 1
NEG = -1e30
GELU_A, GELU_C = 0.7978845608028654, 0.044715

ZQG, ZKG, ZVG, ZRG, ZQN, ZKV = 0, 2, 4, 8, 12, 16
ZT = 22
MISC = RANK + 3 * NH

C_WIN, C_XW, C_XS, C_SLC, C_CMP = 0, WIN, WIN + DS, WIN + 2 * DS, WIN + 2 * DS + PAST
C_ALL = C_CMP + NCS + 1
NPT = 4 + SPAN + 2 + 2
PART = (DS + PAST) // 4

RING, SLOT = 4, 2 * P * KD
N_ADA1, N_IN, N_ADA2, N_O, N_F1, N_F2 = 8, 12, 16, 4, 22, 16
S_IN = N_ADA1
S_ADA2 = S_IN + N_IN
S_O = S_ADA2 + N_ADA2
S_F1 = S_O + N_O
S_F2 = S_F1 + N_F1
S_END = S_F2 + N_F2


def build(nc, a, out):
    (y_t, gla_p, gla_s, cmp_p, cmp_s, slc_p, slc_s, win_p, win_s) = out
    gate_scr = nc.dram_tensor("gate_scr", (LS, R, G, 3), F32, kind="Internal").ap()

    with ExitStack() as ctx:
        def sb(name, shape, dt=F32):
            return ctx.enter_context(nc.sbuf_tensor(name, shape, dt))

        sems = {}

        def sem(name):
            if name not in sems:
                sems[name] = ctx.enter_context(nc.semaphore(name))
            return sems[name]

        RX = sb("trunk", [P, KD * NT])
        RM = sb("mixreg", [P, KD * NT])
        RZ = sb("zreg", [P, ZT * NT])
        W1 = sb("w1", [P, 2, 2, JP, HID])
        RR = sb("ringreg", [P, RING * SLOT])
        RC = sb("creg", [P, SPAN * KVW])
        RS = sb("sreg", [P, SPAN * KVW + 4 * KVW])

        X = RX[:, :].rearrange("p (k t) -> p k t", k=KD)
        XC = RM[:, :].rearrange("p (k t) -> p k t", k=KD)
        MIXT = XC
        U = RC[:, 0:KD * NT].rearrange("p (k t) -> p k t", k=KD)
        SQ = RS[:, 0:KD * NT].rearrange("p (k t) -> p k t", k=KD)
        Z = RZ[:, :].rearrange("p (k t) -> p k t", k=ZT)
        HT = Z
        ring = [RR[:, s * SLOT:(s + 1) * SLOT] for s in range(RING)]
        wslot = [r.rearrange("p (k c) -> p k c", k=KD) for r in ring]
        wslot1 = [r.rearrange("p (k h c) -> p k h c", k=KD, h=2) for r in ring]
        wslot2 = [r[:, 0:KF // 2 * P].rearrange("p (k c) -> p k c", c=P) for r in ring]

        ident = sb("ident", [P, P])
        ones = sb("ones", [P, P])
        pen = sb("pen", [P, LP])
        mod = sb("mod", [P, 6, KD, NC])
        cs = sb("cs", [P, KD, NC])
        cth = sb("cth", [P, KD, NC])
        bada = sb("bada", [P, 6, KD])
        lnv = sb("lnv", [P, 6, KD])
        rstd = sb("rstd", [P, NT])
        w2 = sb("w2", [P, 2, HD])
        pe_t = sb("pe_t", [P, 2, 2, JP])
        cb1 = sb("cb1", [P, 2])
        cbias = sb("cbias", [P, 2])
        wa2 = sb("wa2", [RANK, GH * DK])
        ba = sb("ba", [P, 2])
        gng = sb("gng", [P, 1])
        zM = sb("zM", [MISC, NT])
        GT = sb("GT", [P, TT + 1, MISC])
        zS = sb("zS", [P, 8, LS])
        grow = sb("grow", [ROWS, DB, 3])
        ptab = sb("ptab", [P, DB], I32)
        idx = sb("idx", [P, DB], U32)
        pidx = sb("pidx", [P, 1], I32)
        pmod = sb("pmod", [P, 1], I32)
        pmodf = sb("pmodf", [P, 1])
        qbd = sb("qbd", [P, G, R, DS])
        knew = sb("knew", [P, 2, DS])
        gcur = sb("gcur", [ROWS, 3])
        VX = sb("VX", [DS, 2, P])
        bpen = sb("bpen", [ROWS, NB])
        spen = sb("spen", [ROWS, NB])
        rsum = sb("rsum", [ROWS, ROWS])
        impA = sb("impA", [ROWS, 4 * (NB + 1)])
        score = sb("score", [ROWS, 3, NB])
        top8 = sb("top8", [ROWS, 2, 8])
        smx = sb("smx", [ROWS, 4, 3])
        pmx = sb("pmx", [ROWS, 2, 4])
        gdec = sb("gdec", [P, 2, NCH + DB])
        gares = sb("gares", [P, 2, NC])
        wpen = sb("wpen", [ROWS, WIN + 2 * DS])

        PS = ctx.enter_context(nc.psum_tensor("PS", [P, 8, 512], F32))
        PF = PS[:, :, :].rearrange("p b c -> p (b c)")
        dense = [PF[:, (4 + 2 * b) * 512:(4 + 2 * b) * 512 + NT] for b in range(2)]
        stat = [PF[:, 2 * b * 512:2 * b * 512 + NT] for b in range(2)]
        pmods = PS[:, 4, 0:KD * NC].rearrange("p (k c) -> p k c", k=KD)

        VW = DV * GH + 3 * KVW
        VT = RS[:, 0:(TT + 1) * VW].rearrange("p (t c) -> p t c", t=TT + 1)
        S1 = RS[:, (TT + 1) * VW:(TT + 1) * VW + (NCH + 1) * P].rearrange("p (c v) -> p c v", c=NCH + 1)
        GW = 2 * NT
        LA, BC, DM, DL = (RR[:, i * GW:(i + 1) * GW].rearrange("p (h t) -> p h t", h=2) for i in range(4))
        ATT = RR[:, 2 * GW:2 * GW + 16 * P].rearrange("p (h t i) -> p h t i", h=GH, t=TT)
        SQG = RR[:, 0:GH * NT].rearrange("p (h t) -> p h t", h=GH)
        S0 = RR[:, 4 * GW:4 * GW + 2 * DB * P].rearrange("p (h b v) -> p h b v", h=2, b=DB)
        KE = RR[:, 6400:6400 + (TT + 1) * 256].rearrange("p (t c) -> p t c", t=TT + 1)
        ATTS = RR[0:LS, 7680:7680 + GH * LS].rearrange("p (h i) -> p h i", h=GH)
        E = [RC[:, i * GW:(i + 1) * GW].rearrange("p (h t) -> p h t", h=2) for i in range(4)]
        TH = RC[:, 0:GH * NT].rearrange("p (h t) -> p h t", h=GH)
        S0P = RC[:, 4 * GW:4 * GW + (NCH + 1) * P].rearrange("p (c v) -> p c v", c=NCH + 1)
        SST = [S0P, S1]
        VMB = RC[0:LS, 6528:6528 + DB * P].rearrange("p (b v) -> p b v", b=DB)
        rmask = RC[:, 7552:7552 + NT]
        gmask = sb("gmask", [P, CH])
        smask = sb("smask", [LS, LS])
        bmask = sb("bmask", [LS, DB])

        CP = RC[0:NSEGP, 0:SEG * KVW]
        CPV = CP.rearrange("p (c g j x) -> p c g j x", c=2, g=G, j=JP)
        XTP = RZ[:, 0:16 * 64].rearrange("p (u g n) -> p u g n", u=16, g=G)
        HX = RZ[:, 1024:1024 + 62 * 2].rearrange("p (c g n) -> p c g n", c=2, g=G)
        HG = RZ[:, 1152:1152 + 62 * 2].rearrange("p (c g n) -> p c g n", c=2, g=G)
        kcTp = RZ[:, 1280:1280 + NCP]
        vcp = RZ[0:NCP, 1312:1312 + P]
        pcp = RZ[:, 1440:1440 + TT * NCP].rearrange("p (t n) -> p t n", t=TT)
        PCT = RZ[0:NCP, 2048:2048 + G * R * LP].rearrange("p (h t) -> p h t", h=G * R)
        PB = [RR[:, b * 1024:(b + 1) * 1024] for b in range(3)]
        PTB = [RR[:, 3072 + b * 1024:3072 + (b + 1) * 1024] for b in range(2)]
        qcur = RR[:, 5120:5120 + 2 * LP].rearrange("p (r t) -> p r t", r=2)
        pst = RR[:, 6144:6144 + 2 * 8].rearrange("p (b k j) -> p b k j", b=2, k=4)
        gpc = RR[:, 6160:6160 + 2 * TT * 6].rearrange("p (r t c) -> p r t c", r=2, t=TT)
        PCW = R * TT * NCP
        pc = RR[:, 6208:6208 + G * PCW]
        pcst = RR[:, 7200:7200 + 3 * G * R * TT].rearrange("p (k j) -> p k j", k=3)

        CB = RC[:, :].rearrange("p (e s c x) -> p e s c x", e=2, s=SEG, c=2)
        SBF = RS[:, 0:SPAN * KVW]
        SBV = SBF.rearrange("p (t c x) -> p t c x", t=SPAN, c=2)
        WBF = RS[:, SPAN * KVW:SPAN * KVW + 4 * KVW]
        WBV = WBF.rearrange("p (t c x) -> p t c x", t=4, c=2)
        XTS = RR[:, :].rearrange("p (u g n) -> p u g n", u=16, g=G)
        KT = RZ[:, 0:SPAN * P]
        KTW = RZ[:, 4096:4096 + WIN]
        PSC = RZ[0:ROWS, 4608:4608 + C_ALL]
        PTS = RZ[:, 4608 + C_ALL:4608 + C_ALL + NPT * ROWS].rearrange("p (n r) -> p n r", r=ROWS)
        o_ = 4608 + C_ALL + NPT * ROWS
        kcT = RZ[:, o_:o_ + NSEG]
        vc = sb("vc", [P, 2, P])
        hgx = RZ[:, o_ + NSEG:o_ + NSEG + 2 * NCS]
        osb = RZ[0:ROWS, o_ + NSEG + 2 * NCS:o_ + NSEG + 2 * NCS + P]
        assert o_ + NSEG + 2 * NCS + P <= ZT * NT
        HXS = sb("hxs", [P, 2 * NCS])

        def seg_src(u, h, g):
            return PS[g * HD:(g + 1) * HD, u % 2, h * 2 * P:(h + 1) * 2 * P].rearrange("p (e n) -> p e n", e=2)

        def seg_dst(u, h, g):
            return XTS[h * HD:(h + 1) * HD, u, g, :].rearrange("p (n e) -> p e n", e=2)

        def matmul(o, lhsT, rhs, start, stop, **kw):
            return nc.tensor.matmul(o, lhsT, rhs, start=start, stop=stop, **kw)

        block = ctx.enter_context(nc.Block())

        @block.sync
        def _(sp):
            sp.dma_start(X, a["x_t"]).then_inc(sem("x_in"), 16)

            def stretch(src, base, count, views):
                full = count // RING
                with sp.Fori(0, full) as i:
                    for k in range(RING):
                        sp.wait_ge(sem("weights_used"), i * (2 * RING) + 2 * (base + k - RING + 1))
                        s = (base + k) % RING
                        sp.dma_start(views[s], src[bass.ds(i * RING + k, 1)].rearrange("o p x -> p (o x)")
                                     ).then_inc(sem(f"ring_full{s}"), 16)
                for n in range(base + full * RING, base + count):
                    sp.wait_ge(sem("weights_used"), 2 * (n - RING + 1))
                    sp.dma_start(views[n % RING], src[n - base]).then_inc(sem(f"ring_full{n % RING}"), 16)

            for n in range(RING):
                sp.dma_start(ring[n], a["w_ada"][n]).then_inc(sem(f"ring_full{n}"), 16)
            for n in range(RING, N_ADA1):
                sp.wait_ge(sem("weights_used"), 2 * (n - RING + 1))
                sp.dma_start(ring[n % RING], a["w_ada"][n]).then_inc(sem(f"ring_full{n % RING}"), 16)
            stretch(a["w_in"], S_IN, N_IN - 1, ring)
            n = S_IN + N_IN - 1
            sp.wait_ge(sem("weights_used"), 2 * (n - RING + 1))
            sp.dma_start(ring[n % RING][:, 0:KD * MISC], a["w_misc"]).then_inc(sem(f"ring_full{n % RING}"), 16)
            stretch(a["w_ada"][N_ADA1:], S_ADA2, N_ADA2, ring)

            sp.wait_ge(sem("weights_used"), 2 * S_O)
            sp.dma_start(S0, a["state"]).then_inc(sem("s0_in"), 16)
            sp.wait_ge(sem("rows_ready"), 3 * (TT + 1))
            for o, c in ((cmp_p, 512), (slc_p, 768), (win_p, 1024)):
                sp.dma_start(o.rearrange("(t p) c -> p t c", p=P), VT[:, 0:TT, c:c + KVW]).then_inc(sem("kv_out"), 16)
            for o, c in ((cmp_s, 512), (slc_s, 768)):
                sp.dma_start(o, VT[0:LS, TT, c:c + KVW]).then_inc(sem("kv_out"), 16)
            for b in range(DB):
                sp.dma_start(win_s[b, WIN - DS:WIN, :],
                             VT[b * DS:(b + 1) * DS, TT, 1024:1280]).then_inc(sem("kv_out"), 16)
            sp.dma_start(win_s[:, 0:WIN - DS, :], a["win"][:, DS:WIN, :]).then_inc(sem("winc_out"), 16)
            sp.wait_ge(sem("gates_ready"), 1)
            sp.dma_start(gate_scr.rearrange("t r g j -> t (r g j)"), GT[0:LS, TT, RANK:MISC]).then_inc(sem("gate_out"), 16)
            sp.wait_ge(sem("gate_out"), 16)
            for g in range(G):
                for r in range(R):
                    sp.dma_start(grow[(g * R + r) * DS:(g * R + r + 1) * DS, :, :],
                                 gate_scr[:, r, g, :].rearrange("(b q) j -> q b j", q=DS)).then_inc(sem("grow_in"), 16)
            sp.wait_ge(sem("gla_scan"), 2 * NCH)
            for h in range(2):
                sp.dma_start(gla_p[2 * h:2 * h + 2].rearrange("h k v -> (h k) v"),
                             SST[h][:, NCH, :]).then_inc(sem("gla_out"), 16)
            for h in range(2):
                sp.wait_ge(sem("gla_snew"), h + 1)
                sp.dma_start(gla_s[:, 2 * h:2 * h + 2].rearrange("b h k v -> (h k) b v"),
                             S0[:, h]).then_inc(sem("gla_out"), 16)
            sp.wait_ge(sem("kv_out"), 16 * (5 + DB))
            sp.wait_ge(sem("gla_done"), GH)
            sp.wait_ge(sem("gla_out"), 64)
            for c in range(2):
                for g in range(G):
                    o = (c * G + g) * HD
                    sp.dma_start(CP[:, o * SEG:(o + HD) * SEG].rearrange("p (s d) -> p s d", s=SEG),
                                 cmp_p.rearrange("(n s) x -> n s x", s=SEG)[:, :, o:o + HD]).then_inc(sem("segp_in"), 16)

            def batch(b, waited):
                if waited:
                    sp.wait_ge(sem("pv_done"), b)
                else:
                    sp.wait_ge(sem("zs"), 6)
                sp.dma_start(WBF, a["win"][bass.ds(b, 1)].rearrange("o (p t) c -> p (o t c)", p=P)).then_inc(sem("win_in"), 16)
                sp.dma_start(VX[:, 0, :], win_s[bass.ds(b, 1), WIN - DS:WIN, P:KVW].rearrange("o q c -> (o q) c")).then_inc(sem("win_in"), 16)
                sp.dma_start(VX[:, 1, :], slc_s.rearrange("(b q) c -> b q c", q=DS)[bass.ds(b, 1), :, P:KVW].rearrange("o q c -> (o q) c")).then_inc(sem("win_in"), 16)

            batch(0, False)
            with sp.Fori(1, DB) as b:
                batch(b, True)
            sp.wait_ge(sem("cmp_mm"), 16 * DB)
            stretch(a["w_o"], S_O, N_O, ring)
            stretch(a["w_f1"], S_F1, N_F1, ring)
            stretch(a["w_f2"], S_F2, N_F2, [r[:, 0:KF // 2 * P] for r in ring])
            sp.wait_ge(sem("ln_x"), 3 * KD)
            sp.dma_start(y_t, X).then_inc(sem("y_out"), 16)
            sp.wait_ge(sem("y_out"), 16)
            sp.wait_ge(sem("winc_out"), 16)

        @block.gpsimd
        def _(pool):
            small = ((lnv, a["lnv"]), (cs, a["c_t"]), (bada, a["b_ada"]), (pe_t, a["pe"]), (cb1, a["b1"]), (w2, a["w2"]),
                     (wa2, a["wa2"]), (ba, a["ba"]), (gng, a["gng"]), (W1, a["w1"]))
            for dst, src in small:
                pool.dma_start(dst[:], src).then_inc(sem("consts_in"), 16)
            pool.dma_start(ptab[:, :], a["ptab"].unsqueeze(1).to_broadcast([PAGES, 4, DB])).then_inc(sem("ptab_in"), 16)

            nset = [0]

            def fill(t, v):
                nset[0] += 1
                nc.gpsimd.memset(t, v).then_inc(sem("pool_set"), 1)
                pool.wait_ge(sem("pool_set"), nset[0])
            fill(ident[:, :], 0.0)
            fill(ones[:, :], 1.0 / D)
            fill(pen[:, :], 0.0)
            fill(gmask[:, :], 1.0)
            fill(smask[:, :], 1.0)
            fill(bmask[:, :], 1.0)
            fill(rsum[:, :], 0.0)
            fill(wpen[:, :], 0.0)
            fill(bpen[:, :], 0.0)
            fill(impA[:, :], 0.0)
            fill(qbd[:, :, :, :], 0.0)

            nsel = [0]

            def sel(t, op, base, pattern, cm, fillv):
                nsel[0] += 1
                nc.gpsimd.affine_select(out=t, in_=t, compare_op=op, fill=fillv, base=base, pattern=pattern,
                                        channel_multiplier=cm).then_inc(sem("pool_sel"), 1)
                pool.wait_ge(sem("pool_sel"), nsel[0])

            sel(ident[:, :], ALU.not_equal, 0, [[-1, P]], 1, 1.0)
            sel(pen[:, LP - P:LP], ALU.is_ge, 0, [[-1, P]], 1, NEG)
            for c in range(4):
                sel(gmask[32 * c:32 * c + 32, :], ALU.is_ge, 0, [[1, CH]], -1, 0.0)
            sel(smask[:, :], ALU.is_ge, 0, [[1, LS]], -1, 0.0)
            sel(bmask[:, :], ALU.is_ge, 0, [[-DS, DB]], 1, 0.0)
            for d in range(-(R - 1), R):
                sel(rsum[:, :], ALU.not_equal, DS * d, [[-1, ROWS]], 1, 1.0)
                sel(bmask[:, :], ALU.is_ge, DS - 1, [[DS, DB]], -1, 0.0)
            sel(bpen[:, :], ALU.not_equal, 0, [[1, NB]], 0, 1e4)
            sel(bpen[:, :], ALU.not_equal, -(NB - 1), [[1, NB]], 0, 1e4)
            sel(bpen[:, :], ALU.not_equal, -(NB - 2), [[1, NB]], 0, 1e4)
            nc.gpsimd.iota(pidx[:, :], pattern=[[0, 1]], base=0, channel_multiplier=1).then_inc(sem("pidx"), 1)
            pool.wait_ge(sem("pidx"), 1)
            sel(rsum[0:ROWS, 0:ROWS // 2], ALU.is_ge, ROWS // 2 - 1, [[0, ROWS // 2]], -1, 0.0)
            sel(rsum[0:ROWS, ROWS // 2:ROWS], ALU.is_ge, -(ROWS // 2), [[0, ROWS // 2]], 1, 0.0)
            pool.wait_ge(sem("pool_sel"), nsel[0])
            nc.gpsimd.memset(top8[:, :, :], 0.0).then_inc(sem("pool_consts"), 1)
            pool.wait_ge(sem("pool_consts"), 1)
            nc.gpsimd.memset(rmask, 1.0).then_inc(sem("rmask0"), 1)
            pool.wait_ge(sem("rmask0"), 1)
            nc.gpsimd.memset(rmask[:, 0:LP].rearrange("p (c i) -> p c i", i=CH)[:, :, 0:1], 0.0).then_inc(sem("rmask"), 1)
            pool.wait_ge(sem("rmask"), 1)
            nc.gpsimd.memset(rmask[:, LP:NT].rearrange("p (c i) -> p c i", i=DS)[:, :, 0:1], 0.0).then_inc(sem("rmask"), 1)

            pool.wait_ge(sem("gla_done"), GH)
            pool.wait_ge(sem("gla_out"), 64)
            nc.gpsimd.memset(pcp, 0.0).then_inc(sem("pcp0"), 1)
            pool.wait_ge(sem("pcp0"), 1)
            nc.gpsimd.affine_select(out=pcp, in_=pcp, compare_op=ALU.is_ge, fill=NEG, base=-(2 * SEG - 1),
                                    pattern=[[P, TT], [-SEG, NCP]], channel_multiplier=1).then_inc(sem("pcp"), 1)
            pool.wait_ge(sem("pcp"), 1)

            pool.wait_ge(sem("segp_t"), 16)
            pool.wait_ge(sem("idx"), 1)
            for b in range(DB):
                if b:
                    pool.wait_ge(sem("seg_t"), 16 * b)
                    pool.wait_ge(sem("slc_in"), 16 * b)
                nc.gpsimd.indirect_dma_start(out=RC[:, :], out_offset=None, in_=a["cmp"],
                                             in_offset=bass.IndirectOffsetOnAxis(ap=idx[:, b:b + 1], axis=0)
                                             ).then_inc(sem("cmp_in"), 16)
                pool.wait_ge(sem("cmp_in"), 16 * (b + 1))
                if b:
                    pool.wait_ge(sem("pv_done"), b)
                else:
                    pool.wait_ge(sem("zs"), 6)
                nc.gpsimd.indirect_dma_start(out=SBF, out_offset=None, in_=a["slc"],
                                             in_offset=bass.IndirectOffsetOnAxis(ap=idx[:, b:b + 1], axis=0)
                                             ).then_inc(sem("slc_in"), 16)

        @block.tensor
        def _(pe):
            def ln_mean(base):
                for k in range(KD):
                    matmul(stat[0][:, 0:LP], ones[:, :], X[:, k, 0:LP], k == 0, k == KD - 1)
                    last = matmul(stat[0][:, LP:NT], ones[:, :], X[:, k, LP:NT], k == 0, k == KD - 1)
                last.then_inc(sem("ln_mean"), 1)

            def ln_var(nth):
                for k in range(KD):
                    pe.wait_ge(sem("ln_sq"), nth * KD + k + 1)
                    matmul(stat[1][:, 0:LP], ones[:, :], SQ[:, k, 0:LP], k == 0, k == KD - 1)
                    last = matmul(stat[1][:, LP:NT], ones[:, :], SQ[:, k, LP:NT], k == 0, k == KD - 1)
                last.then_inc(sem("ln_var"), 1)

            def slot_ready(base, i, k):
                pe.wait_ge(sem(f"ring_full{(base + k) % RING}"), i * 16 + 16 * ((base + k) // RING + 1))

            def ada(base, i, nth):
                pe.wait_ge(sem("mod_free"), nth)
                for k in range(RING):
                    slot_ready(base, i, k)
                    for f in range(2):
                        for c in range(KD):
                            last = matmul(pmods[:, 2 * k + f, :], wslot[(base + k) % RING][:, c, f * P:(f + 1) * P],
                                          cs[:, c, :], c == 0, c == KD - 1)
                        last.then_inc(sem("weights_used"), 1)

            def project(w, b, src, m=P):
                for k in range(KD):
                    matmul(dense[b][0:m, 0:LP], w(k), src[:, k, 0:LP], k == 0, k == KD - 1)
                    last = matmul(dense[b][0:m, LP:NT], w(k), src[:, k, LP:NT], k == 0, k == KD - 1)
                return last

            pe.wait_ge(sem("pool_consts"), 1)
            pe.wait_ge(sem("x_in"), 16)
            ln_mean(0)
            pe.wait_ge(sem("silu_c"), 1)
            ada(0, 0, 1)
            ln_var(0)
            ada(RING, 0, 2)

            pe.wait_ge(sem("ln_u"), KD + 1)
            full = (N_IN - 1) // RING

            def in_tiles(i, slots):
                for k in slots:
                    slot_ready(S_IN, i, k)
                    for f in range(2):
                        pe.wait_ge(sem("dense_free"), i * 8 + 2 * k + f + 1)
                        project(lambda c: wslot[(S_IN + k) % RING][:, c, f * P:(f + 1) * P], f, U
                                ).then_inc(sem("weights_used"), 1)
            with pe.Fori(0, full) as i:
                in_tiles(i, range(RING))
            in_tiles(full, range(N_IN - 1 - full * RING))
            n = S_IN + N_IN - 1
            slot_ready(n, 0, 0)
            pe.wait_ge(sem("dense_free"), ZT + 1)
            wm = ring[n % RING][:, 0:KD * MISC].rearrange("p (k c) -> p k c", k=KD)
            project(lambda c: wm[:, c, :], 0, U, MISC).then_inc(sem("weights_used"), 2)

            pe.wait_ge(sem("dense_free"), ZT + 1 + 2)
            with pe.Fori(0, N_ADA2 // RING) as i:
                ada(S_ADA2, i, i + 3)
            pe.wait_ge(sem("mod_free"), 7)

            src = [ZVG + i for i in range(4)] + [ZKV + i for i in range(6)]
            for t in range(TT + 1):
                n = P if t < TT else LS
                cols = slice(t * P, t * P + n)
                if t >= 2:
                    pe.wait_ge(sem("rows_ready"), 3 * (t - 1))
                bank = 4 * (t % 2)
                for q, z in enumerate(src):
                    last = nc.tensor.transpose(PS[0:n, bank + q // 4, (q % 4) * P:(q % 4 + 1) * P], Z[:, z, cols], ident[:, :])
                    if q == 3 or q == 7:
                        last.then_inc(sem("rows_t"), 1)
                nc.tensor.transpose(PS[0:n, bank + 2, 256:256 + MISC], zM[:, cols], ident[0:MISC, 0:MISC]).then_inc(sem("rows_t"), 1)

            pe.wait_ge(sem("rows_ready"), 3 * (TT + 1))
            for c in range(2):
                for n in range(2 * JP):
                    last = matmul(PS[:, 6, c:c + 1], W1[:, c, n // JP, n % JP, :], pe_t[:, c, n // JP, n % JP:n % JP + 1],
                                  n == 0, n == 2 * JP - 1)
            last.then_inc(sem("pe_bias"), 1)

            for h in range(2):
                matmul(stat[h][:, 0:LP], wa2[:, h * P:(h + 1) * P], zM[0:RANK, 0:LP], True, True)
                matmul(stat[h][:, LP:NT], wa2[:, h * P:(h + 1) * P], zM[0:RANK, LP:NT], True, True).then_inc(sem("decay_x"), 1)
            pe.wait_ge(sem("gla_q"), 4)
            for h in range(GH):
                hp, lo = h // 2, (h % 2) * DK
                for t in range(TT):
                    for c in range(4):
                        cols = slice(t * P + c * CH, t * P + (c + 1) * CH)
                        matmul(PS[c * CH:(c + 1) * CH, h % 2, (hp * TT + t) * CH:(hp * TT + t + 1) * CH],
                               E[1][lo:lo + DK, hp, cols], E[0][lo:lo + DK, hp, cols], True, True)
                last = matmul(PS[0:LS, h % 2, 256 + hp * LS:256 + (hp + 1) * LS],
                              E[1][lo:lo + DK, hp, LP:NT], E[0][lo:lo + DK, hp, LP:NT], True, True)
            last.then_inc(sem("gla_att"), 1)
            for h in range(2):
                for t in range(TT + 1):
                    n = P if t < TT else LS
                    last = nc.tensor.transpose(PS[0:n, 4 + t // 2, ((t % 2) * 2 + h) * P:((t % 2) * 2 + h + 1) * P],
                                               E[3][:, h, t * P:t * P + n], ident[:, :])
            last.then_inc(sem("gla_ket"), 1)
            pe.wait_ge(sem("gla_ke"), 3)
            for hp in range(2):
                if hp == 1:
                    pe.wait_ge(sem("gla_attm"), 10)
                for c in range(4):
                    for t in range(TT):
                        for lo in range(2):
                            h = 2 * hp + lo
                            last = matmul(PS[lo * DK:(lo + 1) * DK, 4 - 4 * hp + c, t * P:(t + 1) * P],
                                          KE[c * CH:(c + 1) * CH, t, h * DK:(h + 1) * DK],
                                          VT[c * CH:(c + 1) * CH, t, h * DV:(h + 1) * DV], True, True)
                last.then_inc(sem("gla_u"), 1)
            pe.wait_ge(sem("gla_scan"), 2 * NCH)
            pe.wait_ge(sem("s0_in"), 16)
            for h in range(GH):
                hp, lo = h // 2, (h % 2) * DK
                matmul(PS[:, 4 + h % 2, h * LS:(h + 1) * LS], VT[0:LS, TT, h * DV:(h + 1) * DV], ATTS[:, h, :], True, False, skip_group_check=True)
                for b in range(DB):
                    c = slice(LP + b * DS, LP + (b + 1) * DS)
                    last = matmul(PS[:, 4 + h % 2, h * LS + b * DS:h * LS + (b + 1) * DS], S0[lo:lo + DK, hp, b, :],
                                  E[2][lo:lo + DK, hp, c], False, b == DB - 1, skip_group_check=True)
            last.then_inc(sem("gla_os"), 1)
            for h in range(GH):
                hp, lo = h // 2, (h % 2) * DK
                for t in range(TT):
                    matmul(PS[:, h, t * P:(t + 1) * P], VT[:, t, h * DV:(h + 1) * DV], ATT[:, h, t, :], True, False, skip_group_check=True)
                    for c in range(4):
                        cc = slice(t * P + c * CH, t * P + (c + 1) * CH)
                        last = matmul(PS[:, h, cc], SST[hp][lo:lo + DK, t * 4 + c, :], E[2][lo:lo + DK, hp, cc], False, c == 3, skip_group_check=True)
                last.then_inc(sem("gla_o"), 1)
            for h in range(GH):
                pe.wait_ge(sem("gla_vm"), h + 1)
                if h == 2:
                    pe.wait_ge(sem("gla_snew"), 1)
                for s in range(2):
                    last = matmul(PS[(h % 2) * DK:(h % 2 + 1) * DK, 6 + s, :], KE[0:LS, TT, h * DK:(h + 1) * DK],
                                  VMB[:, 4 * s:4 * s + 4, :], True, True)
                last.then_inc(sem("gla_us"), 1)
            for h in range(GH):
                pe.wait_ge(sem("gla_sq"), h + 1)
                if h == 0:
                    pe.wait_ge(sem("gla_snew"), 2)
                if h >= 2:
                    pe.wait_ge(sem("gla_ms_used"), h - 1)
                matmul(dense[h % 2][:, 0:LP], ones[:, :], SQG[:, h, 0:LP], True, True)
                matmul(dense[h % 2][:, LP:NT], ones[:, :], SQG[:, h, LP:NT], True, True).then_inc(sem("gla_ms"), 1)

            def segments(u):
                c, j = u // JP, u % JP
                for n in range(4):
                    last = nc.tensor.transpose(PS[:, u % 2, n * P:(n + 1) * P], CB[:, n % 2, 2 * j + n // 2, c, :], ident[:, :])
                last.then_inc(sem("seg_t"), 1)

            def compress(b, u, xt, n):
                c, j = u // JP, u % JP
                for m in range(2):
                    last = matmul(PS[:, 2 + c, 0:2 * n].rearrange("p (g n) -> p g n", g=2), W1[:, c, m, j, :],
                                  xt[:, u, :, m:m + n], j == 0 and m == 0, j == JP - 1 and m == 1)
                last.then_inc(sem("cmp_mm"), 1)

            pe.wait_ge(sem("segp_in"), 64)
            pe.wait_ge(sem("gla_done"), GH)
            for u in range(18):
                if u < 16:
                    if u >= 2:
                        pe.wait_ge(sem("segp_ev"), u - 1)
                    c, j = u // JP, u % JP
                    for g in range(G):
                        last = nc.tensor.transpose(PS[:, u % 2, g * NSEGP:(g + 1) * NSEGP], CPV[:, c, g, j, :],
                                                   ident[0:NSEGP, 0:NSEGP])
                    last.then_inc(sem("segp_t"), 1)
                if u >= 2:
                    v = u - 2
                    c, j = v // JP, v % JP
                    pe.wait_ge(sem("segp_ev"), v + 1)
                    for m in range(2):
                        last = matmul(PS[:, 2 + c, 0:2 * NCP].rearrange("p (g n) -> p g n", g=2), W1[:, c, m, j, :],
                                      XTP[:, v, :, m:m + NCP], j == 0 and m == 0, j == JP - 1 and m == 1)
                    last.then_inc(sem("cmpp_mm"), 1)
            pe.wait_ge(sem("cmpp_g"), 2)
            for g in range(G):
                last = matmul(PS[g * HD:(g + 1) * HD, 4, 0:NCP], w2[:, 0, :], HG[:, 0, g, :], True, True)
            last.then_inc(sem("cmpp_kv"), 1)
            for g in range(G):
                last = matmul(PS[0:NCP, 5, g * HD:(g + 1) * HD], HG[:, 1, g, :], w2[:, 1, :], True, True)
            last.then_inc(sem("cmpp_kv"), 1)

            pe.wait_ge(sem("cmpp_ev"), 2)
            for g in range(G):
                for r in range(R):
                    for j in range(TT):
                        n = (r * TT + j) * NCP
                        last = matmul(PS[:, g, n:n + NCP], Z[g * HD:(g + 1) * HD, ZQN + r, j * P:(j + 1) * P],
                                      kcTp[g * HD:(g + 1) * HD, :], True, True)
            last.then_inc(sem("nsa_cs"), 1)
            pe.wait_ge(sem("nsa_cp"), 1)
            for h in range(G * R):
                for j in range(TT):
                    n = (h * TT + j) * NCP
                    last = nc.tensor.transpose(PS[0:NCP, h, j * P:(j + 1) * P], pc[:, n:n + NCP], ident[:, :])
                last.then_inc(sem("nsa_ct"), 1)

            def scores(i, t):
                j, g = t // 2 % TT, t % 2
                lo, w = g * HD, (j + 1) * P
                q = qcur[lo:lo + HD, t // 8, j * P:(j + 1) * P]
                if t >= 2:
                    pe.wait_ge(sem("nsa_exp"), i * 32 + 2 * (t - 1))
                matmul(PS[:, 2 * g, 0:w], q, Z[lo:lo + HD, ZKV + 2, 0:w], True, True)
                matmul(PS[:, 2 * g + 1, 0:w], q, Z[lo:lo + HD, ZKV + 4, 0:w], True, True).then_inc(sem("nsa_sc"), 1)

            def turned(i, t):
                j, pb = t // 2 % TT, PB[t % 3]
                for q in range(2):
                    pe.wait_ge(sem("nsa_p"), i * 32 + 2 * t + q + 1)
                    for k in range(j + 1):
                        last = nc.tensor.transpose(PS[:, 6 + q, k * P:(k + 1) * P],
                                                   pb[:, q * LP + k * P:q * LP + (k + 1) * P], ident[:, :])
                    last.then_inc(sem("nsa_pt"), 1)

            def values(i, t):
                j, g, pt = t // 2 % TT, t % 2, PTB[t % 2]
                pe.wait_ge(sem("nsa_ptev"), i * 32 + 2 * (t + 1))
                if t >= 2:
                    pe.wait_ge(sem("nsa_out"), i * 16 + t)
                o = PS[g * HD:(g + 1) * HD, 4 + g, 0:P]
                for q, c in ((0, 768 + P), (1, 1024 + P)):
                    for k in range(j + 1):
                        last = matmul(o, VT[:, k, c + g * HD:c + (g + 1) * HD], pt[:, (4 * q + k) * P:(4 * q + k + 1) * P],
                                      q == 0 and k == 0, q == 1 and k == j)
                last.then_inc(sem("nsa_pv"), 1)

            pe.wait_ge(sem("nsa_cte"), G * R)
            for r in range(R):
                for g in range(G):
                    last = matmul(PS[g * HD:(g + 1) * HD, r, :], vcp[:, g * HD:(g + 1) * HD], PCT[:, g * R + r, :], True, True)
                last.then_inc(sem("nsa_cv"), 1)
            pe.wait_ge(sem("nsa_co"), R)
            with pe.Fori(0, R // 2) as i:
                pe.wait_ge(sem("nsa_out"), i * 16 + 1)
                pe.wait_ge(sem("nsa_q"), i * 2 + 2)
                scores(i, 0)
                scores(i, 1)
                for t in range(16):
                    if t + 2 < 16:
                        scores(i, t + 2)
                    if t >= 1:
                        values(i, t - 1)
                    turned(i, t)
                values(i, 15)

            def seg_step(b, u):
                if u >= 2:
                    pe.wait_ge(sem("seg_ev"), b * 32 + 2 * u - 2)
                    pe.wait_ge(sem("seg_dve"), b * 32 + 2 * u - 2)
                segments(u)

            def cmp_step(b, u):
                pe.wait_ge(sem("seg_ev"), b * 32 + 2 * u + 2)
                pe.wait_ge(sem("seg_dve"), b * 32 + 2 * u + 2)
                compress(b, u, XTS, NCS)

            def tail(b):
                cols = [(C_WIN + t * P, P) for t in range(4)] + [(C_SLC + t * P, P) for t in range(SPAN)] + \
                       [(C_CMP, P), (C_CMP + P, NCS - P), (C_XW, DS), (C_XS, DS)]
                for n, (c, w) in enumerate(cols):
                    last = nc.tensor.transpose(PS[0:w, 4 + n // 16, (n % 16) * ROWS:(n % 16 + 1) * ROWS], PSC[:, c:c + w],
                                               ident[0:ROWS, 0:ROWS])
                    if n % 16 == 15 or n == NPT - 1:
                        last.then_inc(sem("pt_t"), 1)
                vals = [WBV[:, t, 1, :] for t in range(4)] + [SBV[:, t, 1, :] for t in range(SPAN)] + \
                       [vc[:, 0, :], vc[0:NCS - P, 1, :], VX[:, 0, :], VX[:, 1, :]]
                new_w, new_s = NPT - 2, NPT - 1
                branches = (list(range(4, 4 + SPAN)) + [new_s], [0, 1, 2, 3, new_w], [4 + SPAN, 5 + SPAN])
                for o, tiles_ in zip((1, 0, 2), branches):
                    for n in tiles_:
                        if o == 1 and n in (4, 16, 32):
                            pe.wait_ge(sem("pt_ev"), b * 3 + 1 + n // 16)
                        last = matmul(PS[0:ROWS, 7, o * P:(o + 1) * P], PTS[0:cols[n][1], n, :], vals[n],
                                      n == tiles_[0], n == tiles_[-1])
                last.then_inc(sem("pv_done"), 1)

            def turn(b):
                nc.tensor.transpose(PS[:, 7, 3 * P:3 * P + ROWS], osb, ident[0:ROWS, 0:ROWS]).then_inc(sem("o_t"), 1)

            def batch(b, waited):
                if not waited:
                    pe.wait_ge(sem("zs"), 6)
                pe.wait_ge(sem("cmp_in"), b * 16 + 16)
                seg_step(b, 0)
                seg_step(b, 1)
                if waited:
                    pe.wait_ge(sem("sc_ev"), b * 11)
                for u in range(16):
                    if u == 6 and waited:
                        pe.wait_ge(sem("sc_exp"), b * 6)
                    if u == 8 and waited:
                        pe.wait_ge(sem("o_rows"), b)
                    cmp_step(b, u)
                    if u + 2 < 16:
                        seg_step(b, u + 2)
                    if u == 6 and waited:
                        tail(b - 1)
                    if u == 8 and waited:
                        turn(b - 1)
                    if u == 11:
                        pe.wait_ge(sem("cmp_g"), b * 2 + 1)
                        for g in range(G):
                            last = matmul(PS[g * HD:(g + 1) * HD, 4, 0:NCS], w2[:, 0, :], hgx[:, g * NCS:(g + 1) * NCS], True, True)
                        last.then_inc(sem("cmp_k"), 1)
                    if u == 13:
                        pe.wait_ge(sem("cmp_kev"), b + 1)
                        pe.wait_ge(sem("batch_q"), b * 3 + 3)
                        matmul(PS[0:ROWS, 6, 0:NCS], qbd[:, :, :, :].rearrange("p g r q -> p (g r q)"), kcT[:, 0:NCS], True, True
                               ).then_inc(sem("sc_done"), 1)
                pe.wait_ge(sem("win_in"), b * 48 + 48)
                for n in range(9):
                    if n == 1:
                        pe.wait_ge(sem("slc_in"), b * 16 + 16)
                        pe.wait_ge(sem("pc_ready"), b + 1)
                    if n >= 2:
                        pe.wait_ge(sem("kt_ev"), b * 9 + n - 1)
                    for t in range(4):
                        src = SBV[:, 4 * n - 4 + t, 0, :] if n else WBV[:, t, 0, :]
                        last = nc.tensor.transpose(PS[:, n % 2, t * P:(t + 1) * P], src, ident[:, :])
                    last.then_inc(sem("kt_t"), 1)
                    if n == 1:
                        matmul(PS[0:ROWS, 5, 0:NCS], rsum[:, :], PSC[:, C_CMP:C_CMP + NCS], True, True).then_inc(sem("imp"), 1)
                q = qbd[:, :, :, :].rearrange("p g r q -> p (g r q)")
                pe.wait_ge(sem("kt_ev"), b * 9 + 9)
                pe.wait_ge(sem("cmp_hx"), b * 2 + 2)
                for n in range(10):
                    if n >= 2:
                        pe.wait_ge(sem("sc_ev"), b * 11 + n)
                    if n == 0:
                        last = matmul(PS[0:ROWS, 2, 0:WIN], q, KTW, True, True)
                    elif n == 1:
                        last = matmul(PS[0:ROWS, 3, 0:2 * DS], q, knew[:, :, :].rearrange("p a q -> p (a q)"), True, True)
                    else:
                        last = matmul(PS[0:ROWS, 2 + n % 2, 0:512], q, KT[:, (n - 2) * 512:(n - 1) * 512], True, True)
                    last.then_inc(sem("sc_done"), 1)
                pe.wait_ge(sem("cmp_g"), b * 2 + 2)
                for g in range(G):
                    for s in range(2):
                        n = P if s == 0 else NCS - P
                        last = matmul(PS[0:n, 4, s * P + g * HD:s * P + (g + 1) * HD],
                                      hgx[:, g * NCS + s * P:g * NCS + s * P + n], w2[:, 1, :], True, True)
                last.then_inc(sem("cmp_v"), 1)

            batch(0, False)
            with pe.Fori(1, DB) as b:
                batch(b, True)
            pe.wait_ge(sem("sc_exp"), 6 * DB)
            tail(DB - 1)
            pe.wait_ge(sem("o_rows"), DB)
            turn(DB - 1)

            pe.wait_ge(sem("o_ev"), 2 * DB)
            for k in range(N_O):
                slot_ready(S_O, 0, k)
                for f in range(2):
                    pe.wait_ge(sem("res_free"), 2 * k + f + 1)
                    project(lambda c: wslot[(S_O + k) % RING][:, c, f * P:(f + 1) * P], f, MIXT).then_inc(sem("weights_used"), 1)
            pe.wait_ge(sem("x_res"), KD)
            ln_mean(1)
            ln_var(1)
            pe.wait_ge(sem("ln_u"), 2 * (KD + 1))

            def ffn_in(i, slots):
                for k in slots:
                    slot_ready(S_F1, i, k)
                    for f in range(2):
                        pe.wait_ge(sem("h_ready" if f else "gate_free"), i * RING + k + (2 if f else 1))
                        project(lambda c: wslot1[(S_F1 + k) % RING][:, c, f, :], f, U).then_inc(sem("weights_used"), 1)
            full = N_F1 // RING
            with pe.Fori(0, full) as i:
                ffn_in(i, range(RING))
            ffn_in(full, range(N_F1 - full * RING))
            pe.wait_ge(sem("h_ready"), N_F1 + 2)
            with pe.Fori(0, N_F2 // RING) as i:
                for k in range(RING):
                    f = k // 2
                    slot_ready(S_F2, i, k)
                    if k % 2 == 0:
                        pe.wait_ge(sem("res_free"), i * 2 + KD + f + 1)
                    w = wslot2[(S_F2 + k) % RING]
                    for c in range(KF // 2):
                        h = (k % 2) * (KF // 2) + c
                        matmul(dense[f][:, 0:LP], w[:, c, :], HT[:, h, 0:LP], h == 0, h == KF - 1)
                        last = matmul(dense[f][:, LP:NT], w[:, c, :], HT[:, h, LP:NT], h == 0, h == KF - 1)
                    last.then_inc(sem("weights_used"), 2)
            pe.wait_ge(sem("x_res"), 2 * KD)
            ln_mean(2)
            ln_var(2)

        @block.scalar
        def _(act):
            step = [0]

            def link(ins):
                step[0] += 1
                ins.then_inc(sem("act_step"), 1)
                act.wait_ge(sem("act_step"), step[0])

            def ln_act(nth, g, last=False):
                for k in range(KD):
                    act.wait_ge(sem("ln_cent"), nth * KD + k + 1)
                    nc.scalar.activation(SQ[:, k, :], XC[:, k, :], ACT.Square).then_inc(sem("ln_sq"), 1)
                act.wait_ge(sem("ln_rec"), nth + 1)
                nc.scalar.activation(rstd[:, :], rstd[:, :], ACT.Sqrt).then_inc(sem("ln_rstd"), 1)
                for k in range(KD):
                    act.wait_ge(sem("ln_h"), nth * KD + k + 1)
                    nc.scalar.activation(X[:, k, :], XC[:, k, :], ACT.Identity, bias=lnv[:, 2 * nth + 1, k:k + 1],
                                         scale=lnv[:, 2 * nth, k:k + 1]).then_inc(sem("ln_x"), 1)

            act.wait_ge(sem("consts_in"), 160)
            nc.scalar.activation(cth[:, :, :], cs[:, :, :], ACT.Tanh, scale=0.5).then_inc(sem("c_tanh"), 1)
            ln_act(0, 0)

            def copy_tiles(i, n):
                for t in range(n):
                    act.wait_ge(sem("weights_used"), i * 8 + 2 * S_IN + t + 1)
                    nc.scalar.activation(Z[:, bass.ds(i * 8 + t, 1), :].rearrange("p o t -> p (o t)"), dense[t % 2], ACT.Copy).then_inc(sem("dense_free"), 1)
            full = (N_IN - 1) // RING
            with act.Fori(0, full) as i:
                copy_tiles(i, 8)
            copy_tiles(full, ZT - 8 * full)
            act.wait_ge(sem("weights_used"), 2 * S_ADA2)
            nc.scalar.activation(zM[:, :], dense[0][0:MISC, :], ACT.Copy).then_inc(sem("dense_free"), 1)

            for t in range(TT + 1):
                n = P if t < TT else LS
                bank = 4 * (t % 2)
                for q, w in ((0, 512), (1, 512), (2, 256)):
                    act.wait_ge(sem("rows_t"), 3 * t + q + 1)
                    if q == 2:
                        nc.scalar.activation(GT[0:n, t, :], PS[0:n, bank + 2, 256:256 + MISC], ACT.Copy).then_inc(sem("gt"), 1)
                    nc.scalar.activation(VT[0:n, t, q * 512:q * 512 + w], PS[0:n, bank + q, 0:w], ACT.Copy).then_inc(sem("rows_ready"), 1)
            act.wait_ge(sem("gt"), TT + 1)
            nc.scalar.activation(GT[:, 0:TT, RANK:MISC], GT[:, 0:TT, RANK:MISC], ACT.Tanh, scale=0.5).then_inc(sem("gates_tanh"), 1)
            nc.scalar.activation(GT[0:LS, TT, RANK:MISC], GT[0:LS, TT, RANK:MISC], ACT.Tanh, scale=0.5).then_inc(sem("gates_tanh"), 1)

            for h in range(2):
                act.wait_ge(sem("decay_x"), h + 1)
                link(nc.scalar.activation(DM[:, h, :], stat[h], ACT.Abs, bias=ba[:, h:h + 1]))
            link(nc.scalar.activation(DL[:, :, :], DM[:, :, :], ACT.Exp, scale=-1.0))
            nc.scalar.activation(DM[:, :, :], DL[:, :, :], ACT.Ln, bias=1.0).then_inc(sem("decay_ln"), 1)
            act.wait_ge(sem("gla_sums"), 5)
            for n, (src, s) in enumerate(((DM, 1.0), (DM, -1.0), (BC, 1.0), (DL, 1.0))):
                nc.scalar.activation(E[n][:, :, :], src[:, :, :], ACT.Exp, scale=s / TAU).then_inc(sem("gla_exp"), 1)
            act.wait_ge(sem("gla_ket"), 1)
            for q in range(2):
                nc.scalar.activation(KE[:, 2 * q:2 * q + 2, :].rearrange("p t c -> p (t c)"), PS[:, 4 + q, :], ACT.Copy).then_inc(sem("gla_ke"), 1)
            nc.scalar.activation(KE[0:LS, TT, :], PS[0:LS, 6, 0:256], ACT.Copy).then_inc(sem("gla_ke"), 1)
            act.wait_ge(sem("gla_os"), 1)
            for h in range(GH):
                nc.scalar.activation(MIXT[:, h, LP:NT], PS[:, 4 + h % 2, h * LS:(h + 1) * LS], ACT.Copy).then_inc(sem("gla_cp"), 1)
            act.wait_ge(sem("gla_q"), 4)
            for h in range(GH):
                act.wait_ge(sem("gla_o"), h + 1)
                nc.scalar.activation(MIXT[:, h, 0:LP], PS[:, h, :], ACT.Copy).then_inc(sem("gla_cp"), 1)
            act.wait_ge(sem("gla_cp"), 2 * GH)
            act.wait_ge(sem("gla_o"), GH)
            for h in range(GH):
                nc.scalar.activation(SQG[:, h, :], MIXT[:, h, :], ACT.Square).then_inc(sem("gla_sq"), 1)
            nc.scalar.activation(TH, Z[:, ZRG:ZRG + GH, :], ACT.Tanh, scale=0.5).then_inc(sem("gla_th"), 1)
            for h in range(GH):
                act.wait_ge(sem("gla_rec"), h + 1)
                nc.scalar.activation(SQG[:, h, :], SQG[:, h, :], ACT.Sqrt).then_inc(sem("gla_rstd"), 1)

            for u in range(16):
                act.wait_ge(sem("segp_t"), u + 1)
                nc.scalar.activation(XTP[:, u, :, :].rearrange("p g n -> p (g n)"), PS[:, u % 2, 0:2 * NSEGP], ACT.Copy).then_inc(sem("segp_ev"), 1)
            act.wait_ge(sem("cbias"), 1)
            for c in range(2):
                act.wait_ge(sem("cmpp_mm"), 8 * (c + 1))
                nc.scalar.activation(HX[:, c, :, :].rearrange("p g n -> p (g n)"), PS[:, 2 + c, 0:2 * NCP], ACT.Identity,
                                     bias=cbias[:, c:c + 1]).then_inc(sem("cmpp_hx"), 1)
            act.wait_ge(sem("cmpp_poly"), 1)
            nc.scalar.activation(HG, HG, ACT.Tanh, scale=GELU_A).then_inc(sem("cmpp_tanh"), 1)

            act.wait_ge(sem("nsa_cx"), 1)
            nc.scalar.activation(pc, pc, ACT.Exp).then_inc(sem("nsa_ce"), 1)
            for h in range(0, G * R, 2):
                act.wait_ge(sem("nsa_ct"), h + 1)
                nc.scalar.activation(PCT[:, h, :], PS[0:NCP, h, :], ACT.Copy).then_inc(sem("nsa_cte"), 1)
            for r in range(R):
                act.wait_ge(sem("nsa_cv"), r + 1)
                nc.scalar.activation(MIXT[:, 4 + r, 0:LP], PS[:, r, :], ACT.Copy).then_inc(sem("nsa_co"), 1)

            def exponentials(i, t):
                j, g = t // 2 % TT, t % 2
                w = (j + 1) * P
                if t >= 3:
                    act.wait_ge(sem("nsa_pt"), i * 32 + 2 * (t - 2))
                act.wait_ge(sem("nsa_max"), i * 16 + t + 1)
                for q in range(2):
                    nc.scalar.activation(PB[t % 3][:, q * LP:q * LP + w], PS[:, 2 * g + q, 0:w], ACT.Exp, scale=HD ** -0.5,
                                         bias=pst[:, g, 1, q:q + 1], accum_out=pst[:, g, 2, q:q + 1]).then_inc(sem("nsa_exp"), 1)

            with act.Fori(0, R // 2) as i:
                act.wait_ge(sem("nsa_out"), i * 16 + 1)
                for h in range(2):
                    nc.scalar.activation(qcur[:, h, :], Z[:, bass.ds(i * 2 + ZQN + h, 1), 0:LP].rearrange("p o t -> p (o t)"),
                                         ACT.Copy).then_inc(sem("nsa_q"), 1)
                exponentials(i, 0)
                for t in range(16):
                    if t + 1 < 16:
                        exponentials(i, t + 1)
                    w = (t // 2 % TT + 1) * P
                    pt = PTB[t % 2]
                    if t >= 2:
                        act.wait_ge(sem("nsa_pv"), i * 16 + t - 1)
                    for q in range(2):
                        act.wait_ge(sem("nsa_pt"), i * 32 + 2 * t + 1 + q)
                        nc.scalar.activation(pt[:, 4 * q * P:4 * q * P + w], PS[:, 6 + q, 0:w], ACT.Copy).then_inc(sem("nsa_ptev"), 1)

            def exp_part(b, q):
                if q == 0:
                    act.wait_ge(sem("sc_max"), b * 3 + 3)
                v = PSC[:, C_XS + q * PART:C_XS + (q + 1) * PART]
                nc.scalar.activation(v, v, ACT.Exp, bias=smx[:, 1, 1:2], accum_out=pmx[:, 1, q:q + 1]).then_inc(sem("sc_exp"), 1)

            def seg_copy(b, u):
                act.wait_ge(sem("seg_t"), b * 16 + u + 1)
                for h in range(2):
                    nc.scalar.activation(seg_dst(u, h, 0), seg_src(u, h, 0), ACT.Copy).then_inc(sem("seg_ev"), 1)

            def batch(b, waited):
                seg_copy(b, 0)
                if waited:
                    act.wait_ge(sem("sc_done"), b * 11)
                for g in range(G):
                    nc.scalar.activation(qbd[g * HD:(g + 1) * HD, g, :, :], zS[g * HD:(g + 1) * HD, 0:R, bass.ds(b * DS, DS)],
                                         ACT.Copy).then_inc(sem("batch_q"), 1)
                nc.scalar.activation(knew[:, :, :], zS[:, 4:6, bass.ds(b * DS, DS)], ACT.Copy).then_inc(sem("batch_q"), 1)
                for u in range(1, 10):
                    seg_copy(b, u)
                    if waited and u in (4, 5):
                        exp_part(b - 1, 2 * (u - 4))
                        exp_part(b - 1, 2 * (u - 4) + 1)
                act.wait_ge(sem("cmp_mm"), b * 16 + 8)
                if waited:
                    act.wait_ge(sem("cmp_g"), b * 2)
                nc.scalar.activation(HXS[:, :], PS[:, 2, 0:2 * NCS], ACT.Identity, bias=cbias[:, 0:1]).then_inc(sem("cmp_hx"), 1)
                seg_copy(b, 10)
                seg_copy(b, 11)
                act.wait_ge(sem("cmp_poly"), b * 2 + 1)
                nc.scalar.activation(hgx[:, :], hgx[:, :], ACT.Tanh, scale=GELU_A).then_inc(sem("cmp_tanh"), 1)
                seg_copy(b, 12)
                seg_copy(b, 13)
                act.wait_ge(sem("cmp_k"), b + 1)
                nc.scalar.activation(kcT[:, 0:NCS], PS[:, 4, 0:NCS], ACT.Copy, scale=0.5).then_inc(sem("cmp_kev"), 1)
                seg_copy(b, 14)
                seg_copy(b, 15)
                act.wait_ge(sem("sc_max"), b * 3 + 1)
                nc.scalar.activation(PSC[:, C_CMP:C_CMP + NCS], PSC[:, C_CMP:C_CMP + NCS], ACT.Exp, bias=smx[:, 1, 2:3],
                                     accum_out=smx[:, 2, 2:3]).then_inc(sem("sc_exp"), 1)
                act.wait_ge(sem("cmp_mm"), b * 16 + 16)
                nc.scalar.activation(HXS[:, :], PS[:, 3, 0:2 * NCS], ACT.Identity, bias=cbias[:, 1:2]).then_inc(sem("cmp_hx"), 1)
                for n in range(9):
                    act.wait_ge(sem("kt_t"), b * 9 + n + 1)
                    dst = KT[:, (n - 1) * 512:n * 512] if n else KTW
                    nc.scalar.activation(dst, PS[:, n % 2, :], ACT.Copy).then_inc(sem("kt_ev"), 1)
                act.wait_ge(sem("cmp_poly"), b * 2 + 2)
                nc.scalar.activation(hgx[:, :], hgx[:, :], ACT.Tanh, scale=GELU_A).then_inc(sem("cmp_tanh"), 1)
                act.wait_ge(sem("sc_max"), b * 3 + 2)
                v = PSC[:, C_WIN:C_WIN + WIN + DS]
                nc.scalar.activation(v, v, ACT.Exp, bias=smx[:, 1, 0:1], accum_out=smx[:, 2, 0:1]).then_inc(sem("sc_exp"), 1)

            act.wait_ge(sem("zs"), 6)
            batch(0, False)
            with act.Fori(1, DB) as b:
                batch(b, True)
            for q in range(4):
                exp_part(DB - 1, q)

            for k in range(KD):
                nc.scalar.activation(X[:, k, :], X[:, k, :], ACT.Copy, scale=ALPHA).then_inc(sem("x_alpha"), 1)
            ln_act(1, 2)
            act.wait_ge(sem("ln_u"), 2 * (KD + 1))
            for k in range(KD):
                nc.scalar.activation(X[:, k, :], X[:, k, :], ACT.Copy, scale=ALPHA).then_inc(sem("x_alpha"), 1)

            def gate(i, n):
                for k in range(n):
                    act.wait_ge(sem("weights_used"), i * 8 + 2 * S_F1 + 2 * k + 1)
                    act.wait_ge(sem("h_ready"), i * RING + k + 1)
                    nc.scalar.activation(SQ[:, k % 2, :], dense[0], ACT.Tanh, scale=0.5).then_inc(sem("gate_th"), 1)
            full = N_F1 // RING
            with act.Fori(0, full) as i:
                gate(i, RING)
            gate(full, N_F1 - full * RING)
            ln_act(2, 4)

        @block.vector
        def _(dve):
            step = [0]

            def link(ins):
                step[0] += 1
                ins.then_inc(sem("dve_step"), 1)
                dve.wait_ge(sem("dve_step"), step[0])

            def ln_dve(nth, chunk):
                dve.wait_ge(sem("ln_mean"), nth + 1)
                for k in range(KD):
                    nc.vector.tensor_tensor(XC[:, k, :], X[:, k, :], stat[0], ALU.subtract).then_inc(sem("ln_cent"), 1)
                dve.wait_ge(sem("ln_var"), nth + 1)
                link(nc.vector.tensor_scalar(rstd[:, :], stat[1], 1e-5, None, ALU.add))
                nc.vector.reciprocal(rstd[:, :], rstd[:, :]).then_inc(sem("ln_rec"), 1)
                dve.wait_ge(sem("ln_rstd"), nth + 1)
                for k in range(KD):
                    nc.vector.tensor_tensor(XC[:, k, :], XC[:, k, :], rstd[:, :], ALU.mult).then_inc(sem("ln_h"), 1)
                if chunk is None:
                    return
                for k in range(KD):
                    dve.wait_ge(sem("ln_x"), nth * KD + k + 1)
                    nc.vector.tensor_scalar(U[:, k, 0:LP], X[:, k, 0:LP], mod[:, chunk + 1, k, 0:1], mod[:, chunk, k, 0:1],
                                            ALU.mult, ALU.add).then_inc(sem("ln_u"), 1)
                us = U[:, :, LP:NT].rearrange("p k (b q) -> p k b q", q=DS)
                xs = X[:, :, LP:NT].rearrange("p k (b q) -> p k b q", q=DS)
                shp = [P, KD, DB, DS]
                link(nc.vector.tensor_tensor(us, xs, mod[:, chunk + 1, :, 1:NC].unsqueeze(3).to_broadcast(shp), ALU.mult))
                nc.vector.tensor_tensor(us, us, mod[:, chunk, :, 1:NC].unsqueeze(3).to_broadcast(shp), ALU.add).then_inc(sem("ln_u"), 1)

            def mod_copy(i, base, c):
                dve.wait_ge(sem("weights_used"), i * 8 + base)
                nc.vector.tensor_tensor(mod[:, bass.ds(c, 1), :, :].rearrange("p o k c -> p (o k) c"), pmods,
                                        bada[:, bass.ds(c, 1), :].rearrange("p o k -> p (o k)").unsqueeze(2).to_broadcast([P, KD, NC]),
                                        ALU.add).then_inc(sem("mod_free"), 1)

            dve.sem_inc(sem("mod_free"), 1)
            dve.sem_inc(sem("dense_free"), 2)
            dve.wait_ge(sem("c_tanh"), 1)
            link(nc.vector.scalar_tensor_tensor(out=cth[:, :, :], in0=cth[:, :, :], scalar=1.0, in1=cs[:, :, :], op0=ALU.add, op1=ALU.mult))
            nc.vector.tensor_scalar(cs[:, :, :], cth[:, :, :], 0.5, None, ALU.mult).then_inc(sem("silu_c"), 1)
            dve.wait_ge(sem("pidx"), 1)
            dve.wait_ge(sem("ptab_in"), 16)
            link(nc.vector.tensor_single_scalar(pmod[:, :], pidx[:, :], 3, op=ALU.bitwise_and))
            link(nc.vector.tensor_copy(pmodf[:, :], pmod[:, :]))
            nc.vector.tensor_scalar(idx[:, :], ptab[:, :], 4.0, None, ALU.mult).then_inc(sem("idx4"), 1)
            dve.wait_ge(sem("idx4"), 1)
            nc.vector.tensor_scalar(idx[:, :], idx[:, :], pmodf[:, 0:1], None, ALU.add).then_inc(sem("idx"), 1)
            dve.wait_ge(sem("pool_consts"), 1)
            for q in range(DS):
                link(nc.vector.tensor_scalar(smx[:, 0, 0:1], pmodf[0:ROWS, 0:1], float(q), NEG, ALU.is_ge, ALU.mult))
                link(nc.vector.tensor_copy(wpen[:, q * P:q * P + 1], smx[:, 0, 0:1]))
                link(nc.vector.tensor_scalar(smx[:, 0, 1:2], pmodf[0:ROWS, 0:1], float(q), NEG, ALU.is_lt, ALU.mult))
                link(nc.vector.tensor_copy(wpen[:, WIN + q:WIN + q + 1], smx[:, 0, 1:2]))
                link(nc.vector.tensor_copy(wpen[:, WIN + DS + q:WIN + DS + q + 1], smx[:, 0, 1:2]))
            link(nc.vector.tensor_copy(VMB[:, :, 0:DS], bmask[:, :].unsqueeze(2).to_broadcast([LS, DB, DS])))
            link(nc.vector.tensor_tensor(smask[:, :].rearrange("p (b q) -> p b q", q=DS), smask[:, :].rearrange("p (b q) -> p b q", q=DS),
                                         VMB[:, :, 0:DS], ALU.mult))

            dve.wait_ge(sem("ln_mean"), 1)
            for k in range(KD):
                nc.vector.tensor_tensor(XC[:, k, :], X[:, k, :], stat[0], ALU.subtract).then_inc(sem("ln_cent"), 1)
            mod_copy(0, 8, 0)
            dve.wait_ge(sem("ln_var"), 1)
            link(nc.vector.tensor_scalar(rstd[:, :], stat[1], 1e-5, None, ALU.add))
            nc.vector.reciprocal(rstd[:, :], rstd[:, :]).then_inc(sem("ln_rec"), 1)
            dve.wait_ge(sem("ln_rstd"), 1)
            for k in range(KD):
                nc.vector.tensor_tensor(XC[:, k, :], XC[:, k, :], rstd[:, :], ALU.mult).then_inc(sem("ln_h"), 1)
            mod_copy(0, 16, 1)
            dve.wait_ge(sem("mod_free"), 3)
            link(nc.vector.tensor_scalar(mod[:, 1, :, :], mod[:, 1, :, :], 1.0, None, ALU.add))
            for k in range(KD):
                dve.wait_ge(sem("ln_x"), k + 1)
                nc.vector.tensor_scalar(U[:, k, 0:LP], X[:, k, 0:LP], mod[:, 1, k, 0:1], mod[:, 0, k, 0:1],
                                        ALU.mult, ALU.add).then_inc(sem("ln_u"), 1)
            us = U[:, :, LP:NT].rearrange("p k (b q) -> p k b q", q=DS)
            xs = X[:, :, LP:NT].rearrange("p k (b q) -> p k b q", q=DS)
            shp = [P, KD, DB, DS]
            link(nc.vector.tensor_tensor(us, xs, mod[:, 1, :, 1:NC].unsqueeze(3).to_broadcast(shp), ALU.mult))
            nc.vector.tensor_tensor(us, us, mod[:, 0, :, 1:NC].unsqueeze(3).to_broadcast(shp), ALU.add).then_inc(sem("ln_u"), 1)

            with dve.Fori(0, N_ADA2 // RING) as i:
                mod_copy(i, 2 * S_ADA2 + 8, i + 2)
            dve.wait_ge(sem("mod_free"), 7)
            link(nc.vector.tensor_scalar(mod[:, 4, :, :], mod[:, 4, :, :], 1.0, None, ALU.add))

            dve.wait_ge(sem("gates_tanh"), 2)
            link(nc.vector.tensor_scalar(GT[:, 0:TT, RANK:MISC], GT[:, 0:TT, RANK:MISC], 0.5, 0.5, ALU.mult, ALU.add))
            nc.vector.tensor_scalar(GT[0:LS, TT, RANK:MISC], GT[0:LS, TT, RANK:MISC], 0.5, 0.5, ALU.mult, ALU.add).then_inc(sem("gates_ready"), 1)
            dve.wait_ge(sem("pe_bias"), 1)
            nc.vector.tensor_tensor(cbias[:, :], PS[:, 6, 0:2], cb1[:, :], ALU.add).then_inc(sem("cbias"), 1)

            dve.wait_ge(sem("decay_ln"), 1)
            for h in range(2):
                link(nc.vector.tensor_scalar(LA[:, h, :], stat[h], ba[:, h:h + 1], 0.0, ALU.add, ALU.min))
            link(nc.vector.tensor_tensor(LA[:, :, :], LA[:, :, :], DM[:, :, :], ALU.subtract))
            dve.wait_ge(sem("rmask"), 2)
            for h in range(2):
                link(nc.vector.tensor_tensor_scan(BC[:, h, :], rmask, LA[:, h, :], 0.0, ALU.mult, ALU.add))
            nc.vector.memset(S0P[:, 0, :], 0.0).then_inc(sem("gla_sums"), 1)
            nc.vector.memset(S1[:, 0, :], 0.0)
            for lo, hi, n, w in ((0, LP, NCH, CH), (LP, NT, DB, DS)):
                b4 = BC[:, :, lo:hi].rearrange("p h (c i) -> p h c i", i=w)
                shp4 = [P, 2, n, w]
                nc.vector.tensor_tensor(DM[:, :, lo:hi].rearrange("p h (c i) -> p h c i", i=w), b4,
                                        b4[:, :, :, w // 2 - 1:w // 2].to_broadcast(shp4), ALU.subtract).then_inc(sem("gla_sums"), 1)
                nc.vector.tensor_tensor(DL[:, :, lo:hi].rearrange("p h (c i) -> p h c i", i=w),
                                        b4[:, :, :, w - 1:w].to_broadcast(shp4), b4, ALU.subtract).then_inc(sem("gla_sums"), 1)
            dve.wait_ge(sem("gla_exp"), 4)
            dec = gdec[:, :, 0:NCH]
            decs = gdec[:, :, NCH:NCH + DB]
            nc.vector.tensor_copy(dec, E[2][:, :, CH - 1:LP:CH]).then_inc(sem("gla_dec"), 1)
            nc.vector.tensor_copy(decs, E[2][:, :, LP + DS - 1:NT:DS]).then_inc(sem("gla_dec"), 1)
            dve.wait_ge(sem("gla_dec"), 2)
            for n, z in ((0, ZQG), (1, ZKG), (2, ZQG), (3, ZKG)):
                nc.vector.scalar_tensor_tensor(out=E[n][:, :, :], in0=E[n][:, :, :], scalar=DK ** -0.5 if z == ZQG else 1.0,
                                               in1=Z[:, z:z + 2, :], op0=ALU.mult, op1=ALU.mult).then_inc(sem("gla_q"), 1)
            nc.vector.memset(ATT, 0.0).then_inc(sem("att_zero"), 1)
            dve.wait_ge(sem("gla_att"), 1)
            dve.wait_ge(sem("att_zero"), 1)
            for h2 in range(2):
                for c in range(4):
                    rows = slice(c * CH, (c + 1) * CH)
                    nc.vector.tensor_tensor(
                        RR[rows, 2 * GW:2 * GW + 16 * P].rearrange("p (a b t i) -> p a b t i", a=2, b=2, t=TT)[:, :, h2, :, rows],
                        PS[rows, h2, 0:256].rearrange("p (a t i) -> p a t i", a=2, t=TT),
                        gmask[rows, :].unsqueeze(1).unsqueeze(1).to_broadcast([CH, 2, TT, CH]), ALU.mult).then_inc(sem("gla_attm"), 1)
                nc.vector.tensor_tensor(ATTS.rearrange("p (a b) i -> p a b i", b=2)[:, :, h2, :],
                                        PS[0:LS, h2, 256:256 + 2 * LS].rearrange("p (a i) -> p a i", a=2),
                                        smask[:, :].unsqueeze(1).to_broadcast([LS, 2, LS]), ALU.mult).then_inc(sem("gla_attm"), 1)
            for h in range(2):
                dve.wait_ge(sem("gla_u"), h + 1)
                for c in range(NCH):
                    nc.vector.scalar_tensor_tensor(out=SST[h][:, c + 1, :], in0=SST[h][:, c, :], scalar=dec[:, h, c:c + 1],
                                                   in1=PS[:, 4 - 4 * h + c % 4, (c // 4) * P:(c // 4 + 1) * P],
                                                   op0=ALU.mult, op1=ALU.add).then_inc(sem("gla_scan"), 1)
                    dve.wait_ge(sem("gla_scan"), h * NCH + c + 1)
            for h in range(GH):
                if h >= 1:
                    dve.wait_ge(sem("gla_us"), h)
                nc.vector.tensor_tensor(VMB, VT[0:LS, TT, h * DV:(h + 1) * DV].unsqueeze(1).to_broadcast([LS, DB, DV]),
                                        bmask[:, :].unsqueeze(2).to_broadcast([LS, DB, DV]), ALU.mult).then_inc(sem("gla_vm"), 1)
                if h % 2 == 1:
                    dve.wait_ge(sem("gla_us"), h + 1)
                    dve.wait_ge(sem("gla_os"), 1)
                    hp = h // 2
                    for b in range(DB):
                        last = nc.vector.scalar_tensor_tensor(out=S0[:, hp, b, :], in0=S0[:, hp, b, :], scalar=decs[:, hp, b:b + 1],
                                                              in1=PS[:, 6 + b // 4, (b % 4) * P:(b % 4 + 1) * P], op0=ALU.mult, op1=ALU.add)
                    last.then_inc(sem("gla_snew"), 1)
            dve.wait_ge(sem("gla_th"), 1)
            link(nc.vector.scalar_tensor_tensor(out=TH, in0=TH, scalar=1.0, in1=Z[:, ZRG:ZRG + GH, :], op0=ALU.add, op1=ALU.mult))
            for h in range(GH):
                dve.wait_ge(sem("gla_ms"), h + 1)
                nc.vector.tensor_scalar(SQG[:, h, :], dense[h % 2], float(D // DV), 1e-6, ALU.mult, ALU.add).then_inc(sem("gla_ms_used"), 1)
                dve.wait_ge(sem("gla_ms_used"), h + 1)
                nc.vector.reciprocal(SQG[:, h, :], SQG[:, h, :]).then_inc(sem("gla_rec"), 1)
            for h in range(GH):
                dve.wait_ge(sem("gla_rstd"), h + 1)
                link(nc.vector.scalar_tensor_tensor(out=MIXT[:, h, :], in0=MIXT[:, h, :], scalar=gng[:, 0:1], in1=SQG[:, h, :], op0=ALU.mult, op1=ALU.mult))
                nc.vector.scalar_tensor_tensor(out=MIXT[:, h, :], in0=MIXT[:, h, :], scalar=0.5, in1=TH[:, h, :], op0=ALU.mult, op1=ALU.mult).then_inc(sem("gla_done"), 1)

            dve.wait_ge(sem("cmpp_hx"), 2)
            link(nc.vector.tensor_tensor(HG, HX, HX, ALU.mult))
            link(nc.vector.tensor_scalar(HG, HG, GELU_C, 1.0, ALU.mult, ALU.add))
            nc.vector.tensor_tensor(HG, HG, HX, ALU.mult).then_inc(sem("cmpp_poly"), 1)
            dve.wait_ge(sem("cmpp_tanh"), 1)
            nc.vector.scalar_tensor_tensor(out=HG.rearrange("p c g n -> p (c g n)"), in0=HG.rearrange("p c g n -> p (c g n)"), scalar=1.0,
                                           in1=HX.rearrange("p c g n -> p (c g n)"), op0=ALU.add, op1=ALU.mult).then_inc(sem("cmpp_g"), 2)
            dve.wait_ge(sem("cmpp_kv"), 2)
            nc.vector.tensor_scalar(kcTp, PS[:, 4, 0:NCP], 0.5, None, ALU.mult).then_inc(sem("cmpp_ev"), 1)
            nc.vector.tensor_scalar(vcp, PS[0:NCP, 5, 0:P], 0.5, None, ALU.mult).then_inc(sem("cmpp_ev"), 1)

            dve.wait_ge(sem("pcp"), 1)
            dve.wait_ge(sem("nsa_cs"), 1)
            by_tile = pc.rearrange("p (c n) -> p c n", n=NCP)
            tiles_ = [P, G * R * TT, NCP]
            for g in range(G):
                link(nc.vector.scalar_tensor_tensor(
                    out=pc[:, g * PCW:(g + 1) * PCW].rearrange("p (r n) -> p r n", r=R), in0=PS[:, g, 0:PCW].rearrange("p (r n) -> p r n", r=R),
                    scalar=HD ** -0.5, in1=pcp.rearrange("p t n -> p (t n)").unsqueeze(1).to_broadcast([P, R, TT * NCP]),
                    op0=ALU.mult, op1=ALU.add))
            link(nc.vector.tensor_reduce(pcst[:, 0, :], by_tile, AX.X, ALU.max))
            link(nc.vector.tensor_scalar(pcst[:, 0, :], pcst[:, 0, :], 0.9 * NEG, None, ALU.max))
            nc.vector.tensor_tensor(by_tile, by_tile, pcst[:, 0, :].unsqueeze(2).to_broadcast(tiles_), ALU.subtract).then_inc(sem("nsa_cx"), 1)
            dve.wait_ge(sem("nsa_ce"), 1)
            link(nc.vector.tensor_reduce(pcst[:, 1, :], by_tile, AX.X, ALU.add))
            link(nc.vector.tensor_scalar(pcst[:, 1, :], pcst[:, 1, :], 1e-30, None, ALU.max))
            link(nc.vector.reciprocal(pcst[:, 1, :], pcst[:, 1, :]))
            for g in range(G):
                n = slice(g * R * TT, (g + 1) * R * TT)
                gate_c = GT[:, 0:TT, RANK:MISC].rearrange("p t (r c) -> p r t c", r=R)[:, :, :, 3 * g:3 * g + 1].rearrange("p r t o -> p r (t o)")
                link(nc.vector.tensor_tensor(pcst[:, 2, n].rearrange("p (r t) -> p r t", r=R), pcst[:, 1, n].rearrange("p (r t) -> p r t", r=R),
                                             gate_c, ALU.mult))
            nc.vector.tensor_tensor(by_tile, by_tile, pcst[:, 2, :].unsqueeze(2).to_broadcast(tiles_), ALU.mult).then_inc(sem("nsa_cp"), 1)
            for h in range(1, G * R, 2):
                dve.wait_ge(sem("nsa_ct"), h + 1)
                nc.vector.tensor_copy(PCT[:, h, :], PS[0:NCP, h, :]).then_inc(sem("nsa_cte"), 1)

            dve.wait_ge(sem("nsa_co"), R)
            dve.sem_inc(sem("nsa_out"), 1)
            base = step[0]
            PER = 2 + 16 * 5
            with dve.Fori(0, R // 2) as i:
                count = [0]

                def lk(ins):
                    count[0] += 1
                    ins.then_inc(sem("dve_step"), 1)
                    dve.wait_ge(sem("dve_step"), i * PER + base + count[0])
                for h in range(2):
                    lk(nc.vector.tensor_copy(gpc[:, h, :, :], GT[:, 0:TT, bass.ds(i * 12 + RANK + 6 * h, 6)]))

                def prepare(t):
                    j, g = t // 2 % TT, t % 2
                    w = (j + 1) * P
                    st = pst[:, g]
                    dve.wait_ge(sem("nsa_sc"), i * 16 + t + 1)
                    diag = PS[:, 2 * g:2 * g + 2, w - P:w]
                    lk(nc.vector.tensor_tensor(diag, diag, pen[:, LP - P:LP].unsqueeze(1).to_broadcast([P, 2, P]), ALU.add))
                    lk(nc.vector.tensor_reduce(st[:, 0, :], PS[:, 2 * g:2 * g + 2, 0:w], AX.X, ALU.max))
                    nc.vector.tensor_scalar(st[:, 1, :], st[:, 0, :], -HD ** -0.5, None, ALU.mult).then_inc(sem("nsa_max"), 1)

                def finish(t):
                    j, g = t // 2 % TT, t % 2
                    w = (j + 1) * P
                    st = pst[:, g]
                    dve.wait_ge(sem("nsa_exp"), i * 32 + 2 * (t + 1))
                    lk(nc.vector.tensor_scalar(st[:, 2, :], st[:, 2, :], 1e-30, None, ALU.max))
                    lk(nc.vector.reciprocal(st[:, 2, :], st[:, 2, :]))
                    lk(nc.vector.tensor_tensor(st[:, 3, :], st[:, 2, :], gpc[:, t // 8, j, g * 3 + 1:g * 3 + 3], ALU.mult))
                    for q in range(2):
                        v = PB[t % 3][:, q * LP:q * LP + w]
                        nc.vector.tensor_scalar(v, v, st[:, 3, q:q + 1], None, ALU.mult).then_inc(sem("nsa_p"), 1)

                def output(t):
                    j, g = t // 2 % TT, t % 2
                    dve.wait_ge(sem("nsa_pv"), i * 16 + t + 1)
                    o = MIXT[g * HD:(g + 1) * HD, bass.ds(i * 2 + 4 + t // 8, 1), j * P:(j + 1) * P].rearrange("p o t -> p (o t)")
                    nc.vector.tensor_tensor(o, o, PS[g * HD:(g + 1) * HD, 4 + g, 0:P], ALU.add).then_inc(sem("nsa_out"), 1)

                prepare(0)
                for t in range(16):
                    if t + 1 < 16:
                        prepare(t + 1)
                    finish(t)
                    if t >= 2:
                        output(t - 2)
                output(14)
                output(15)
                assert count[0] == PER, count[0]
            step[0] += PER * (R // 2)
            dve.wait_ge(sem("nsa_out"), 8 * R + 1)
            for r in range(R):
                nc.vector.tensor_scalar(zS[:, r, :], Z[:, ZQN + r, LP:NT], HD ** -0.5, None, ALU.mult).then_inc(sem("zs"), 1)
            nc.vector.tensor_copy(zS[:, 4, :], Z[:, ZKV + 4, LP:NT]).then_inc(sem("zs"), 1)
            nc.vector.tensor_copy(zS[:, 5, :], Z[:, ZKV + 2, LP:NT]).then_inc(sem("zs"), 1)
            dve.wait_ge(sem("zs"), 6)

            sbase = step[0]
            SPER, TPER = 17, 11

            def tlk(b, n, ins):
                ins.then_inc(sem("tail_step"), 1)
                dve.wait_ge(sem("tail_step"), b * TPER + n)

            def max_part(b, q):
                tlk(b, q + 1, nc.vector.tensor_reduce(pmx[:, 0, q:q + 1], PSC[:, C_XS + q * PART:C_XS + (q + 1) * PART], AX.X, ALU.max))
                if q == 3:
                    tlk(b, 5, nc.vector.tensor_reduce(smx[:, 0, 1:2], pmx[:, 0, :], AX.X, ALU.max))
                    nc.vector.tensor_scalar(smx[:, 1, 1:2], smx[:, 0, 1:2], -1.0, None, ALU.mult).then_inc(sem("sc_max"), 1)

            def tail(b):
                for q in range(3):
                    dve.wait_ge(sem("pt_t"), b * 3 + q + 1)
                    if q < 2:
                        last = nc.vector.tensor_copy(PTS[:, 16 * q:16 * q + 16, :], PS[:, 4 + q, :].rearrange("p (n r) -> p n r", r=ROWS))
                    else:
                        nc.vector.tensor_copy(PTS[:, 32:37, :], PS[:, 6, 0:5 * ROWS].rearrange("p (n r) -> p n r", r=ROWS))
                        nc.vector.tensor_copy(PTS[0:NCS - P, 37, :], PS[0:NCS - P, 6, 5 * ROWS:6 * ROWS])
                        last = nc.vector.tensor_copy(PTS[0:DS, 38:40, :], PS[0:DS, 6, 6 * ROWS:8 * ROWS].rearrange("p (n r) -> p n r", r=ROWS))
                    last.then_inc(sem("pt_ev"), 1)
                dve.wait_ge(sem("sc_exp"), b * 6 + 6)
                tlk(b, 6, nc.vector.tensor_copy(gcur[:, :], grow[:, bass.ds(b, 1), :].rearrange("p o j -> p (o j)")))
                tlk(b, 7, nc.vector.tensor_reduce(smx[:, 2, 1:2], pmx[:, 1, :], AX.X, ALU.add))
                tlk(b, 8, nc.vector.reciprocal(smx[:, 3, 0:2], smx[:, 2, 0:2]))
                nc.vector.tensor_tensor(smx[:, 3, 0:1], smx[:, 3, 0:1], gcur[:, 2:3], ALU.mult)
                tlk(b, 9, nc.vector.tensor_tensor(smx[:, 3, 1:2], smx[:, 3, 1:2], gcur[:, 1:2], ALU.mult))
                dve.wait_ge(sem("pv_done"), b + 1)
                tlk(b, 10, nc.vector.tensor_scalar(osb, PS[0:ROWS, 7, 0:P], smx[:, 3, 0:1], None, ALU.mult))
                tlk(b, 11, nc.vector.scalar_tensor_tensor(out=osb, in0=PS[0:ROWS, 7, P:2 * P], scalar=smx[:, 3, 1:2], in1=osb,
                                                          op0=ALU.mult, op1=ALU.add))
                nc.vector.scalar_tensor_tensor(out=osb, in0=PS[0:ROWS, 7, 2 * P:3 * P], scalar=gcur[:, 0:1], in1=osb,
                                               op0=ALU.mult, op1=ALU.add).then_inc(sem("o_rows"), 1)

            def output(b):
                dve.wait_ge(sem("o_t"), b + 1)
                for g in range(G):
                    rows = slice(g * HD, (g + 1) * HD)
                    nc.vector.tensor_copy(MIXT[rows, R:2 * R, bass.ds(b * DS + LP, DS)],
                                          PS[rows, 7, 3 * P + g * R * DS:3 * P + (g + 1) * R * DS].rearrange("p (r q) -> p r q", r=R)).then_inc(sem("o_ev"), 1)

            def batch(b, waited):
                count = [0]

                def lk(ins):
                    count[0] += 1
                    ins.then_inc(sem("dve_step"), 1)
                    dve.wait_ge(sem("dve_step"), b * SPER + sbase + count[0])

                def seg_copy(u):
                    dve.wait_ge(sem("seg_t"), b * 16 + u + 1)
                    for h in range(2):
                        nc.vector.tensor_copy(seg_dst(u, h, 1), seg_src(u, h, 1)).then_inc(sem("seg_dve"), 1)

                def gelu_poly(c):
                    dve.wait_ge(sem("cmp_hx"), b * 2 + c + 1)
                    if c == 1:
                        dve.wait_ge(sem("cmp_k"), b + 1)
                    elif waited:
                        dve.wait_ge(sem("cmp_v"), b)
                    lk(nc.vector.tensor_tensor(hgx[:, :], HXS[:, :], HXS[:, :], ALU.mult))
                    lk(nc.vector.tensor_scalar(hgx[:, :], hgx[:, :], GELU_C, 1.0, ALU.mult, ALU.add))
                    nc.vector.tensor_tensor(hgx[:, :], hgx[:, :], HXS[:, :], ALU.mult).then_inc(sem("cmp_poly"), 1)

                def gelu_last(c):
                    dve.wait_ge(sem("cmp_tanh"), b * 2 + c + 1)
                    nc.vector.scalar_tensor_tensor(out=hgx[:, :], in0=hgx[:, :], scalar=1.0, in1=HXS[:, :], op0=ALU.add, op1=ALU.mult
                                                   ).then_inc(sem("cmp_g"), 1)

                def maximum(c0, w, q):
                    lk(nc.vector.tensor_reduce(smx[:, 0, q:q + 1], PSC[:, c0:c0 + w], AX.X, ALU.max))
                    nc.vector.tensor_scalar(smx[:, 1, q:q + 1], smx[:, 0, q:q + 1], -1.0, None, ALU.mult).then_inc(sem("sc_max"), 1)

                for u in range(9):
                    seg_copy(u)
                    if waited and u < 4:
                        max_part(b - 1, u)
                if waited:
                    tail(b - 1)
                seg_copy(9)
                seg_copy(10)
                if waited:
                    output(b - 1)
                gelu_poly(0)
                seg_copy(11)
                seg_copy(12)
                gelu_last(0)
                seg_copy(13)
                seg_copy(14)
                seg_copy(15)
                dve.wait_ge(sem("sc_done"), b * 11 + 1)
                nc.vector.tensor_copy(PSC[:, C_CMP:C_CMP + NCS], PS[0:ROWS, 6, 0:NCS]).then_inc(sem("sc_ev"), 1)
                dve.wait_ge(sem("sc_ev"), b * 11 + 1)
                maximum(C_CMP, NCS, 2)
                dve.wait_ge(sem("sc_exp"), b * 6 + 1)
                lk(nc.vector.reciprocal(smx[:, 3, 2:3], smx[:, 2, 2:3]))
                nc.vector.tensor_scalar(PSC[:, C_CMP:C_CMP + NCS], PSC[:, C_CMP:C_CMP + NCS], smx[:, 3, 2:3], None, ALU.mult).then_inc(sem("pc_ready"), 1)
                dve.wait_ge(sem("imp"), b + 1)
                lk(nc.vector.tensor_copy(impA[:, 4:4 + NCS], PS[0:ROWS, 5, 0:NCS]))
                lk(nc.vector.tensor_reduce(score[:, 0, :], impA[:, 4:4 + 4 * NB].rearrange("p (j n) -> p j n", n=4), AX.X, ALU.add))
                lk(nc.vector.tensor_tensor(score[:, 0, :], score[:, 0, :], impA[:, 3:3 + 4 * NB:4], ALU.add))
                lk(nc.vector.tensor_tensor(score[:, 0, :], score[:, 0, :], bpen[:, :], ALU.add))

                def pause():
                    nc.vector.tensor_copy(smx[:, 3, 0:1], smx[:, 3, 2:3])

                for n in range(2):
                    pause()
                    lk(nc.vector.max(top8[:, n, :], score[:, n, :]))
                    pause()
                    lk(nc.vector.match_replace(score[:, n + 1, :], top8[:, n, :], score[:, n, :], -3e38))
                lk(nc.vector.tensor_scalar(spen[:, :], score[:, 2, :], -1e38, NEG, ALU.is_gt, ALU.mult))
                gelu_poly(1)
                for n in range(10):
                    dve.wait_ge(sem("sc_done"), b * 11 + 2 + n)
                    if n == 0:
                        last = nc.vector.tensor_tensor(PSC[:, 0:WIN], PS[0:ROWS, 2, :], wpen[:, 0:WIN], ALU.add)
                    elif n == 1:
                        last = nc.vector.tensor_tensor(PSC[:, C_XW:C_XW + 2 * DS], PS[0:ROWS, 3, 0:2 * DS], wpen[:, WIN:WIN + 2 * DS], ALU.add)
                    else:
                        last = nc.vector.tensor_tensor(
                            PSC[:, C_SLC + (n - 2) * 512:C_SLC + (n - 1) * 512].rearrange("p (t j e) -> p t j e", t=4, e=2),
                            PS[0:ROWS, 2 + n % 2, :].rearrange("p (t j e) -> p t j e", t=4, e=2),
                            spen[:, 0:NB - 1].unsqueeze(1).unsqueeze(3).to_broadcast([ROWS, 4, NB - 1, 2]), ALU.add)
                    last.then_inc(sem("sc_ev"), 1)
                    if n == 1:
                        dve.wait_ge(sem("sc_ev"), b * 11 + 3)
                        maximum(C_WIN, WIN + DS, 0)
                    if n == 3:
                        gelu_last(1)
                dve.wait_ge(sem("cmp_v"), b + 1)
                nc.vector.tensor_scalar(vc[:, 0, :], PS[:, 4, 0:P], 0.5, None, ALU.mult)
                lk(nc.vector.tensor_scalar(vc[0:NCS - P, 1, :], PS[0:NCS - P, 4, P:2 * P], 0.5, None, ALU.mult))
                assert count[0] == SPER, count[0]

            dve.wait_ge(sem("grow_in"), 16 * NH)
            batch(0, False)
            with dve.Fori(1, DB) as b:
                batch(b, True)
            step[0] += SPER * DB
            for q in range(4):
                max_part(DB - 1, q)
            tail(DB - 1)
            output(DB - 1)

            dve.sem_inc(sem("res_free"), 2)
            dve.wait_ge(sem("x_alpha"), KD)
            for f in range(KD):
                dve.wait_ge(sem("weights_used"), 2 * S_O + f + 1)
                if f:
                    dve.wait_ge(sem("x_res"), f)
                ga = mod[:, 2, f, :]
                x = X[:, f, :]
                nc.vector.scalar_tensor_tensor(out=x[:, 0:LP], in0=dense[f % 2][:, 0:LP], scalar=ga[:, 0:1], in1=x[:, 0:LP],
                                               op0=ALU.mult, op1=ALU.add)
                t = rstd[:, 0:LS].rearrange("p (b q) -> p b q", q=DS)
                nc.vector.tensor_tensor(t, dense[f % 2][:, LP:NT].rearrange("p (b q) -> p b q", q=DS),
                                        ga[:, 1:NC].unsqueeze(2).to_broadcast([P, DB, DS]), ALU.mult).then_inc(sem("res_free"), 1)
                dve.wait_ge(sem("res_free"), f + 3)
                nc.vector.tensor_tensor(x[:, LP:NT], x[:, LP:NT], rstd[:, 0:LS], ALU.add).then_inc(sem("x_res"), 1)
            dve.wait_ge(sem("x_res"), KD)
            ln_dve(1, 3)

            dve.sem_inc(sem("gate_free"), 1)
            dve.sem_inc(sem("h_ready"), 2)

            def hidden(i, n):
                for k in range(n):
                    dve.wait_ge(sem("gate_th"), i * RING + k + 1)
                    th = SQ[:, k % 2, :]
                    nc.vector.scalar_tensor_tensor(out=th, in0=th, scalar=1.0, in1=dense[0], op0=ALU.add, op1=ALU.mult).then_inc(sem("gate_free"), 1)
                    dve.wait_ge(sem("gate_free"), i * RING + k + 2)
                    dve.wait_ge(sem("weights_used"), i * 8 + 2 * S_F1 + 2 * k + 2)
                    nc.vector.scalar_tensor_tensor(out=HT[:, bass.ds(i * RING + k, 1), :].rearrange("p o t -> p (o t)"), in0=dense[1],
                                                   scalar=0.5, in1=th, op0=ALU.mult, op1=ALU.mult).then_inc(sem("h_ready"), 1)
            full = N_F1 // RING
            with dve.Fori(0, full) as i:
                hidden(i, RING)
            hidden(full, N_F1 - full * RING)

            dve.wait_ge(sem("x_alpha"), 2 * KD)
            with dve.Fori(0, KD // 2) as i:
                for f in range(2):
                    nc.vector.tensor_copy(gares[:, f, :], mod[:, 5, bass.ds(i * 2 + f, 1), :].rearrange("p o c -> p (o c)")).then_inc(sem("gares"), 1)
                    dve.wait_ge(sem("gares"), i * 2 + f + 1)
                    ga = gares[:, f, :]
                    dve.wait_ge(sem("weights_used"), i * 8 + 2 * S_F2 + 4 * (f + 1))
                    dve.wait_ge(sem("x_res"), i * 2 + KD + f)
                    x = X[:, bass.ds(i * 2 + f, 1), :].rearrange("p o t -> p (o t)")
                    nc.vector.scalar_tensor_tensor(out=x[:, 0:LP], in0=dense[f][:, 0:LP], scalar=ga[:, 0:1], in1=x[:, 0:LP],
                                                   op0=ALU.mult, op1=ALU.add)
                    t = rstd[:, 0:LS].rearrange("p (b q) -> p b q", q=DS)
                    nc.vector.tensor_tensor(t, dense[f][:, LP:NT].rearrange("p (b q) -> p b q", q=DS),
                                            ga[:, 1:NC].unsqueeze(2).to_broadcast([P, DB, DS]), ALU.mult).then_inc(sem("res_free"), 1)
                    dve.wait_ge(sem("res_free"), i * 2 + KD + f + 3)
                    nc.vector.tensor_tensor(x[:, LP:NT], x[:, LP:NT], rstd[:, 0:LS], ALU.add).then_inc(sem("x_res"), 1)
            dve.wait_ge(sem("x_res"), 2 * KD)
            ln_dve(2, None)


_OUTS = [(P, KD, NT), (GH, DK, DV), (DB, GH, DK, DV), (LP, KVW), (LS, KVW), (LP, KVW), (LS, KVW), (LP, KVW), (DB, WIN, KVW)]


def kernel(**inputs):
    import numpy as np
    import concourse.bacc as bacc
    from concourse import mybir as mb
    from concourse.bass_utils import run_bass_kernel_spmd

    v = {k: np.asarray(x) for k, x in inputs.items()}

    def rows(m):
        return m.reshape(-1, KD, P).transpose(2, 1, 0)

    def tiles(w, per):
        k, f = w.shape
        return w.reshape(k // P, P, f // (P * per), per * P).transpose(2, 1, 0, 3).reshape(f // (P * per), P, -1)

    def vec(x):
        return x.reshape(-1, P).T

    w_in = v["w_in"][0]
    cut = np.cumsum([256, 256, 512, RANK, 512, 512, KVW, KVW, KVW])
    q_g, k_g, v_g, a_g, r_g, q_n, kc, ks, kw, g_n = np.split(w_in, cut, axis=1)
    q_n = q_n.reshape(D, G, R, HD).transpose(0, 2, 1, 3).reshape(D, -1)
    g_n = g_n.reshape(D, G, R, 3).transpose(0, 2, 1, 3).reshape(D, -1)
    w_main = np.concatenate([q_g, k_g, v_g, r_g, q_n, kc, ks, kw], axis=1)
    w_misc = np.concatenate([a_g, g_n], axis=1)
    w_o = v["w_o"][0]
    w_o = np.concatenate([w_o[:GH * DV], w_o[GH * DV:].reshape(G, R, HD, D).transpose(1, 0, 2, 3).reshape(-1, D)])
    f1 = v["w_ffn_in"][0].reshape(KD, P, 2, KF, P).transpose(3, 1, 0, 2, 4).reshape(KF, P, -1)
    f2 = v["w_ffn_out"][0].reshape(2, KF // 2, P, KD, P).transpose(3, 0, 2, 1, 4).reshape(2 * KD, P, -1)
    ins = {
        "x_t": rows(np.concatenate([v["x_prompt"].reshape(LP, D), v["x_sample"].reshape(LS, D)])),
        "c_t": rows(np.concatenate([v["c_prompt"], v["c_sample"]])),
        "w_ada": tiles(v["w_ada"][0], 2), "b_ada": vec(v["b_ada"][0]).reshape(P, 6, KD),
        "lnv": np.stack([vec(v[n].reshape(-1)) for n in ("ln_in_g", "ln_in_b", "ln1_g", "ln1_b", "ln2_g", "ln2_b")], 1),
        "w_in": tiles(w_main, 2), "w_misc": w_misc.reshape(KD, P, MISC).transpose(1, 0, 2).reshape(P, -1),
        "wa2": v["gla_w_a2"][0], "ba": vec(v["gla_b_a"][0]), "gng": v["gla_norm_g"][0].reshape(P, 1),
        "pe": v["cmp_pe"][0].reshape(2, JP, 2, 2, HD).transpose(2, 4, 3, 0, 1).reshape(P, 2, 2, JP),
        "w1": v["cmp_w1"][0].reshape(2, 2, JP, P, HID).transpose(3, 0, 1, 2, 4),
        "b1": v["cmp_b1"][0].T, "w2": v["cmp_w2"][0].transpose(1, 0, 2),
        "w_o": tiles(w_o, 2), "w_f1": f1, "w_f2": f2,
        "state": v["state_gla"][0].reshape(DB, 2, 2 * DK, DV).transpose(2, 1, 0, 3),
        "ptab": v["page_table"].T,
        "cmp": v["cache_cmp_kv"][0].reshape(-1, SPAN * KVW), "slc": v["cache_slc_kv"][0].reshape(-1, SPAN * KVW),
        "win": v["cache_win_kv"][0].reshape(DB, WIN, KVW),
    }
    nc = bacc.Bacc("TRN2", target_bir_lowering=False, num_devices=1, dynamic_dma_scratch_size=4096)
    arrays, aps = {}, {}
    for name, x in ins.items():
        x = np.ascontiguousarray(x)
        arrays[f"in_{name}_dram"] = x
        aps[name] = nc.dram_tensor(f"in_{name}_dram", x.shape, mb.dt.from_np(x.dtype), kind="ExternalInput").ap()
    outs = [nc.dram_tensor(f"out_{i}_dram", s, F32, kind="ExternalOutput").ap() for i, s in enumerate(_OUTS)]
    build(nc, aps, outs)
    res = run_bass_kernel_spmd(nc, [arrays], core_ids=[0]).results[0]
    y, gp, gs, cp, c_s, slp, sls, wp, ws = (res[f"out_{i}_dram"] for i in range(len(_OUTS)))
    y = y.transpose(2, 1, 0).reshape(NT, D)
    kv = (2, G, HD)
    return (y[:LP].reshape(1, LP, D), y[LP:].reshape(DB, DS, D), gp.reshape(1, 1, GH, DK, DV), gs.reshape(1, DB, GH, DK, DV),
            cp.reshape(1, 1, LP, *kv), c_s.reshape(1, DB, DS, *kv), slp.reshape(1, 1, LP, *kv), sls.reshape(1, DB, DS, *kv),
            wp.reshape(1, 1, LP, *kv), ws.reshape(1, DB, WIN, *kv))
```

```python
from contextlib import ExitStack

import concourse.bass as bass
from concourse import mybir

ALU = mybir.AluOpType
ACT = mybir.ActivationFunctionType
F32 = mybir.dt.float32
I32 = mybir.dt.int32
U32 = mybir.dt.uint32
AX = mybir.AxisListType

P = 128
D = 1024
KD = D // P
LP = 512
TT = LP // P
DB, DS = 8, 4
LS = DB * DS
NT = LP + LS
HALF = NT // 2
NC = 1 + DB
FF = 2816
KF = FF // P
ALPHA = 2.0 ** 0.25

GH, DK, DV = 4, 64, 128
RANK, TAU = 16, 16.0
CH = 32
NCH = LP // CH
NH, G, R, HD = 8, 2, 4, 64
ROWS = G * R * DS
KVW = 2 * G * HD
PAGES, PSZ = 32, 128
PAST = PAGES * PSZ
WIN = 512
SPAN = PAST // P
SEG = 16
NSEG = PAST // SEG
NCS = NSEG - 1
NSEGP = LP // SEG
NCP = NSEGP - 1
HID = 128
JP = SEG // 2
NB = PAST // 64 + 1
NEG = -1e30
GELU_A, GELU_C = 0.7978845608028654, 0.044715

ZQG, ZKG, ZVG, ZRG, ZQN, ZKV = 0, 2, 4, 8, 12, 16
ZT = 22
MISC = RANK + 3 * NH

C_WIN, C_XW, C_XS, C_SLC, C_CMP = 0, WIN, WIN + DS, WIN + 2 * DS, WIN + 2 * DS + PAST
C_ALL = C_CMP + NCS + 1
NPT = 4 + SPAN + 2 + 2
PART = (DS + PAST) // 4

RING, SLOT = 4, 2 * P * KD
N_ADA1, N_IN, N_ADA3, N_O, N_F1, N_F2 = 8, 12, 4, 4, 22, 16
S_IN = N_ADA1
TURNS = N_IN // RING
S_O = S_IN + 2 * N_IN
S_ADA3 = S_O + N_O
S_F1 = S_ADA3 + N_ADA3
S_F2 = S_F1 + N_F1


def build(nc, a, out):
    (y_t, gla_p, gla_s, cmp_p, cmp_s, slc_p, slc_s, win_p, win_s) = out
    gate_scr = nc.dram_tensor("gate_scr", (LS, R, G, 3), F32, kind="Internal").ap()

    with ExitStack() as ctx:
        def sb(name, shape, dt=F32):
            return ctx.enter_context(nc.sbuf_tensor(name, shape, dt))

        sems = {}

        def sem(name):
            if name not in sems:
                sems[name] = ctx.enter_context(nc.semaphore(name))
            return sems[name]

        RX = sb("trunk", [P, KD * NT])
        RM = sb("mixreg", [P, KD * NT])
        RZ = sb("zreg", [P, ZT * NT])
        W1 = sb("w1", [P, 2, 2, JP, HID])
        RR = sb("ringreg", [P, RING * SLOT])
        RC = sb("creg", [P, SPAN * KVW])
        RS = sb("sreg", [P, SPAN * KVW + 4 * KVW])

        X = RX[:, :].rearrange("p (k t) -> p k t", k=KD)
        XC = RM[:, :].rearrange("p (k t) -> p k t", k=KD)
        MIXT = XC
        U = RC[:, 0:KD * NT].rearrange("p (k t) -> p k t", k=KD)
        bias_row = RC[0:1, 0:2 * HID]
        xsum = RC[:, 0:NT]
        SQ = RS[:, 0:KD * NT].rearrange("p (k t) -> p k t", k=KD)
        Z = RZ[:, :].rearrange("p (k t) -> p k t", k=ZT)
        HT = Z
        ring = [RR[:, s * SLOT:(s + 1) * SLOT] for s in range(RING)]
        wslot = [r.rearrange("p (k c) -> p k c", k=KD) for r in ring]
        wslot1 = [r.rearrange("p (k h c) -> p k h c", k=KD, h=2) for r in ring]
        wslot2 = [r[:, 0:KF // 2 * P].rearrange("p (k c) -> p k c", c=P) for r in ring]

        ident = sb("ident", [P, P])
        ones = sb("ones", [P, P])
        pen = sb("pen", [P, LP])
        mod = sb("mod", [P, 6, KD, NC])
        cs = sb("cs", [P, KD, NC])
        cth = sb("cth", [P, KD, NC])
        bada = sb("bada", [P, 6, KD])
        lnv = sb("lnv", [P, 6, KD])
        rstd = sb("rstd", [P, NT])
        w2 = sb("w2", [P, 2, HD])
        pe_t = sb("pe_t", [P, 2, 2, JP])
        cb1 = sb("cb1", [P, 2])
        cbias = sb("cbias", [P, 2])
        wa2 = sb("wa2", [RANK, GH * DK])
        ba = sb("ba", [P, 2])
        gng = sb("gng", [P, 1])
        zM = sb("zM", [MISC, NT])
        GT = sb("GT", [P, TT + 1, MISC])
        zS = sb("zS", [P, 8, LS])
        grow = sb("grow", [ROWS, DB, 3])
        ptab = sb("ptab", [P, DB], I32)
        idx = sb("idx", [P, DB], U32)
        pidx = sb("pidx", [P, 1], I32)
        pmod = sb("pmod", [P, 1], I32)
        pmodf = sb("pmodf", [P, 1])
        qbd = sb("qbd", [P, G, R, DS])
        knew = sb("knew", [P, 2, DS])
        gcur = sb("gcur", [ROWS, 3])
        VX = sb("VX", [DS, 2, P])
        bpen = sb("bpen", [ROWS, NB])
        spen = sb("spen", [ROWS, NB])
        rsum = sb("rsum", [ROWS, ROWS])
        impA = sb("impA", [ROWS, 4 * (NB + 1)])
        score = sb("score", [ROWS, 3, NB])
        top8 = sb("top8", [ROWS, 2, 8])
        smx = sb("smx", [ROWS, 4, 3])
        pmx = sb("pmx", [ROWS, 2, 4])
        gdec = sb("gdec", [P, 2, NCH + DB])
        gares = sb("gares", [P, 2, NC])
        wpen = sb("wpen", [ROWS, WIN + 2 * DS])

        PS = ctx.enter_context(nc.psum_tensor("PS", [P, 8, 512], F32))
        dense = [PS[:, 4 + 2 * b:6 + 2 * b, 0:HALF] for b in range(2)]
        stat = [PS[:, 2 * b:2 * b + 2, 0:HALF] for b in range(2)]
        out_acc = stat + dense

        def halves(t):
            return t.rearrange("p (h t) -> p h t", h=2)

        def pmods(bank):
            return PS[:, bank, 0:KD * NC].rearrange("p (k c) -> p k c", k=KD)
        ada_rows = [RS[0:NC, 4352 + b * 2 * P:4352 + (b + 1) * 2 * P] for b in range(2)]

        VW = DV * GH + 3 * KVW
        VT = RS[:, 0:(TT + 1) * VW].rearrange("p (t c) -> p t c", t=TT + 1)
        S1 = RS[:, (TT + 1) * VW:(TT + 1) * VW + (NCH + 1) * P].rearrange("p (c v) -> p c v", c=NCH + 1)
        GW = 2 * NT
        LA, BC, DM, DL = (RR[:, i * GW:(i + 1) * GW].rearrange("p (h t) -> p h t", h=2) for i in range(4))
        ATT = RR[:, 2 * GW:2 * GW + 16 * P].rearrange("p (h t i) -> p h t i", h=GH, t=TT)
        SQG = RR[:, 0:GH * NT].rearrange("p (h t) -> p h t", h=GH)
        S0 = RR[:, 4 * GW:4 * GW + 2 * DB * P].rearrange("p (h b v) -> p h b v", h=2, b=DB)
        KE = RR[:, 6400:6400 + (TT + 1) * 256].rearrange("p (t c) -> p t c", t=TT + 1)
        ATTS = RR[0:LS, 7680:7680 + GH * LS].rearrange("p (h i) -> p h i", h=GH)
        E = [RC[:, i * GW:(i + 1) * GW].rearrange("p (h t) -> p h t", h=2) for i in range(4)]
        TH = RC[:, 0:GH * NT].rearrange("p (h t) -> p h t", h=GH)
        S0P = RC[:, 4 * GW:4 * GW + (NCH + 1) * P].rearrange("p (c v) -> p c v", c=NCH + 1)
        SST = [S0P, S1]
        VMB = RC[0:LS, 6528:6528 + DB * P].rearrange("p (b v) -> p b v", b=DB)
        rmask = RC[:, 7552:7552 + NT]
        gmask = sb("gmask", [P, CH])
        smask = sb("smask", [LS, LS])
        bmask = sb("bmask", [LS, DB])

        QB = RZ[:, ZVG * NT:(ZVG + 4) * NT].rearrange("p (h l t) -> p h l t", h=2, l=2)

        XTP = RM[:, 4 * NT:4 * NT + 16 * 64].rearrange("p (u g n) -> p u g n", u=16, g=G)
        HX = RM[:, 4 * NT + 1024:4 * NT + 1024 + 62 * 2].rearrange("p (c g n) -> p c g n", c=2, g=G)
        HG = RM[:, 4 * NT + 1152:4 * NT + 1152 + 62 * 2].rearrange("p (c g n) -> p c g n", c=2, g=G)
        o_ = (TT + 1) * VW + (NCH + 1) * P
        kcTp = RS[:, o_:o_ + NCP]
        vcp = RS[0:NCP, o_ + 32:o_ + 32 + P]
        pcp = RS[:, o_ + 160:o_ + 160 + TT * NCP].rearrange("p (t n) -> p t n", t=TT)
        PCT = RZ[0:NCP, 2048:2048 + G * R * LP].rearrange("p (h t) -> p h t", h=G * R)
        PB = [RR[:, b * 1024:(b + 1) * 1024] for b in range(3)]
        PTB = [RR[:, 3072 + b * 1024:3072 + (b + 1) * 1024] for b in range(2)]
        qcur = RR[:, 5120:5120 + 2 * LP].rearrange("p (r t) -> p r t", r=2)
        pst = RR[:, 6144:6144 + 2 * 8].rearrange("p (b k j) -> p b k j", b=2, k=4)
        gpc = RR[:, 6160:6160 + 2 * TT * 6].rearrange("p (r t c) -> p r t c", r=2, t=TT)
        PCW = R * TT * NCP
        pc = RZ[:, 0:G * PCW]
        pcst = RZ[:, G * PCW:G * PCW + 3 * G * R * TT].rearrange("p (k j) -> p k j", k=3)

        CB = RC[:, :].rearrange("p (e s c x) -> p e s c x", e=2, s=SEG, c=2)
        SBF = RS[:, 0:SPAN * KVW]
        SBV = SBF.rearrange("p (t c x) -> p t c x", t=SPAN, c=2)
        WBF = RS[:, SPAN * KVW:SPAN * KVW + 4 * KVW]
        WBV = WBF.rearrange("p (t c x) -> p t c x", t=4, c=2)
        XTS = RR[:, :].rearrange("p (u g n) -> p u g n", u=16, g=G)
        KT = RZ[:, 0:SPAN * P]
        KTW = RZ[:, 4096:4096 + WIN]
        PSC = RZ[0:ROWS, 4608:4608 + C_ALL]
        PTS = RZ[:, 4608 + C_ALL:4608 + C_ALL + NPT * ROWS].rearrange("p (n r) -> p n r", r=ROWS)
        o_ = 4608 + C_ALL + NPT * ROWS
        kcT = RZ[:, o_:o_ + NSEG]
        vc = sb("vc", [P, 2, P])
        hgx = RZ[:, o_ + NSEG:o_ + NSEG + 2 * NCS]
        osb = RZ[0:ROWS, o_ + NSEG + 2 * NCS:o_ + NSEG + 2 * NCS + P]
        assert o_ + NSEG + 2 * NCS + P <= ZT * NT
        HXS = sb("hxs", [P, 2 * NCS])

        kt_bank = (0, 1, 7)

        def seg_src(u, h, g):
            return PS[g * HD:(g + 1) * HD, u % 2, h * 2 * P:(h + 1) * 2 * P].rearrange("p (e n) -> p e n", e=2)

        def seg_dst(u, h, g):
            return XTS[h * HD:(h + 1) * HD, u, g, :].rearrange("p (n e) -> p e n", e=2)

        def matmul(o, lhsT, rhs, start, stop, **kw):
            return nc.tensor.matmul(o, lhsT, rhs, start=start, stop=stop, **kw)

        block = ctx.enter_context(nc.Block())

        @block.sync
        def _(sp):
            sp.dma_start(X, a["x_t"]).then_inc(sem("x_in"), 16)

            def stretch(src, base, count, views):
                full = count // RING
                with sp.Fori(0, full) as i:
                    for k in range(RING):
                        sp.wait_ge(sem("weights_used"), i * (2 * RING) + 2 * (base + k - RING + 1))
                        s = (base + k) % RING
                        sp.dma_start(views[s], src[bass.ds(i * RING + k, 1)].rearrange("o p x -> p (o x)")
                                     ).then_inc(sem(f"ring_full{s}"), 16)
                for n in range(base + full * RING, base + count):
                    sp.wait_ge(sem("weights_used"), 2 * (n - RING + 1))
                    sp.dma_start(views[n % RING], src[n - base]).then_inc(sem(f"ring_full{n % RING}"), 16)

            for n in range(RING):
                sp.dma_start(ring[n], a["w_ada"][n]).then_inc(sem(f"ring_full{n}"), 16)
            for n in range(RING, N_ADA1):
                sp.wait_ge(sem("weights_used"), 2 * (n - RING + 1))
                sp.dma_start(ring[n % RING], a["w_ada"][n]).then_inc(sem(f"ring_full{n % RING}"), 16)

            def turn_loads(i, slots):
                for k in slots:
                    for src, n in ((a["w_in"], S_IN + 2 * k), (a["w_ada"][N_ADA1:], S_IN + 2 * k + 1)):
                        sp.wait_ge(sem("weights_used"), i * 16 + 2 * (n - RING + 1))
                        sp.dma_start(ring[n % RING], src[bass.ds(i * RING + k, 1)].rearrange("o p x -> p (o x)")
                                     ).then_inc(sem(f"ring_full{n % RING}"), 16)
            with sp.Fori(0, TURNS - 1) as i:
                turn_loads(i, range(RING))
            turn_loads(TURNS - 1, range(RING - 1))
            n = S_IN + 2 * N_IN - 2
            sp.wait_ge(sem("weights_used"), 2 * (n - RING + 1))
            sp.dma_start(ring[n % RING][:, 0:KD * MISC], a["w_misc"]).then_inc(sem(f"ring_full{n % RING}"), 16)
            sp.wait_ge(sem("weights_used"), 2 * (n - RING + 2))
            sp.dma_start(ring[(n + 1) % RING], a["w_ada"][N_ADA1 + N_IN - 1]).then_inc(sem(f"ring_full{(n + 1) % RING}"), 16)

            sp.wait_ge(sem("weights_used"), 2 * S_O)
            sp.dma_start(S0, a["state"]).then_inc(sem("s0_in"), 16)
            sp.wait_ge(sem("rows_ready"), 3 * (TT + 1))
            for o, c in ((cmp_p, 512), (slc_p, 768), (win_p, 1024)):
                sp.dma_start(o.rearrange("(t p) c -> p t c", p=P), VT[:, 0:TT, c:c + KVW]).then_inc(sem("kv_out"), 16)
            for o, c in ((cmp_s, 512), (slc_s, 768)):
                sp.dma_start(o, VT[0:LS, TT, c:c + KVW]).then_inc(sem("kv_out"), 16)
            for b in range(DB):
                sp.dma_start(win_s[b, WIN - DS:WIN, :],
                             VT[b * DS:(b + 1) * DS, TT, 1024:1280]).then_inc(sem("kv_out"), 16)
            sp.dma_start(win_s[:, 0:WIN - DS, :], a["win"][:, DS:WIN, :]).then_inc(sem("winc_out"), 16)
            sp.wait_ge(sem("gates_ready"), 1)
            sp.dma_start(gate_scr.rearrange("t r g j -> t (r g j)"), GT[0:LS, TT, RANK:MISC]).then_inc(sem("gate_out"), 16)
            sp.wait_ge(sem("gate_out"), 16)
            for g in range(G):
                for r in range(R):
                    sp.dma_start(grow[(g * R + r) * DS:(g * R + r + 1) * DS, :, :],
                                 gate_scr[:, r, g, :].rearrange("(b q) j -> q b j", q=DS)).then_inc(sem("grow_in"), 16)
            sp.wait_ge(sem("gla_scan"), 2 * NCH)
            for h in range(2):
                sp.dma_start(gla_p[2 * h:2 * h + 2].rearrange("h k v -> (h k) v"),
                             SST[h][:, NCH, :]).then_inc(sem("gla_out"), 16)
            for h in range(2):
                sp.wait_ge(sem("gla_snew"), h + 1)
                sp.dma_start(gla_s[:, 2 * h:2 * h + 2].rearrange("b h k v -> (h k) b v"),
                             S0[:, h]).then_inc(sem("gla_out"), 16)
            sp.wait_ge(sem("kv_out"), 16 * (5 + DB))
            sp.wait_ge(sem("gla_out"), 64)

            def batch(b, waited):
                if waited:
                    sp.wait_ge(sem("pv_done"), b)
                else:
                    sp.wait_ge(sem("zs"), 6)
                sp.dma_start(WBF, a["win"][bass.ds(b, 1)].rearrange("o (p t) c -> p (o t c)", p=P)).then_inc(sem("win_in"), 16)
                sp.dma_start(VX[:, 0, :], win_s[bass.ds(b, 1), WIN - DS:WIN, P:KVW].rearrange("o q c -> (o q) c")).then_inc(sem("win_in"), 16)
                sp.dma_start(VX[:, 1, :], slc_s.rearrange("(b q) c -> b q c", q=DS)[bass.ds(b, 1), :, P:KVW].rearrange("o q c -> (o q) c")).then_inc(sem("win_in"), 16)

            batch(0, False)
            with sp.Fori(1, DB) as b:
                batch(b, True)
            sp.wait_ge(sem("cmp_mm"), 16 * DB)
            stretch(a["w_o"], S_O, N_O, ring)
            stretch(a["w_ada"][N_ADA1 + N_IN:], S_ADA3, N_ADA3, ring)
            stretch(a["w_f1"], S_F1, N_F1, ring)
            stretch(a["w_f2"], S_F2, N_F2, [r[:, 0:KF // 2 * P] for r in ring])
            for k in range(0, KD, 2):
                sp.wait_ge(sem("ln_x"), 2 * KD + k + 2)
                sp.dma_start(y_t[:, k:k + 2, :], X[:, k:k + 2, :]).then_inc(sem("y_out"), 16)
            sp.wait_ge(sem("y_out"), 16 * (KD // 2))
            sp.wait_ge(sem("winc_out"), 16)

        @block.gpsimd
        def _(pool):
            nset = [0]

            def fill(t, v):
                nset[0] += 1
                nc.gpsimd.memset(t, v).then_inc(sem("pool_set"), 1)
                pool.wait_ge(sem("pool_set"), nset[0])
            fill(ident[:, :], 0.0)
            nc.gpsimd.affine_select(out=ident[:, :], in_=ident[:, :], compare_op=ALU.not_equal, fill=1.0, base=0, pattern=[[-1, P]],
                                    channel_multiplier=1).then_inc(sem("ident_ready"), 1)
            fill(ones[:, :], 1.0 / D)
            small = ((lnv, a["lnv"]), (bada, a["b_ada"]), (pe_t, a["pe"]), (cb1, a["b1"]), (w2, a["w2"]),
                     (wa2, a["wa2"]), (ba, a["ba"]), (gng, a["gng"]))
            for dst, src in small:
                pool.dma_start(dst[:], src).then_inc(sem("consts_in"), 16)
            pool.dma_start(ptab[:, :], a["ptab"].unsqueeze(1).to_broadcast([PAGES, 4, DB])).then_inc(sem("ptab_in"), 16)
            pool.wait_ge(sem("ident_ready"), 1)
            fill(pen[:, :], 0.0)
            fill(gmask[:, :], 1.0)
            fill(smask[:, :], 1.0)
            fill(bmask[:, :], 1.0)
            fill(rsum[:, :], 0.0)
            fill(wpen[:, :], 0.0)
            fill(bpen[:, :], 0.0)
            fill(impA[:, :], 0.0)
            fill(qbd[:, :, :, :], 0.0)

            nsel = [0]

            def sel(t, op, base, pattern, cm, fillv):
                nsel[0] += 1
                nc.gpsimd.affine_select(out=t, in_=t, compare_op=op, fill=fillv, base=base, pattern=pattern,
                                        channel_multiplier=cm).then_inc(sem("pool_sel"), 1)
                pool.wait_ge(sem("pool_sel"), nsel[0])

            sel(pen[:, LP - P:LP], ALU.is_ge, 0, [[-1, P]], 1, NEG)
            for c in range(4):
                sel(gmask[32 * c:32 * c + 32, :], ALU.is_ge, 0, [[1, CH]], -1, 0.0)
            sel(smask[:, :], ALU.is_ge, 0, [[1, LS]], -1, 0.0)
            sel(bmask[:, :], ALU.is_ge, 0, [[-DS, DB]], 1, 0.0)
            for d in range(-(R - 1), R):
                sel(rsum[:, :], ALU.not_equal, DS * d, [[-1, ROWS]], 1, 1.0)
                sel(bmask[:, :], ALU.is_ge, DS - 1, [[DS, DB]], -1, 0.0)
            sel(bpen[:, :], ALU.not_equal, 0, [[1, NB]], 0, 1e4)
            sel(bpen[:, :], ALU.not_equal, -(NB - 1), [[1, NB]], 0, 1e4)
            sel(bpen[:, :], ALU.not_equal, -(NB - 2), [[1, NB]], 0, 1e4)
            nc.gpsimd.iota(pidx[:, :], pattern=[[0, 1]], base=0, channel_multiplier=1).then_inc(sem("pidx"), 1)
            pool.wait_ge(sem("pidx"), 1)
            sel(rsum[0:ROWS, 0:ROWS // 2], ALU.is_ge, ROWS // 2 - 1, [[0, ROWS // 2]], -1, 0.0)
            sel(rsum[0:ROWS, ROWS // 2:ROWS], ALU.is_ge, -(ROWS // 2), [[0, ROWS // 2]], 1, 0.0)
            pool.wait_ge(sem("pool_sel"), nsel[0])
            nc.gpsimd.memset(top8[:, :, :], 0.0).then_inc(sem("pool_consts"), 1)
            pool.wait_ge(sem("pool_consts"), 1)
            nc.gpsimd.memset(rmask, 1.0).then_inc(sem("rmask0"), 1)
            pool.wait_ge(sem("rmask0"), 1)
            nc.gpsimd.memset(rmask[:, 0:LP].rearrange("p (c i) -> p c i", i=CH)[:, :, 0:1], 0.0).then_inc(sem("rmask"), 1)
            pool.wait_ge(sem("rmask"), 1)
            nc.gpsimd.memset(rmask[:, LP:NT].rearrange("p (c i) -> p c i", i=DS)[:, :, 0:1], 0.0).then_inc(sem("rmask"), 1)

            pool.wait_ge(sem("mod_free"), 3)
            pool.dma_start(W1[:], a["w1"]).then_inc(sem("w1_in"), 16)

            pool.wait_ge(sem("mod_free"), 6)
            nc.gpsimd.memset(pcp, 0.0).then_inc(sem("pcp0"), 1)
            pool.wait_ge(sem("pcp0"), 1)
            nc.gpsimd.affine_select(out=pcp, in_=pcp, compare_op=ALU.is_ge, fill=NEG, base=-(2 * SEG - 1),
                                    pattern=[[P, TT], [-SEG, NCP]], channel_multiplier=1).then_inc(sem("pcp"), 1)
            pool.wait_ge(sem("pcp"), 1)

            pool.wait_ge(sem("gla_done"), GH)
            pool.wait_ge(sem("gla_out"), 64)
            pool.wait_ge(sem("idx"), 1)
            for b in range(DB):
                if b:
                    pool.wait_ge(sem("seg_t"), 16 * b)
                    pool.wait_ge(sem("slc_in"), 16 * b)
                nc.gpsimd.indirect_dma_start(out=RC[:, :], out_offset=None, in_=a["cmp"],
                                             in_offset=bass.IndirectOffsetOnAxis(ap=idx[:, b:b + 1], axis=0)
                                             ).then_inc(sem("cmp_in"), 16)
                pool.wait_ge(sem("cmp_in"), 16 * (b + 1))
                if b:
                    pool.wait_ge(sem("pv_done"), b)
                else:
                    pool.wait_ge(sem("zs"), 6)
                nc.gpsimd.indirect_dma_start(out=SBF, out_offset=None, in_=a["slc"],
                                             in_offset=bass.IndirectOffsetOnAxis(ap=idx[:, b:b + 1], axis=0)
                                             ).then_inc(sem("slc_in"), 16)

        @block.tensor
        def _(pe):
            def sum_mean(nth):
                pe.wait_ge(sem("x_sum"), nth * (KD + 1))
                for h in range(2):
                    last = matmul(stat[0][:, h, :], ones[:, :], xsum[:, h * HALF:(h + 1) * HALF], True, True)
                last.then_inc(sem("ln_mean"), 1)

            def ln_mean():
                for k in range(KD):
                    for h in range(2):
                        last = matmul(stat[0][:, h, :], ones[:, :], X[:, k, h * HALF:(h + 1) * HALF], k == 0, k == KD - 1)
                last.then_inc(sem("ln_mean"), 1)

            def ln_var(nth):
                for k in range(KD):
                    pe.wait_ge(sem("ln_sq"), nth * KD + k + 1)
                    for h in range(2):
                        last = matmul(stat[1][:, h, :], ones[:, :], SQ[:, k, h * HALF:(h + 1) * HALF], k == 0, k == KD - 1)
                last.then_inc(sem("ln_var"), 1)

            def slot_ready(base, i, k):
                pe.wait_ge(sem(f"ring_full{(base + k) % RING}"), i * 16 + 16 * ((base + k) // RING + 1))

            def slot_ready_in_turn(n, i):
                pe.wait_ge(sem(f"ring_full{n % RING}"), i * 32 + 16 * (n // RING + 1))

            def ada(n, a_, bank, i=0):
                if a_ >= 2 or not isinstance(i, int):
                    pe.wait_ge(sem("ada_row"), i * 4 + a_ - 1)
                for c in range(KD):
                    last = matmul(PS[0:NC, bank + a_ % 2, 0:2 * P], cs[:, c, :], wslot[n % RING][:, c, :], c == 0, c == KD - 1)
                last.then_inc(sem("weights_used"), 2)

            def ada_turn(a_, bank):
                k = a_ % 4
                for f in range(2):
                    last = nc.tensor.transpose(pmods(bank)[:, 2 * k + f, :], ada_rows[a_ % 2][:, f * P:(f + 1) * P], ident[0:NC, 0:NC])
                last.then_inc(sem("ada_t"), 1)

            def project(w, b, src, m=P):
                for k in range(KD):
                    for h in range(2):
                        last = matmul(dense[b][0:m, h, :], w(k), src[:, k, h * HALF:(h + 1) * HALF], k == 0, k == KD - 1)
                return last

            pe.wait_ge(sem("ident_ready"), 1)
            pe.wait_ge(sem("pool_set"), 2)
            pe.wait_ge(sem("x_in"), 16)
            ln_mean()
            pe.wait_ge(sem("silu_c"), 1)
            for k in range(N_ADA1 + 1):
                if k < N_ADA1:
                    slot_ready(k, 0, 0)
                    ada(k, k, 6)
                if k == 1:
                    ln_var(0)
                if k >= 1:
                    pe.wait_ge(sem("ada_row"), k)
                    ada_turn(k - 1, 4 + (k - 1) // 4)

            pe.wait_ge(sem("ln_u"), KD + 1)

            def in_turn(i, first, last_turn):
                for k in range(RING):
                    n = S_IN + 2 * k
                    slot_ready_in_turn(n, i)
                    if last_turn and k == RING - 1:
                        pe.wait_ge(sem("dense_free"), ZT + 1)
                        wm = ring[n % RING][:, 0:KD * MISC].rearrange("p (k c) -> p k c", k=KD)
                        project(lambda c: wm[:, c, :], 0, U, MISC).then_inc(sem("weights_used"), 2)
                    else:
                        for f in range(2):
                            pe.wait_ge(sem("dense_free"), i * 8 + 2 * k + f + 1)
                            project(lambda c: wslot[n % RING][:, c, f * P:(f + 1) * P], f, U).then_inc(sem("weights_used"), 1)
                    slot_ready_in_turn(n + 1, i)
                    if k:
                        pe.wait_ge(sem("ada_row"), i * 4 + N_ADA1 + k)
                        if k == 1:
                            pe.wait_ge(sem("mod_free"), i + 3)
                    ada(n + 1, k + N_ADA1, 0, i)
                    if k:
                        ada_turn(k - 1, 2)
                pe.wait_ge(sem("ada_row"), i * 4 + N_ADA1 + 4)
                nc.tensor.transpose(PS[:, 3, 0:P], ident[:, :], ident[:, :])
                ada_turn(3, 2)
            with pe.Fori(0, TURNS - 1) as i:
                in_turn(i, False, False)
            in_turn(TURNS - 1, False, True)
            pe.wait_ge(sem("dense_free"), ZT + 1 + 2)
            pe.wait_ge(sem("mod_free"), 6)

            src = [ZVG + i for i in range(4)] + [ZKV + i for i in range(6)]
            for t in range(TT + 1):
                n = P if t < TT else LS
                cols = slice(t * P, t * P + n)
                if t >= 2:
                    pe.wait_ge(sem("rows_ready"), 3 * (t - 1))
                bank = 4 * (t % 2)
                for q, z in enumerate(src):
                    last = nc.tensor.transpose(PS[0:n, bank + q // 4, (q % 4) * P:(q % 4 + 1) * P], Z[:, z, cols], ident[:, :])
                    if q == 3 or q == 7:
                        last.then_inc(sem("rows_t"), 1)
                nc.tensor.transpose(PS[0:n, bank + 2, 256:256 + MISC], zM[:, cols], ident[0:MISC, 0:MISC]).then_inc(sem("rows_t"), 1)

            pe.wait_ge(sem("rows_ready"), 3 * (TT + 1))
            pe.wait_ge(sem("w1_in"), 16)
            for c in range(2):
                for n in range(2 * JP):
                    last = matmul(PS[0:1, 6, c * HID:(c + 1) * HID], pe_t[:, c, n // JP, n % JP:n % JP + 1], W1[:, c, n // JP, n % JP, :],
                                  n == 0, n == 2 * JP - 1)
            last.then_inc(sem("pe_bias"), 1)

            for h in range(2):
                for n in range(2):
                    last = matmul(stat[h][:, n, :], wa2[:, h * P:(h + 1) * P], zM[0:RANK, n * HALF:(n + 1) * HALF], True, True)
                last.then_inc(sem("decay_x"), 1)
            pe.wait_ge(sem("pe_row"), 1)
            for c in range(2):
                last = nc.tensor.transpose(PS[:, 6, 256 + c:257 + c], bias_row[:, c * HID:(c + 1) * HID], ident[0:1, 0:1])
            last.then_inc(sem("pe_bias"), 1)
            pe.wait_ge(sem("xtp"), 8)
            pe.wait_ge(sem("rows_ready"), 3 * (TT + 1))
            for u in range(16):
                c, j = u // JP, u % JP
                for m in range(2):
                    last = matmul(PS[:, 4 + c, 0:2 * NCP].rearrange("p (g n) -> p g n", g=2), W1[:, c, m, j, :],
                                  XTP[:, u, :, m:m + NCP], j == 0 and m == 0, j == JP - 1 and m == 1)
                if j == JP - 1:
                    last.then_inc(sem("cmpp_mm"), 1)
            pe.wait_ge(sem("gla_q"), 2)
            for h in range(GH):
                hp, lo = h // 2, (h % 2) * DK
                for t in range(TT):
                    for c in range(4):
                        cols = slice(t * P + c * CH, t * P + (c + 1) * CH)
                        matmul(PS[c * CH:(c + 1) * CH, h % 2, (hp * TT + t) * CH:(hp * TT + t + 1) * CH],
                               E[1][lo:lo + DK, hp, cols], E[0][lo:lo + DK, hp, cols], True, True)
                last = matmul(PS[0:LS, h % 2, 256 + hp * LS:256 + (hp + 1) * LS],
                              E[1][lo:lo + DK, hp, LP:NT], E[0][lo:lo + DK, hp, LP:NT], True, True)
            last.then_inc(sem("gla_att"), 1)
            pe.wait_ge(sem("cmpp_g"), 2)
            pe.wait_ge(sem("cbias"), 1)
            for g in range(G):
                last = matmul(PS[g * HD:(g + 1) * HD, 7, 0:NCP], w2[:, 0, :], HG[:, 0, g, :], True, True)
            for g in range(G):
                last = matmul(PS[0:NCP, 7, P + g * HD:P + (g + 1) * HD], HG[:, 1, g, :], w2[:, 1, :], True, True)
            last.then_inc(sem("cmpp_kv"), 1)
            pe.wait_ge(sem("gla_q"), 3)
            for h in range(2):
                for t in range(TT + 1):
                    n = P if t < TT else LS
                    last = nc.tensor.transpose(PS[0:n, 4 + t // 2, ((t % 2) * 2 + h) * P:((t % 2) * 2 + h + 1) * P],
                                               E[3][:, h, t * P:t * P + n], ident[:, :])
            last.then_inc(sem("gla_ket"), 1)
            pe.wait_ge(sem("gla_ke"), 3)
            pe.wait_ge(sem("cmpp_ev"), 2)
            for hp in range(2):
                if hp == 1:
                    pe.wait_ge(sem("gla_attm"), 10)
                for c in range(4):
                    for t in range(TT):
                        for lo in range(2):
                            h = 2 * hp + lo
                            last = matmul(PS[lo * DK:(lo + 1) * DK, 4 - 4 * hp + c, t * P:(t + 1) * P],
                                          KE[c * CH:(c + 1) * CH, t, h * DK:(h + 1) * DK],
                                          VT[c * CH:(c + 1) * CH, t, h * DV:(h + 1) * DV], True, True)
                last.then_inc(sem("gla_u"), 1)
            pe.wait_ge(sem("gla_scan"), NCH)
            for g in range(G):
                for r in range(R):
                    for j in range(TT):
                        n = (r * TT + j) * NCP
                        last = matmul(PS[:, 6 + g, n:n + NCP], Z[g * HD:(g + 1) * HD, ZQN + r, j * P:(j + 1) * P],
                                      kcTp[g * HD:(g + 1) * HD, :], True, True)
            last.then_inc(sem("nsa_cs"), 1)
            pe.wait_ge(sem("gla_scan"), 2 * NCH)
            pe.wait_ge(sem("s0_in"), 16)
            pe.wait_ge(sem("gla_q"), 5)
            for hp in range(2):
                pair = PS[:, 4, 2 * hp * LS:(2 * hp + 2) * LS].rearrange("p (l t) -> p l t", l=2)
                for lo in range(2):
                    h = 2 * hp + lo
                    matmul(pair[:, lo, :], VT[0:LS, TT, h * DV:(h + 1) * DV], ATTS[:, h, :], lo == 0, False, skip_group_check=True)
                for b in range(DB):
                    last = matmul(pair[:, :, b * DS:(b + 1) * DS], S0[:, hp, b, :], QB[:, hp, :, LP + b * DS:LP + (b + 1) * DS],
                                  False, b == DB - 1, skip_group_check=True)
            last.then_inc(sem("gla_os"), 1)

            def prompt_out(hp, half):
                for n in range(2):
                    t = 2 * half + n
                    pair = PS[:, 2 * hp + half, n * 2 * P:(n + 1) * 2 * P].rearrange("p (l i) -> p l i", l=2)
                    for lo in range(2):
                        h = 2 * hp + lo
                        matmul(pair[:, lo, :], VT[:, t, h * DV:(h + 1) * DV], ATT[:, h, t, :], lo == 0, False, skip_group_check=True)
                    for c in range(4):
                        cc = slice(t * P + c * CH, t * P + (c + 1) * CH)
                        last = matmul(pair[:, :, c * CH:(c + 1) * CH], SST[hp][:, t * 4 + c, :], QB[:, hp, :, cc],
                                      False, c == 3, skip_group_check=True)
                last.then_inc(sem("gla_o"), 1)

            def state_update(h):
                pe.wait_ge(sem("gla_vm"), h + 1)
                if h == 0:
                    pe.wait_ge(sem("nsa_cev"), 2)
                if h == 2:
                    pe.wait_ge(sem("gla_snew"), 1)
                for s in range(2):
                    last = matmul(PS[(h % 2) * DK:(h % 2 + 1) * DK, 6 + s, :], KE[0:LS, TT, h * DK:(h + 1) * DK],
                                  VMB[:, 4 * s:4 * s + 4, :], True, True)
                last.then_inc(sem("gla_us"), 1)

            def mean_square(h):
                pe.wait_ge(sem("gla_sq"), h + 1)
                if h == 1:
                    pe.wait_ge(sem("gla_snew"), 2)
                if h >= 2:
                    pe.wait_ge(sem("gla_ms_used"), h - 1)
                for n in range(2):
                    last = matmul(dense[h % 2][:, n, :], ones[:, :], SQG[:, h, n * HALF:(n + 1) * HALF], True, True)
                last.then_inc(sem("gla_ms"), 1)

            state_update(0)
            state_update(1)
            prompt_out(0, 0)
            prompt_out(0, 1)
            state_update(2)
            state_update(3)
            prompt_out(1, 0)
            mean_square(0)
            mean_square(1)
            prompt_out(1, 1)
            mean_square(2)
            mean_square(3)

            def segments(u):
                c, j = u // JP, u % JP
                for n in range(4):
                    last = nc.tensor.transpose(PS[:, u % 2, n * P:(n + 1) * P], CB[:, n % 2, 2 * j + n // 2, c, :], ident[:, :])
                last.then_inc(sem("seg_t"), 1)

            def compress(b, u, xt, n):
                c, j = u // JP, u % JP
                for m in range(2):
                    last = matmul(PS[:, 2 + c, 0:2 * n].rearrange("p (g n) -> p g n", g=2), W1[:, c, m, j, :],
                                  xt[:, u, :, m:m + n], j == 0 and m == 0, j == JP - 1 and m == 1)
                last.then_inc(sem("cmp_mm"), 1)

            pe.wait_ge(sem("nsa_cp"), 1)
            pe.wait_ge(sem("gla_cp"), 5)
            for h in range(G * R):
                if h >= 4:
                    pe.wait_ge(sem("nsa_cte"), h - 3)
                for j in range(TT):
                    n = (h * TT + j) * NCP
                    last = nc.tensor.transpose(PS[0:NCP, h % 4, j * P:(j + 1) * P], pc[:, n:n + NCP], ident[:, :])
                last.then_inc(sem("nsa_ct"), 1)

            def scores(i, t):
                j, g = t // 2 % TT, t % 2
                lo, w = g * HD, (j + 1) * P
                q = qcur[lo:lo + HD, t // 8, j * P:(j + 1) * P]
                if t >= 2:
                    pe.wait_ge(sem("nsa_exp"), i * 32 + 2 * (t - 1))
                matmul(PS[:, 2 * g, 0:w], q, Z[lo:lo + HD, ZKV + 2, 0:w], True, True)
                matmul(PS[:, 2 * g + 1, 0:w], q, Z[lo:lo + HD, ZKV + 4, 0:w], True, True).then_inc(sem("nsa_sc"), 1)

            def turned(i, t):
                j, pb = t // 2 % TT, PB[t % 3]
                for q in range(2):
                    pe.wait_ge(sem("nsa_p"), i * 32 + 2 * t + q + 1)
                    for k in range(j + 1):
                        last = nc.tensor.transpose(PS[:, 6 + q, k * P:(k + 1) * P],
                                                   pb[:, q * LP + k * P:q * LP + (k + 1) * P], ident[:, :])
                    last.then_inc(sem("nsa_pt"), 1)

            def values(i, t):
                j, g, pt = t // 2 % TT, t % 2, PTB[t % 2]
                pe.wait_ge(sem("nsa_ptev"), i * 32 + 2 * (t + 1))
                if t >= 2:
                    pe.wait_ge(sem("nsa_out"), i * 16 + t)
                o = PS[g * HD:(g + 1) * HD, 4 + g, 0:P]
                for q, c in ((0, 768 + P), (1, 1024 + P)):
                    for k in range(j + 1):
                        last = matmul(o, VT[:, k, c + g * HD:c + (g + 1) * HD], pt[:, (4 * q + k) * P:(4 * q + k + 1) * P],
                                      q == 0 and k == 0, q == 1 and k == j)
                last.then_inc(sem("nsa_pv"), 1)

            pe.wait_ge(sem("nsa_cte"), G * R)
            for r in range(R):
                for g in range(G):
                    last = matmul(PS[g * HD:(g + 1) * HD, r, :], vcp[:, g * HD:(g + 1) * HD], PCT[:, g * R + r, :], True, True)
                last.then_inc(sem("nsa_cv"), 1)
            pe.wait_ge(sem("nsa_co"), R)
            pe.wait_ge(sem("gla_ms_used"), GH)
            with pe.Fori(0, R // 2) as i:
                pe.wait_ge(sem("nsa_out"), i * 16 + 1)
                pe.wait_ge(sem("nsa_q"), i * 2 + 2)
                scores(i, 0)
                scores(i, 1)
                for t in range(16):
                    if t + 2 < 16:
                        scores(i, t + 2)
                    if t >= 1:
                        values(i, t - 1)
                    turned(i, t)
                values(i, 15)

            def seg_step(b, u):
                if u >= 2:
                    pe.wait_ge(sem("seg_ev"), b * 32 + 2 * u - 2)
                    pe.wait_ge(sem("seg_dve"), b * 32 + 2 * u - 2)
                segments(u)

            def cmp_step(b, u):
                pe.wait_ge(sem("seg_ev"), b * 32 + 2 * u + 2)
                pe.wait_ge(sem("seg_dve"), b * 32 + 2 * u + 2)
                compress(b, u, XTS, NCS)

            def tail(b):
                cols = [(C_WIN + t * P, P) for t in range(4)] + [(C_SLC + t * P, P) for t in range(SPAN)] + \
                       [(C_CMP, P), (C_CMP + P, NCS - P), (C_XW, DS), (C_XS, DS)]
                for n, (c, w) in enumerate(cols):
                    last = nc.tensor.transpose(PS[0:w, 4 + n // 16, (n % 16) * ROWS:(n % 16 + 1) * ROWS], PSC[:, c:c + w],
                                               ident[0:ROWS, 0:ROWS])
                    if n % 16 == 15 or n == NPT - 1:
                        last.then_inc(sem("pt_t"), 1)
                vals = [WBV[:, t, 1, :] for t in range(4)] + [SBV[:, t, 1, :] for t in range(SPAN)] + \
                       [vc[:, 0, :], vc[0:NCS - P, 1, :], VX[:, 0, :], VX[:, 1, :]]
                new_w, new_s = NPT - 2, NPT - 1
                branches = (list(range(4, 4 + SPAN)) + [new_s], [0, 1, 2, 3, new_w], [4 + SPAN, 5 + SPAN])
                for o, tiles_ in zip((1, 0, 2), branches):
                    for n in tiles_:
                        if o == 1 and n in (4, 16, 32):
                            pe.wait_ge(sem("pt_ev"), b * 3 + 1 + n // 16)
                        last = matmul(PS[0:ROWS, 7, o * P:(o + 1) * P], PTS[0:cols[n][1], n, :], vals[n],
                                      n == tiles_[0], n == tiles_[-1])
                last.then_inc(sem("pv_done"), 1)

            def turn(b):
                nc.tensor.transpose(PS[:, 7, 3 * P:3 * P + ROWS], osb, ident[0:ROWS, 0:ROWS]).then_inc(sem("o_t"), 1)

            def cmp_values(b):
                pe.wait_ge(sem("cmp_g"), b * 2 + 2)
                for g in range(G):
                    for s in range(2):
                        n = P if s == 0 else NCS - P
                        last = matmul(PS[0:n, 4, s * P + g * HD:s * P + (g + 1) * HD],
                                      hgx[:, g * NCS + s * P:g * NCS + s * P + n], w2[:, 1, :], True, True)
                last.then_inc(sem("cmp_v"), 1)

            def batch(b, waited):
                if not waited:
                    pe.wait_ge(sem("zs"), 6)
                pe.wait_ge(sem("cmp_in"), b * 16 + 16)
                seg_step(b, 0)
                seg_step(b, 1)
                if waited:
                    cmp_values(b - 1)
                if waited:
                    pe.wait_ge(sem("sc_ev"), b * 11)
                    pe.wait_ge(sem("vc_ev"), b)
                for u in range(16):
                    if u == 6 and waited:
                        pe.wait_ge(sem("sc_exp"), b * 6)
                    if u == 8 and waited:
                        pe.wait_ge(sem("o_rows"), b)
                    cmp_step(b, u)
                    if u + 2 < 16:
                        seg_step(b, u + 2)
                    if u == 6 and waited:
                        tail(b - 1)
                    if u == 8 and waited:
                        turn(b - 1)
                    if u == 11:
                        pe.wait_ge(sem("cmp_g"), b * 2 + 1)
                        for g in range(G):
                            last = matmul(PS[g * HD:(g + 1) * HD, 4, 0:NCS], w2[:, 0, :], hgx[:, g * NCS:(g + 1) * NCS], True, True)
                        last.then_inc(sem("cmp_k"), 1)
                    if u == 13:
                        pe.wait_ge(sem("cmp_kev"), b + 1)
                        pe.wait_ge(sem("batch_q"), b * 3 + 3)
                        matmul(PS[0:ROWS, 6, 0:NCS], qbd[:, :, :, :].rearrange("p g r q -> p (g r q)"), kcT[:, 0:NCS], True, True
                               ).then_inc(sem("sc_done"), 1)
                pe.wait_ge(sem("win_in"), b * 48 + 48)
                for n in range(9):
                    if n == 1:
                        pe.wait_ge(sem("slc_in"), b * 16 + 16)
                        pe.wait_ge(sem("pc_ready"), b + 1)
                    if n >= 3:
                        pe.wait_ge(sem("kt_ev"), b * 9 + n - 2)
                    for t in range(4):
                        src = SBV[:, 4 * n - 4 + t, 0, :] if n else WBV[:, t, 0, :]
                        last = nc.tensor.transpose(PS[:, kt_bank[n % 3], t * P:(t + 1) * P], src, ident[:, :])
                    last.then_inc(sem("kt_t"), 1)
                    if n == 1:
                        matmul(PS[0:ROWS, 5, 0:NCS], rsum[:, :], PSC[:, C_CMP:C_CMP + NCS], True, True).then_inc(sem("imp"), 1)
                q = qbd[:, :, :, :].rearrange("p g r q -> p (g r q)")
                pe.wait_ge(sem("cmp_hx"), b * 2 + 2)
                for n in range(10):
                    pe.wait_ge(sem("kt_ev"), b * 9 + max(n, 1))
                    if n >= 2:
                        pe.wait_ge(sem("sc_ev"), b * 11 + n)
                    if n == 0:
                        last = matmul(PS[0:ROWS, 2, 0:WIN], q, KTW, True, True)
                    elif n == 1:
                        last = matmul(PS[0:ROWS, 3, 0:2 * DS], q, knew[:, :, :].rearrange("p a q -> p (a q)"), True, True)
                    else:
                        last = matmul(PS[0:ROWS, 2 + n % 2, 0:512], q, KT[:, (n - 2) * 512:(n - 1) * 512], True, True)
                    last.then_inc(sem("sc_done"), 1)

            batch(0, False)
            with pe.Fori(1, DB) as b:
                batch(b, True)
            cmp_values(DB - 1)
            pe.wait_ge(sem("sc_ev"), 11 * DB)
            slot_ready(S_O, 0, 0)
            for f in range(2):
                for c in range(KD):
                    matmul(out_acc[f][:, 0, :], wslot[S_O % RING][:, c, f * P:(f + 1) * P], MIXT[:, c, 0:HALF], c == 0, c == KD - 1)
            pe.wait_ge(sem("sc_exp"), 6 * DB)
            tail(DB - 1)
            pe.wait_ge(sem("o_rows"), DB)
            turn(DB - 1)

            pe.wait_ge(sem("o_ev"), 2 * DB)
            for k in range(N_O):
                slot_ready(S_O, 0, k)
                for f in range(2):
                    n = 2 * k + f
                    pe.wait_ge(sem("res_free"), n + 1)
                    for c in range(KD):
                        for h in range(0 if k else 1, 2):
                            last = matmul(out_acc[n % 4][:, h, :], wslot[(S_O + k) % RING][:, c, f * P:(f + 1) * P],
                                          MIXT[:, c, h * HALF:(h + 1) * HALF], c == 0, c == KD - 1)
                    last.then_inc(sem("weights_used"), 1)
            pe.wait_ge(sem("x_res"), KD)
            sum_mean(1)
            first = N_ADA1 + N_IN
            for k in range(5):
                if k < 4:
                    slot_ready(S_ADA3 + k, 0, 0)
                    ada(S_ADA3 + k, first + k, 6)
                if k == 1:
                    ln_var(1)
                if k >= 1:
                    pe.wait_ge(sem("ada_row"), first + k)
                    ada_turn(first + k - 1, 0)
            pe.wait_ge(sem("ln_u"), 2 * (KD + 1))

            def ffn_in(i, slots):
                for k in slots:
                    slot_ready(S_F1, i, k)
                    for f in range(2):
                        pe.wait_ge(sem("h_ready" if f else "gate_free"), i * RING + k + (2 if f else 1))
                        project(lambda c: wslot1[(S_F1 + k) % RING][:, c, f, :], f, U).then_inc(sem("weights_used"), 1)
            full = N_F1 // RING
            with pe.Fori(0, full) as i:
                ffn_in(i, range(RING))
            ffn_in(full, range(N_F1 - full * RING))
            pe.wait_ge(sem("h_ready"), N_F1 + 2)
            with pe.Fori(0, N_F2 // RING) as i:
                for k in range(RING):
                    f = k // 2
                    slot_ready(S_F2, i, k)
                    if k % 2 == 0:
                        pe.wait_ge(sem("res_free"), i * 2 + KD + f + 3)
                    w = wslot2[(S_F2 + k) % RING]
                    for c in range(KF // 2):
                        h = (k % 2) * (KF // 2) + c
                        for n in range(2):
                            last = matmul(dense[f][:, n, :], w[:, c, :], HT[:, h, n * HALF:(n + 1) * HALF], h == 0, h == KF - 1)
                    last.then_inc(sem("weights_used"), 2)
            pe.wait_ge(sem("x_res"), 2 * KD)
            sum_mean(2)
            ln_var(2)

        @block.scalar
        def _(act):
            step = [0]

            def link(ins):
                step[0] += 1
                ins.then_inc(sem("act_step"), 1)
                act.wait_ge(sem("act_step"), step[0])

            def ln_act(nth, g, last=False):
                for k in range(KD):
                    act.wait_ge(sem("ln_cent"), nth * KD + k + 1)
                    nc.scalar.activation(SQ[:, k, :], XC[:, k, :], ACT.Square).then_inc(sem("ln_sq"), 1)
                act.wait_ge(sem("ln_rec"), nth + 1)
                nc.scalar.activation(rstd[:, :], rstd[:, :], ACT.Sqrt).then_inc(sem("ln_rstd"), 1)
                for k in range(KD):
                    act.wait_ge(sem("ln_h"), nth * KD + k + 1)
                    nc.scalar.activation(X[:, k, :], XC[:, k, :], ACT.Identity, bias=lnv[:, 2 * nth + 1, k:k + 1],
                                         scale=lnv[:, 2 * nth, k:k + 1]).then_inc(sem("ln_x"), 1)

            act.dma_start(cs[:], a["c_t"]).then_inc(sem("c_in"), 16)
            act.wait_ge(sem("c_in"), 16)
            nc.scalar.activation(cth[:, :, :], cs[:, :, :], ACT.Tanh, scale=0.5).then_inc(sem("c_tanh"), 1)
            act.wait_ge(sem("consts_in"), 128)
            ln_act(0, 0)

            def copy_tiles(i, n):
                for t in range(n):
                    act.wait_ge(sem("weights_used"), i * 16 + 2 * (S_IN + t // 2 * 2) + t % 2 + 1)
                    nc.scalar.activation(Z[:, bass.ds(i * 8 + t, 1), :].rearrange("p o (h t) -> p (o h) t", h=2), dense[t % 2], ACT.Copy).then_inc(sem("dense_free"), 1)
            with act.Fori(0, TURNS - 1) as i:
                copy_tiles(i, 8)
            copy_tiles(TURNS - 1, 6)
            act.wait_ge(sem("weights_used"), 2 * (S_IN + 2 * N_IN - 2) + 2)
            nc.scalar.activation(halves(zM[:, :]), dense[0][0:MISC], ACT.Copy).then_inc(sem("dense_free"), 1)

            for t in range(TT + 1):
                n = P if t < TT else LS
                bank = 4 * (t % 2)
                for q, w in ((0, 512), (1, 512), (2, 256)):
                    act.wait_ge(sem("rows_t"), 3 * t + q + 1)
                    if q == 2:
                        nc.scalar.activation(GT[0:n, t, :], PS[0:n, bank + 2, 256:256 + MISC], ACT.Copy).then_inc(sem("gt"), 1)
                    nc.scalar.activation(VT[0:n, t, q * 512:q * 512 + w], PS[0:n, bank + q, 0:w], ACT.Copy).then_inc(sem("rows_ready"), 1)
            act.wait_ge(sem("gt"), TT + 1)
            nc.scalar.activation(GT[:, 0:TT, RANK:MISC], GT[:, 0:TT, RANK:MISC], ACT.Tanh, scale=0.5).then_inc(sem("gates_tanh"), 1)
            nc.scalar.activation(GT[0:LS, TT, RANK:MISC], GT[0:LS, TT, RANK:MISC], ACT.Tanh, scale=0.5).then_inc(sem("gates_tanh"), 1)

            for h in range(2):
                act.wait_ge(sem("decay_x"), h + 1)
                link(nc.scalar.activation(halves(DM[:, h, :]), stat[h], ACT.Abs, bias=ba[:, h:h + 1]))
            link(nc.scalar.activation(DL[:, :, :], DM[:, :, :], ACT.Exp, scale=-1.0))
            nc.scalar.activation(DM[:, :, :], DL[:, :, :], ACT.Ln, bias=1.0).then_inc(sem("decay_ln"), 1)
            act.wait_ge(sem("gla_sums"), 5)
            for n, (src, s) in enumerate(((DM, 1.0), (DM, -1.0), (BC, 1.0), (DL, 1.0))):
                nc.scalar.activation(E[n][:, :, :], src[:, :, :], ACT.Exp, scale=s / TAU).then_inc(sem("gla_exp"), 1)
            act.wait_ge(sem("cbias"), 1)
            for c in range(2):
                act.wait_ge(sem("cmpp_mm"), c + 1)
                nc.scalar.activation(HX[:, c, :, :].rearrange("p g n -> p (g n)"), PS[:, 4 + c, 0:2 * NCP], ACT.Identity,
                                     bias=cbias[:, c:c + 1]).then_inc(sem("cmpp_hx"), 1)
            act.wait_ge(sem("cmpp_poly"), 1)
            nc.scalar.activation(HG, HG, ACT.Tanh, scale=GELU_A).then_inc(sem("cmpp_tanh"), 1)
            act.wait_ge(sem("gla_ket"), 1)
            for q in range(2):
                nc.scalar.activation(KE[:, 2 * q:2 * q + 2, :].rearrange("p t c -> p (t c)"), PS[:, 4 + q, :], ACT.Copy).then_inc(sem("gla_ke"), 1)
            nc.scalar.activation(KE[0:LS, TT, :], PS[0:LS, 6, 0:256], ACT.Copy).then_inc(sem("gla_ke"), 1)
            act.wait_ge(sem("gla_att"), 1)
            nc.scalar.activation(TH, Z[:, ZRG:ZRG + GH, :], ACT.Tanh, scale=0.5).then_inc(sem("gla_th"), 1)
            act.wait_ge(sem("nsa_cx"), 1)
            nc.scalar.activation(pc, pc, ACT.Exp).then_inc(sem("nsa_ce"), 1)
            act.wait_ge(sem("gla_os"), 1)
            nc.scalar.activation(MIXT[:, 0:GH, LP:NT], PS[:, 4, 0:GH * LS].rearrange("p (h t) -> p h t", h=GH), ACT.Copy).then_inc(sem("gla_cp"), 1)
            for hp in range(2):
                for half in range(2):
                    act.wait_ge(sem("gla_o"), 2 * hp + half + 1)
                    nc.scalar.activation(MIXT[:, 2 * hp:2 * hp + 2, half * 2 * P:(half + 1) * 2 * P].rearrange("p l (n i) -> p l n i", n=2),
                                         PS[:, 2 * hp + half, :].rearrange("p (n l i) -> p l n i", n=2, l=2), ACT.Copy).then_inc(sem("gla_cp"), 1)
                act.wait_ge(sem("gla_cp"), 2 * hp + 3)
                for h in (2 * hp, 2 * hp + 1):
                    nc.scalar.activation(SQG[:, h, :], MIXT[:, h, :], ACT.Square).then_inc(sem("gla_sq"), 1)

            def rms(h):
                act.wait_ge(sem("gla_rec"), h + 1)
                nc.scalar.activation(SQG[:, h, :], SQG[:, h, :], ACT.Sqrt).then_inc(sem("gla_rstd"), 1)

            rms(0)
            rms(1)
            for h in range(G * R):
                act.wait_ge(sem("nsa_ct"), h + 1)
                nc.scalar.activation(PCT[:, h, :], PS[0:NCP, h % 4, :], ACT.Copy).then_inc(sem("nsa_cte"), 1)
                if h == 3:
                    rms(2)
            rms(3)

            for r in range(R):
                act.wait_ge(sem("nsa_cv"), r + 1)
                nc.scalar.activation(MIXT[:, 4 + r, 0:LP], PS[:, r, :], ACT.Copy).then_inc(sem("nsa_co"), 1)

            def exponentials(i, t):
                j, g = t // 2 % TT, t % 2
                w = (j + 1) * P
                if t >= 3:
                    act.wait_ge(sem("nsa_pt"), i * 32 + 2 * (t - 2))
                act.wait_ge(sem("nsa_max"), i * 16 + t + 1)
                for q in range(2):
                    nc.scalar.activation(PB[t % 3][:, q * LP:q * LP + w], PS[:, 2 * g + q, 0:w], ACT.Exp, scale=HD ** -0.5,
                                         bias=pst[:, g, 1, q:q + 1], accum_out=pst[:, g, 2, q:q + 1]).then_inc(sem("nsa_exp"), 1)

            with act.Fori(0, R // 2) as i:
                act.wait_ge(sem("nsa_out"), i * 16 + 1)
                for h in range(2):
                    nc.scalar.activation(qcur[:, h, :], Z[:, bass.ds(i * 2 + ZQN + h, 1), 0:LP].rearrange("p o t -> p (o t)"),
                                         ACT.Copy).then_inc(sem("nsa_q"), 1)
                exponentials(i, 0)
                for t in range(16):
                    if t + 1 < 16:
                        exponentials(i, t + 1)
                    w = (t // 2 % TT + 1) * P
                    pt = PTB[t % 2]
                    if t >= 2:
                        act.wait_ge(sem("nsa_pv"), i * 16 + t - 1)
                    for q in range(2):
                        act.wait_ge(sem("nsa_pt"), i * 32 + 2 * t + 1 + q)
                        nc.scalar.activation(pt[:, 4 * q * P:4 * q * P + w], PS[:, 6 + q, 0:w], ACT.Copy).then_inc(sem("nsa_ptev"), 1)

            def exp_part(b, q):
                if q == 0:
                    act.wait_ge(sem("sc_max"), b * 3 + 3)
                v = PSC[:, C_XS + q * PART:C_XS + (q + 1) * PART]
                nc.scalar.activation(v, v, ACT.Exp, bias=smx[:, 1, 1:2], accum_out=pmx[:, 1, q:q + 1]).then_inc(sem("sc_exp"), 1)

            def seg_copy(b, u):
                act.wait_ge(sem("seg_t"), b * 16 + u + 1)
                for h in range(2):
                    nc.scalar.activation(seg_dst(u, h, 0), seg_src(u, h, 0), ACT.Copy).then_inc(sem("seg_ev"), 1)

            def batch(b, waited):
                seg_copy(b, 0)
                if waited:
                    act.wait_ge(sem("sc_done"), b * 11)
                for g in range(G):
                    nc.scalar.activation(qbd[g * HD:(g + 1) * HD, g, :, :], zS[g * HD:(g + 1) * HD, 0:R, bass.ds(b * DS, DS)],
                                         ACT.Copy).then_inc(sem("batch_q"), 1)
                nc.scalar.activation(knew[:, :, :], zS[:, 4:6, bass.ds(b * DS, DS)], ACT.Copy).then_inc(sem("batch_q"), 1)
                for u in range(1, 10):
                    seg_copy(b, u)
                    if waited and u in (4, 5):
                        exp_part(b - 1, 2 * (u - 4))
                        exp_part(b - 1, 2 * (u - 4) + 1)
                act.wait_ge(sem("cmp_mm"), b * 16 + 8)
                if waited:
                    act.wait_ge(sem("cmp_g"), b * 2)
                nc.scalar.activation(HXS[:, :], PS[:, 2, 0:2 * NCS], ACT.Identity, bias=cbias[:, 0:1]).then_inc(sem("cmp_hx"), 1)
                seg_copy(b, 10)
                seg_copy(b, 11)
                act.wait_ge(sem("cmp_poly"), b * 2 + 1)
                nc.scalar.activation(hgx[:, :], hgx[:, :], ACT.Tanh, scale=GELU_A).then_inc(sem("cmp_tanh"), 1)
                seg_copy(b, 12)
                seg_copy(b, 13)
                act.wait_ge(sem("cmp_k"), b + 1)
                nc.scalar.activation(kcT[:, 0:NCS], PS[:, 4, 0:NCS], ACT.Copy, scale=0.5).then_inc(sem("cmp_kev"), 1)
                seg_copy(b, 14)
                seg_copy(b, 15)
                act.wait_ge(sem("sc_max"), b * 3 + 1)
                nc.scalar.activation(PSC[:, C_CMP:C_CMP + NCS], PSC[:, C_CMP:C_CMP + NCS], ACT.Exp, bias=smx[:, 1, 2:3],
                                     accum_out=smx[:, 2, 2:3]).then_inc(sem("sc_exp"), 1)
                act.wait_ge(sem("cmp_mm"), b * 16 + 16)
                nc.scalar.activation(HXS[:, :], PS[:, 3, 0:2 * NCS], ACT.Identity, bias=cbias[:, 1:2]).then_inc(sem("cmp_hx"), 1)
                for n in range(9):
                    act.wait_ge(sem("kt_t"), b * 9 + n + 1)
                    dst = KT[:, (n - 1) * 512:n * 512] if n else KTW
                    nc.scalar.activation(dst, PS[:, kt_bank[n % 3], :], ACT.Copy).then_inc(sem("kt_ev"), 1)
                act.wait_ge(sem("cmp_poly"), b * 2 + 2)
                nc.scalar.activation(hgx[:, :], hgx[:, :], ACT.Tanh, scale=GELU_A).then_inc(sem("cmp_tanh"), 1)
                act.wait_ge(sem("sc_max"), b * 3 + 2)
                v = PSC[:, C_WIN:C_WIN + WIN + DS]
                nc.scalar.activation(v, v, ACT.Exp, bias=smx[:, 1, 0:1], accum_out=smx[:, 2, 0:1]).then_inc(sem("sc_exp"), 1)

            act.wait_ge(sem("zs"), 6)
            batch(0, False)
            with act.Fori(1, DB) as b:
                batch(b, True)
            for q in range(4):
                exp_part(DB - 1, q)

            for k in range(KD):
                nc.scalar.activation(X[:, k, :], X[:, k, :], ACT.Copy, scale=ALPHA).then_inc(sem("x_alpha"), 1)
            ln_act(1, 2)
            act.wait_ge(sem("ln_u"), 2 * (KD + 1))
            for k in range(KD):
                nc.scalar.activation(X[:, k, :], X[:, k, :], ACT.Copy, scale=ALPHA).then_inc(sem("x_alpha"), 1)

            def gate(i, n):
                for k in range(n):
                    act.wait_ge(sem("weights_used"), i * 8 + 2 * S_F1 + 2 * k + 1)
                    act.wait_ge(sem("h_ready"), i * RING + k + 1)
                    nc.scalar.activation(halves(SQ[:, k % 2, :]), dense[0], ACT.Tanh, scale=0.5).then_inc(sem("gate_th"), 1)
            full = N_F1 // RING
            with act.Fori(0, full) as i:
                gate(i, RING)
            gate(full, N_F1 - full * RING)
            ln_act(2, 4)

        @block.vector
        def _(dve):
            step = [0]

            def link(ins):
                step[0] += 1
                ins.then_inc(sem("dve_step"), 1)
                dve.wait_ge(sem("dve_step"), step[0])

            def ada_row(a_, n, bank, i=0):
                dve.wait_ge(sem("weights_used"), i * 16 + 2 * n + 2)
                if a_ >= 2 or not isinstance(i, int):
                    dve.wait_ge(sem("ada_t"), i * 4 + a_ - 1)
                nc.vector.tensor_copy(ada_rows[a_ % 2], PS[0:NC, bank + a_ % 2, 0:2 * P]).then_inc(sem("ada_row"), 1)

            def ln_dve(nth, chunk, between=None):
                dve.wait_ge(sem("ln_mean"), nth + 1)
                for k in range(KD):
                    nc.vector.tensor_tensor(halves(XC[:, k, :]), halves(X[:, k, :]), stat[0], ALU.subtract).then_inc(sem("ln_cent"), 1)
                if between:
                    between(0)
                    between(1)
                dve.wait_ge(sem("ln_var"), nth + 1)
                link(nc.vector.tensor_scalar(halves(rstd[:, :]), stat[1], 1e-5, None, ALU.add))
                nc.vector.reciprocal(rstd[:, :], rstd[:, :]).then_inc(sem("ln_rec"), 1)
                if between:
                    between(2)
                dve.wait_ge(sem("ln_rstd"), nth + 1)
                for k in range(KD):
                    nc.vector.tensor_tensor(XC[:, k, :], XC[:, k, :], rstd[:, :], ALU.mult).then_inc(sem("ln_h"), 1)
                if between:
                    between(3)
                if chunk is None:
                    return
                for k in range(KD):
                    dve.wait_ge(sem("ln_x"), nth * KD + k + 1)
                    nc.vector.tensor_scalar(U[:, k, 0:LP], X[:, k, 0:LP], mod[:, chunk + 1, k, 0:1], mod[:, chunk, k, 0:1],
                                            ALU.mult, ALU.add).then_inc(sem("ln_u"), 1)
                us = U[:, :, LP:NT].rearrange("p k (b q) -> p k b q", q=DS)
                xs = X[:, :, LP:NT].rearrange("p k (b q) -> p k b q", q=DS)
                shp = [P, KD, DB, DS]
                link(nc.vector.tensor_tensor(us, xs, mod[:, chunk + 1, :, 1:NC].unsqueeze(3).to_broadcast(shp), ALU.mult))
                nc.vector.tensor_tensor(us, us, mod[:, chunk, :, 1:NC].unsqueeze(3).to_broadcast(shp), ALU.add).then_inc(sem("ln_u"), 1)

            def mod_copy(i, t, c, bank):
                dve.wait_ge(sem("ada_t"), i * 4 + t)
                nc.vector.tensor_tensor(mod[:, bass.ds(c, 1), :, :].rearrange("p o k c -> p (o k) c"), pmods(bank),
                                        bada[:, bass.ds(c, 1), :].rearrange("p o k -> p (o k)").unsqueeze(2).to_broadcast([P, KD, NC]),
                                        ALU.add).then_inc(sem("mod_free"), 1)

            dve.sem_inc(sem("mod_free"), 1)
            dve.sem_inc(sem("dense_free"), 2)
            dve.wait_ge(sem("c_tanh"), 1)
            link(nc.vector.scalar_tensor_tensor(out=cth[:, :, :], in0=cth[:, :, :], scalar=1.0, in1=cs[:, :, :], op0=ALU.add, op1=ALU.mult))
            nc.vector.tensor_scalar(cs[:, :, :], cth[:, :, :], 0.5, None, ALU.mult).then_inc(sem("silu_c"), 1)
            dve.wait_ge(sem("ln_mean"), 1)
            for k in range(KD):
                nc.vector.tensor_tensor(halves(XC[:, k, :]), halves(X[:, k, :]), stat[0], ALU.subtract).then_inc(sem("ln_cent"), 1)
            ada_row(0, 0, 6)
            ada_row(1, 1, 6)
            dve.wait_ge(sem("ln_var"), 1)
            link(nc.vector.tensor_scalar(halves(rstd[:, :]), stat[1], 1e-5, None, ALU.add))
            nc.vector.reciprocal(rstd[:, :], rstd[:, :]).then_inc(sem("ln_rec"), 1)
            ada_row(2, 2, 6)
            dve.wait_ge(sem("ln_rstd"), 1)
            for k in range(KD):
                nc.vector.tensor_tensor(XC[:, k, :], XC[:, k, :], rstd[:, :], ALU.mult).then_inc(sem("ln_h"), 1)
            for k in range(3, N_ADA1):
                ada_row(k, k, 6)
                if k == 5:
                    mod_copy(0, 4, 0, 4)
            mod_copy(0, 8, 1, 5)
            dve.wait_ge(sem("mod_free"), 3)
            link(nc.vector.tensor_scalar(mod[:, 1, :, :], mod[:, 1, :, :], 1.0, None, ALU.add))
            for k in range(KD):
                dve.wait_ge(sem("ln_x"), k + 1)
                nc.vector.tensor_scalar(U[:, k, 0:LP], X[:, k, 0:LP], mod[:, 1, k, 0:1], mod[:, 0, k, 0:1],
                                        ALU.mult, ALU.add).then_inc(sem("ln_u"), 1)
            us = U[:, :, LP:NT].rearrange("p k (b q) -> p k b q", q=DS)
            xs = X[:, :, LP:NT].rearrange("p k (b q) -> p k b q", q=DS)
            shp = [P, KD, DB, DS]
            link(nc.vector.tensor_tensor(us, xs, mod[:, 1, :, 1:NC].unsqueeze(3).to_broadcast(shp), ALU.mult))
            nc.vector.tensor_tensor(us, us, mod[:, 0, :, 1:NC].unsqueeze(3).to_broadcast(shp), ALU.add).then_inc(sem("ln_u"), 1)

            dve.wait_ge(sem("pidx"), 1)
            dve.wait_ge(sem("ptab_in"), 16)
            link(nc.vector.tensor_single_scalar(pmod[:, :], pidx[:, :], 3, op=ALU.bitwise_and))
            link(nc.vector.tensor_copy(pmodf[:, :], pmod[:, :]))
            nc.vector.tensor_scalar(idx[:, :], ptab[:, :], 4.0, None, ALU.mult).then_inc(sem("idx4"), 1)
            dve.wait_ge(sem("idx4"), 1)
            nc.vector.tensor_scalar(idx[:, :], idx[:, :], pmodf[:, 0:1], None, ALU.add).then_inc(sem("idx"), 1)
            dve.wait_ge(sem("pool_consts"), 1)
            for q in range(DS):
                link(nc.vector.tensor_scalar(smx[:, 0, 0:1], pmodf[0:ROWS, 0:1], float(q), NEG, ALU.is_ge, ALU.mult))
                link(nc.vector.tensor_copy(wpen[:, q * P:q * P + 1], smx[:, 0, 0:1]))
                link(nc.vector.tensor_scalar(smx[:, 0, 1:2], pmodf[0:ROWS, 0:1], float(q), NEG, ALU.is_lt, ALU.mult))
                link(nc.vector.tensor_copy(wpen[:, WIN + q:WIN + q + 1], smx[:, 0, 1:2]))
                link(nc.vector.tensor_copy(wpen[:, WIN + DS + q:WIN + DS + q + 1], smx[:, 0, 1:2]))
            link(nc.vector.tensor_copy(VMB[:, :, 0:DS], bmask[:, :].unsqueeze(2).to_broadcast([LS, DB, DS])))
            link(nc.vector.tensor_tensor(smask[:, :].rearrange("p (b q) -> p b q", q=DS), smask[:, :].rearrange("p (b q) -> p b q", q=DS),
                                         VMB[:, :, 0:DS], ALU.mult))

            def turn_rows(i):
                for k in range(4):
                    ada_row(N_ADA1 + k, S_IN + 2 * k + 1, 0, i)
                mod_copy(i, N_ADA1 + 4, i + 2, 2)
            with dve.Fori(0, TURNS - 1) as i:
                turn_rows(i)
            turn_rows(TURNS - 1)
            dve.wait_ge(sem("mod_free"), 6)
            link(nc.vector.tensor_scalar(mod[:, 4, :, :], mod[:, 4, :, :], 1.0, None, ALU.add))

            dve.wait_ge(sem("dense_free"), ZT + 3)
            for c in range(2):
                for h in range(2):
                    for g in range(G):
                        nc.vector.tensor_copy(XTP[h * HD:(h + 1) * HD, c * JP:(c + 1) * JP, g, :],
                                              Z[g * HD:(g + 1) * HD, ZKV + c, 0:LP].rearrange("p (n j h) -> p h j n", j=JP, h=2)[:, h]
                                              ).then_inc(sem("xtp"), 1)

            dve.wait_ge(sem("gates_tanh"), 2)
            link(nc.vector.tensor_scalar(GT[:, 0:TT, RANK:MISC], GT[:, 0:TT, RANK:MISC], 0.5, 0.5, ALU.mult, ALU.add))
            nc.vector.tensor_scalar(GT[0:LS, TT, RANK:MISC], GT[0:LS, TT, RANK:MISC], 0.5, 0.5, ALU.mult, ALU.add).then_inc(sem("gates_ready"), 1)
            dve.wait_ge(sem("pe_bias"), 1)
            nc.vector.tensor_copy(bias_row, PS[0:1, 6, 0:2 * HID]).then_inc(sem("pe_row"), 1)

            dve.wait_ge(sem("rows_ready"), 3 * (TT + 1))
            nc.vector.memset(QB[0:DK, :, 1, :], 0.0)
            nc.vector.memset(QB[DK:P, :, 0, :], 0.0)
            dve.wait_ge(sem("pe_bias"), 2)
            nc.vector.tensor_tensor(cbias[:, :], PS[:, 6, 256:258], cb1[:, :], ALU.add).then_inc(sem("cbias"), 1)
            dve.wait_ge(sem("decay_ln"), 1)
            for h in range(2):
                link(nc.vector.tensor_scalar(halves(LA[:, h, :]), stat[h], ba[:, h:h + 1], 0.0, ALU.add, ALU.min))
            link(nc.vector.tensor_tensor(LA[:, :, :], LA[:, :, :], DM[:, :, :], ALU.subtract))
            dve.wait_ge(sem("rmask"), 2)
            for h in range(2):
                link(nc.vector.tensor_tensor_scan(BC[:, h, :], rmask, LA[:, h, :], 0.0, ALU.mult, ALU.add))
            nc.vector.memset(S0P[:, 0, :], 0.0).then_inc(sem("gla_sums"), 1)
            nc.vector.memset(S1[:, 0, :], 0.0)
            for lo, hi, n, w in ((0, LP, NCH, CH), (LP, NT, DB, DS)):
                b4 = BC[:, :, lo:hi].rearrange("p h (c i) -> p h c i", i=w)
                shp4 = [P, 2, n, w]
                nc.vector.tensor_tensor(DM[:, :, lo:hi].rearrange("p h (c i) -> p h c i", i=w), b4,
                                        b4[:, :, :, w // 2 - 1:w // 2].to_broadcast(shp4), ALU.subtract).then_inc(sem("gla_sums"), 1)
                nc.vector.tensor_tensor(DL[:, :, lo:hi].rearrange("p h (c i) -> p h c i", i=w),
                                        b4[:, :, :, w - 1:w].to_broadcast(shp4), b4, ALU.subtract).then_inc(sem("gla_sums"), 1)
            dve.wait_ge(sem("gla_exp"), 4)
            dec = gdec[:, :, 0:NCH]
            decs = gdec[:, :, NCH:NCH + DB]
            nc.vector.tensor_copy(dec, E[2][:, :, CH - 1:LP:CH]).then_inc(sem("gla_dec"), 1)
            nc.vector.tensor_copy(decs, E[2][:, :, LP + DS - 1:NT:DS]).then_inc(sem("gla_dec"), 1)
            dve.wait_ge(sem("gla_dec"), 2)
            for n, z in ((0, ZQG), (1, ZKG), (3, ZKG)):
                nc.vector.scalar_tensor_tensor(out=E[n][:, :, :], in0=E[n][:, :, :], scalar=DK ** -0.5 if z == ZQG else 1.0,
                                               in1=Z[:, z:z + 2, :], op0=ALU.mult, op1=ALU.mult).then_inc(sem("gla_q"), 1)
            for lo in range(2):
                rows = slice(lo * DK, (lo + 1) * DK)
                nc.vector.scalar_tensor_tensor(out=QB[rows, :, lo, :], in0=E[2][rows, :, :], scalar=DK ** -0.5,
                                               in1=Z[rows, ZQG:ZQG + 2, :], op0=ALU.mult, op1=ALU.mult).then_inc(sem("gla_q"), 1)
            nc.vector.memset(ATT, 0.0).then_inc(sem("att_zero"), 1)
            dve.wait_ge(sem("cmpp_hx"), 2)
            link(nc.vector.tensor_tensor(HG, HX, HX, ALU.mult))
            link(nc.vector.tensor_scalar(HG, HG, GELU_C, 1.0, ALU.mult, ALU.add))
            nc.vector.tensor_tensor(HG, HG, HX, ALU.mult).then_inc(sem("cmpp_poly"), 1)
            dve.wait_ge(sem("cmpp_tanh"), 1)
            nc.vector.scalar_tensor_tensor(out=HG.rearrange("p c g n -> p (c g n)"), in0=HG.rearrange("p c g n -> p (c g n)"), scalar=1.0,
                                           in1=HX.rearrange("p c g n -> p (c g n)"), op0=ALU.add, op1=ALU.mult).then_inc(sem("cmpp_g"), 2)
            dve.wait_ge(sem("gla_att"), 1)
            dve.wait_ge(sem("att_zero"), 1)
            for h2 in range(2):
                for c in range(4):
                    rows = slice(c * CH, (c + 1) * CH)
                    nc.vector.tensor_tensor(
                        RR[rows, 2 * GW:2 * GW + 16 * P].rearrange("p (a b t i) -> p a b t i", a=2, b=2, t=TT)[:, :, h2, :, rows],
                        PS[rows, h2, 0:256].rearrange("p (a t i) -> p a t i", a=2, t=TT),
                        gmask[rows, :].unsqueeze(1).unsqueeze(1).to_broadcast([CH, 2, TT, CH]), ALU.mult).then_inc(sem("gla_attm"), 1)
                nc.vector.tensor_tensor(ATTS.rearrange("p (a b) i -> p a b i", b=2)[:, :, h2, :],
                                        PS[0:LS, h2, 256:256 + 2 * LS].rearrange("p (a i) -> p a i", a=2),
                                        smask[:, :].unsqueeze(1).to_broadcast([LS, 2, LS]), ALU.mult).then_inc(sem("gla_attm"), 1)
            dve.wait_ge(sem("cmpp_kv"), 1)
            nc.vector.tensor_scalar(kcTp, PS[:, 7, 0:NCP], 0.5, None, ALU.mult).then_inc(sem("cmpp_ev"), 1)
            nc.vector.tensor_scalar(vcp, PS[0:NCP, 7, P:2 * P], 0.5, None, ALU.mult).then_inc(sem("cmpp_ev"), 1)
            for h in range(2):
                dve.wait_ge(sem("gla_u"), h + 1)
                for c in range(NCH):
                    nc.vector.scalar_tensor_tensor(out=SST[h][:, c + 1, :], in0=SST[h][:, c, :], scalar=dec[:, h, c:c + 1],
                                                   in1=PS[:, 4 - 4 * h + c % 4, (c // 4) * P:(c // 4 + 1) * P],
                                                   op0=ALU.mult, op1=ALU.add).then_inc(sem("gla_scan"), 1)
                    dve.wait_ge(sem("gla_scan"), h * NCH + c + 1)
            dve.wait_ge(sem("pcp"), 1)
            dve.wait_ge(sem("nsa_cs"), 1)
            by_tile = pc.rearrange("p (c n) -> p c n", n=NCP)
            tiles_ = [P, G * R * TT, NCP]
            for g in range(G):
                nc.vector.scalar_tensor_tensor(
                    out=pc[:, g * PCW:(g + 1) * PCW].rearrange("p (r n) -> p r n", r=R), in0=PS[:, 6 + g, 0:PCW].rearrange("p (r n) -> p r n", r=R),
                    scalar=HD ** -0.5, in1=pcp.rearrange("p t n -> p (t n)").unsqueeze(1).to_broadcast([P, R, TT * NCP]),
                    op0=ALU.mult, op1=ALU.add).then_inc(sem("nsa_cev"), 1)
            dve.wait_ge(sem("nsa_cev"), 2)
            link(nc.vector.tensor_reduce(pcst[:, 0, :], by_tile, AX.X, ALU.max))
            link(nc.vector.tensor_scalar(pcst[:, 0, :], pcst[:, 0, :], 0.9 * NEG, None, ALU.max))
            nc.vector.tensor_tensor(by_tile, by_tile, pcst[:, 0, :].unsqueeze(2).to_broadcast(tiles_), ALU.subtract).then_inc(sem("nsa_cx"), 1)
            for h in range(GH):
                if h >= 1:
                    dve.wait_ge(sem("gla_us"), h)
                nc.vector.tensor_tensor(VMB, VT[0:LS, TT, h * DV:(h + 1) * DV].unsqueeze(1).to_broadcast([LS, DB, DV]),
                                        bmask[:, :].unsqueeze(2).to_broadcast([LS, DB, DV]), ALU.mult).then_inc(sem("gla_vm"), 1)
                if h % 2 == 1:
                    dve.wait_ge(sem("gla_us"), h + 1)
                    dve.wait_ge(sem("gla_os"), 1)
                    hp = h // 2
                    for b in range(DB):
                        last = nc.vector.scalar_tensor_tensor(out=S0[:, hp, b, :], in0=S0[:, hp, b, :], scalar=decs[:, hp, b:b + 1],
                                                              in1=PS[:, 6 + b // 4, (b % 4) * P:(b % 4 + 1) * P], op0=ALU.mult, op1=ALU.add)
                    last.then_inc(sem("gla_snew"), 1)
            dve.wait_ge(sem("gla_th"), 1)
            link(nc.vector.scalar_tensor_tensor(out=TH, in0=TH, scalar=1.0, in1=Z[:, ZRG:ZRG + GH, :], op0=ALU.add, op1=ALU.mult))
            dve.wait_ge(sem("nsa_ce"), 1)
            link(nc.vector.tensor_reduce(pcst[:, 1, :], by_tile, AX.X, ALU.add))
            link(nc.vector.tensor_scalar(pcst[:, 1, :], pcst[:, 1, :], 1e-30, None, ALU.max))
            link(nc.vector.reciprocal(pcst[:, 1, :], pcst[:, 1, :]))
            for g in range(G):
                n = slice(g * R * TT, (g + 1) * R * TT)
                gate_c = GT[:, 0:TT, RANK:MISC].rearrange("p t (r c) -> p r t c", r=R)[:, :, :, 3 * g:3 * g + 1].rearrange("p r t o -> p r (t o)")
                link(nc.vector.tensor_tensor(pcst[:, 2, n].rearrange("p (r t) -> p r t", r=R), pcst[:, 1, n].rearrange("p (r t) -> p r t", r=R),
                                             gate_c, ALU.mult))
            nc.vector.tensor_tensor(by_tile, by_tile, pcst[:, 2, :].unsqueeze(2).to_broadcast(tiles_), ALU.mult).then_inc(sem("nsa_cp"), 1)

            def scale_output(h):
                dve.wait_ge(sem("gla_rstd"), h + 1)
                link(nc.vector.scalar_tensor_tensor(out=MIXT[:, h, :], in0=MIXT[:, h, :], scalar=gng[:, 0:1], in1=SQG[:, h, :], op0=ALU.mult, op1=ALU.mult))
                nc.vector.scalar_tensor_tensor(out=MIXT[:, h, :], in0=MIXT[:, h, :], scalar=0.5, in1=TH[:, h, :], op0=ALU.mult, op1=ALU.mult).then_inc(sem("gla_done"), 1)

            for h in range(GH):
                dve.wait_ge(sem("gla_ms"), h + 1)
                nc.vector.tensor_scalar(halves(SQG[:, h, :]), dense[h % 2], float(D // DV), 1e-6, ALU.mult, ALU.add).then_inc(sem("gla_ms_used"), 1)
                dve.wait_ge(sem("gla_ms_used"), h + 1)
                nc.vector.reciprocal(SQG[:, h, :], SQG[:, h, :]).then_inc(sem("gla_rec"), 1)
                if h >= 1:
                    scale_output(h - 1)
            scale_output(GH - 1)


            dve.wait_ge(sem("gla_out"), 64)

            dve.wait_ge(sem("nsa_co"), R)
            dve.sem_inc(sem("nsa_out"), 1)
            base = step[0]
            PER = 2 + 16 * 5
            with dve.Fori(0, R // 2) as i:
                count = [0]

                def lk(ins):
                    count[0] += 1
                    ins.then_inc(sem("dve_step"), 1)
                    dve.wait_ge(sem("dve_step"), i * PER + base + count[0])
                for h in range(2):
                    lk(nc.vector.tensor_copy(gpc[:, h, :, :], GT[:, 0:TT, bass.ds(i * 12 + RANK + 6 * h, 6)]))

                def prepare(t):
                    j, g = t // 2 % TT, t % 2
                    w = (j + 1) * P
                    st = pst[:, g]
                    dve.wait_ge(sem("nsa_sc"), i * 16 + t + 1)
                    diag = PS[:, 2 * g:2 * g + 2, w - P:w]
                    lk(nc.vector.tensor_tensor(diag, diag, pen[:, LP - P:LP].unsqueeze(1).to_broadcast([P, 2, P]), ALU.add))
                    lk(nc.vector.tensor_reduce(st[:, 0, :], PS[:, 2 * g:2 * g + 2, 0:w], AX.X, ALU.max))
                    nc.vector.tensor_scalar(st[:, 1, :], st[:, 0, :], -HD ** -0.5, None, ALU.mult).then_inc(sem("nsa_max"), 1)

                def finish(t):
                    j, g = t // 2 % TT, t % 2
                    w = (j + 1) * P
                    st = pst[:, g]
                    dve.wait_ge(sem("nsa_exp"), i * 32 + 2 * (t + 1))
                    lk(nc.vector.tensor_scalar(st[:, 2, :], st[:, 2, :], 1e-30, None, ALU.max))
                    lk(nc.vector.reciprocal(st[:, 2, :], st[:, 2, :]))
                    lk(nc.vector.tensor_tensor(st[:, 3, :], st[:, 2, :], gpc[:, t // 8, j, g * 3 + 1:g * 3 + 3], ALU.mult))
                    for q in range(2):
                        v = PB[t % 3][:, q * LP:q * LP + w]
                        nc.vector.tensor_scalar(v, v, st[:, 3, q:q + 1], None, ALU.mult).then_inc(sem("nsa_p"), 1)

                def output(t):
                    j, g = t // 2 % TT, t % 2
                    dve.wait_ge(sem("nsa_pv"), i * 16 + t + 1)
                    o = MIXT[g * HD:(g + 1) * HD, bass.ds(i * 2 + 4 + t // 8, 1), j * P:(j + 1) * P].rearrange("p o t -> p (o t)")
                    nc.vector.tensor_tensor(o, o, PS[g * HD:(g + 1) * HD, 4 + g, 0:P], ALU.add).then_inc(sem("nsa_out"), 1)

                prepare(0)
                for t in range(16):
                    if t + 1 < 16:
                        prepare(t + 1)
                    finish(t)
                    if t >= 2:
                        output(t - 2)
                output(14)
                output(15)
                assert count[0] == PER, count[0]
            step[0] += PER * (R // 2)
            dve.wait_ge(sem("nsa_out"), 8 * R + 1)
            for r in range(R):
                nc.vector.tensor_scalar(zS[:, r, :], Z[:, ZQN + r, LP:NT], HD ** -0.5, None, ALU.mult).then_inc(sem("zs"), 1)
            nc.vector.tensor_copy(zS[:, 4, :], Z[:, ZKV + 4, LP:NT]).then_inc(sem("zs"), 1)
            nc.vector.tensor_copy(zS[:, 5, :], Z[:, ZKV + 2, LP:NT]).then_inc(sem("zs"), 1)
            dve.wait_ge(sem("zs"), 6)

            sbase = step[0]
            SPER, TPER = 16, 11

            def tlk(b, n, ins):
                ins.then_inc(sem("tail_step"), 1)
                dve.wait_ge(sem("tail_step"), b * TPER + n)

            def value_rows(b):
                dve.wait_ge(sem("cmp_v"), b + 1)
                nc.vector.tensor_scalar(vc[:, 0, :], PS[:, 4, 0:P], 0.5, None, ALU.mult)
                nc.vector.tensor_scalar(vc[0:NCS - P, 1, :], PS[0:NCS - P, 4, P:2 * P], 0.5, None, ALU.mult).then_inc(sem("vc_ev"), 1)

            def max_part(b, q):
                tlk(b, q + 1, nc.vector.tensor_reduce(pmx[:, 0, q:q + 1], PSC[:, C_XS + q * PART:C_XS + (q + 1) * PART], AX.X, ALU.max))
                if q == 3:
                    tlk(b, 5, nc.vector.tensor_reduce(smx[:, 0, 1:2], pmx[:, 0, :], AX.X, ALU.max))
                    nc.vector.tensor_scalar(smx[:, 1, 1:2], smx[:, 0, 1:2], -1.0, None, ALU.mult).then_inc(sem("sc_max"), 1)

            def tail(b):
                for q in range(3):
                    dve.wait_ge(sem("pt_t"), b * 3 + q + 1)
                    if q < 2:
                        last = nc.vector.tensor_copy(PTS[:, 16 * q:16 * q + 16, :], PS[:, 4 + q, :].rearrange("p (n r) -> p n r", r=ROWS))
                    else:
                        nc.vector.tensor_copy(PTS[:, 32:37, :], PS[:, 6, 0:5 * ROWS].rearrange("p (n r) -> p n r", r=ROWS))
                        nc.vector.tensor_copy(PTS[0:NCS - P, 37, :], PS[0:NCS - P, 6, 5 * ROWS:6 * ROWS])
                        last = nc.vector.tensor_copy(PTS[0:DS, 38:40, :], PS[0:DS, 6, 6 * ROWS:8 * ROWS].rearrange("p (n r) -> p n r", r=ROWS))
                    last.then_inc(sem("pt_ev"), 1)
                dve.wait_ge(sem("sc_exp"), b * 6 + 6)
                tlk(b, 6, nc.vector.tensor_copy(gcur[:, :], grow[:, bass.ds(b, 1), :].rearrange("p o j -> p (o j)")))
                tlk(b, 7, nc.vector.tensor_reduce(smx[:, 2, 1:2], pmx[:, 1, :], AX.X, ALU.add))
                tlk(b, 8, nc.vector.reciprocal(smx[:, 3, 0:2], smx[:, 2, 0:2]))
                nc.vector.tensor_tensor(smx[:, 3, 0:1], smx[:, 3, 0:1], gcur[:, 2:3], ALU.mult)
                tlk(b, 9, nc.vector.tensor_tensor(smx[:, 3, 1:2], smx[:, 3, 1:2], gcur[:, 1:2], ALU.mult))
                dve.wait_ge(sem("pv_done"), b + 1)
                tlk(b, 10, nc.vector.tensor_scalar(osb, PS[0:ROWS, 7, 0:P], smx[:, 3, 0:1], None, ALU.mult))
                tlk(b, 11, nc.vector.scalar_tensor_tensor(out=osb, in0=PS[0:ROWS, 7, P:2 * P], scalar=smx[:, 3, 1:2], in1=osb,
                                                          op0=ALU.mult, op1=ALU.add))
                nc.vector.scalar_tensor_tensor(out=osb, in0=PS[0:ROWS, 7, 2 * P:3 * P], scalar=gcur[:, 0:1], in1=osb,
                                               op0=ALU.mult, op1=ALU.add).then_inc(sem("o_rows"), 1)

            def output(b):
                dve.wait_ge(sem("o_t"), b + 1)
                for g in range(G):
                    rows = slice(g * HD, (g + 1) * HD)
                    nc.vector.tensor_copy(MIXT[rows, R:2 * R, bass.ds(b * DS + LP, DS)],
                                          PS[rows, 7, 3 * P + g * R * DS:3 * P + (g + 1) * R * DS].rearrange("p (r q) -> p r q", r=R)).then_inc(sem("o_ev"), 1)

            def batch(b, waited):
                count = [0]

                def lk(ins):
                    count[0] += 1
                    ins.then_inc(sem("dve_step"), 1)
                    dve.wait_ge(sem("dve_step"), b * SPER + sbase + count[0])

                def seg_copy(u):
                    dve.wait_ge(sem("seg_t"), b * 16 + u + 1)
                    for h in range(2):
                        nc.vector.tensor_copy(seg_dst(u, h, 1), seg_src(u, h, 1)).then_inc(sem("seg_dve"), 1)

                def gelu_poly(c):
                    dve.wait_ge(sem("cmp_hx"), b * 2 + c + 1)
                    if c == 1:
                        dve.wait_ge(sem("cmp_k"), b + 1)
                    elif waited:
                        dve.wait_ge(sem("cmp_v"), b)
                    lk(nc.vector.tensor_tensor(hgx[:, :], HXS[:, :], HXS[:, :], ALU.mult))
                    lk(nc.vector.tensor_scalar(hgx[:, :], hgx[:, :], GELU_C, 1.0, ALU.mult, ALU.add))
                    nc.vector.tensor_tensor(hgx[:, :], hgx[:, :], HXS[:, :], ALU.mult).then_inc(sem("cmp_poly"), 1)

                def gelu_last(c):
                    dve.wait_ge(sem("cmp_tanh"), b * 2 + c + 1)
                    nc.vector.scalar_tensor_tensor(out=hgx[:, :], in0=hgx[:, :], scalar=1.0, in1=HXS[:, :], op0=ALU.add, op1=ALU.mult
                                                   ).then_inc(sem("cmp_g"), 1)

                def maximum(c0, w, q):
                    lk(nc.vector.tensor_reduce(smx[:, 0, q:q + 1], PSC[:, c0:c0 + w], AX.X, ALU.max))
                    nc.vector.tensor_scalar(smx[:, 1, q:q + 1], smx[:, 0, q:q + 1], -1.0, None, ALU.mult).then_inc(sem("sc_max"), 1)

                for u in range(9):
                    seg_copy(u)
                    if waited and u == 0:
                        value_rows(b - 1)
                    if waited and u < 4:
                        max_part(b - 1, u)
                if waited:
                    tail(b - 1)
                seg_copy(9)
                seg_copy(10)
                if waited:
                    output(b - 1)
                gelu_poly(0)
                seg_copy(11)
                seg_copy(12)
                gelu_last(0)
                seg_copy(13)
                seg_copy(14)
                seg_copy(15)
                dve.wait_ge(sem("sc_done"), b * 11 + 1)
                nc.vector.tensor_copy(PSC[:, C_CMP:C_CMP + NCS], PS[0:ROWS, 6, 0:NCS]).then_inc(sem("sc_ev"), 1)
                dve.wait_ge(sem("sc_ev"), b * 11 + 1)
                maximum(C_CMP, NCS, 2)
                dve.wait_ge(sem("sc_exp"), b * 6 + 1)
                lk(nc.vector.reciprocal(smx[:, 3, 2:3], smx[:, 2, 2:3]))
                nc.vector.tensor_scalar(PSC[:, C_CMP:C_CMP + NCS], PSC[:, C_CMP:C_CMP + NCS], smx[:, 3, 2:3], None, ALU.mult).then_inc(sem("pc_ready"), 1)
                gelu_poly(1)
                dve.wait_ge(sem("imp"), b + 1)
                lk(nc.vector.tensor_copy(impA[:, 4:4 + NCS], PS[0:ROWS, 5, 0:NCS]))
                lk(nc.vector.tensor_reduce(score[:, 0, :], impA[:, 4:4 + 4 * NB].rearrange("p (j n) -> p j n", n=4), AX.X, ALU.add))
                lk(nc.vector.tensor_tensor(score[:, 0, :], score[:, 0, :], impA[:, 3:3 + 4 * NB:4], ALU.add))
                lk(nc.vector.tensor_tensor(score[:, 0, :], score[:, 0, :], bpen[:, :], ALU.add))

                def pause():
                    nc.vector.tensor_copy(smx[:, 3, 0:1], smx[:, 3, 2:3])

                for n in range(2):
                    pause()
                    lk(nc.vector.max(top8[:, n, :], score[:, n, :]))
                    pause()
                    lk(nc.vector.match_replace(score[:, n + 1, :], top8[:, n, :], score[:, n, :], -3e38))
                lk(nc.vector.tensor_scalar(spen[:, :], score[:, 2, :], -1e38, NEG, ALU.is_gt, ALU.mult))
                for n in range(10):
                    dve.wait_ge(sem("sc_done"), b * 11 + 2 + n)
                    if n == 0:
                        last = nc.vector.tensor_tensor(PSC[:, 0:WIN], PS[0:ROWS, 2, :], wpen[:, 0:WIN], ALU.add)
                    elif n == 1:
                        last = nc.vector.tensor_tensor(PSC[:, C_XW:C_XW + 2 * DS], PS[0:ROWS, 3, 0:2 * DS], wpen[:, WIN:WIN + 2 * DS], ALU.add)
                    else:
                        last = nc.vector.tensor_tensor(
                            PSC[:, C_SLC + (n - 2) * 512:C_SLC + (n - 1) * 512].rearrange("p (t j e) -> p t j e", t=4, e=2),
                            PS[0:ROWS, 2 + n % 2, :].rearrange("p (t j e) -> p t j e", t=4, e=2),
                            spen[:, 0:NB - 1].unsqueeze(1).unsqueeze(3).to_broadcast([ROWS, 4, NB - 1, 2]), ALU.add)
                    last.then_inc(sem("sc_ev"), 1)
                    if n == 1:
                        dve.wait_ge(sem("sc_ev"), b * 11 + 3)
                        maximum(C_WIN, WIN + DS, 0)
                    if n == 4:
                        gelu_last(1)
                assert count[0] == SPER, count[0]

            dve.wait_ge(sem("grow_in"), 16 * NH)
            batch(0, False)
            with dve.Fori(1, DB) as b:
                batch(b, True)
            step[0] += SPER * DB
            value_rows(DB - 1)
            for q in range(4):
                max_part(DB - 1, q)
            tail(DB - 1)
            output(DB - 1)

            dve.sem_inc(sem("res_free"), 4)
            nc.vector.memset(xsum, 0.0).then_inc(sem("x_sum"), 1)
            dve.wait_ge(sem("x_alpha"), KD)
            for f in range(KD):
                dve.wait_ge(sem("weights_used"), 2 * S_O + f + 1)
                if f:
                    dve.wait_ge(sem("x_res"), f)
                ga = mod[:, 2, f, :]
                x = X[:, f, :]
                for lo, hi in ((0, HALF), (HALF, LP)):
                    nc.vector.scalar_tensor_tensor(out=x[:, lo:hi], in0=out_acc[f % 4][:, lo // HALF, 0:hi - lo], scalar=ga[:, 0:1], in1=x[:, lo:hi],
                                                   op0=ALU.mult, op1=ALU.add)
                t = rstd[:, 0:LS].rearrange("p (b q) -> p b q", q=DS)
                nc.vector.tensor_tensor(t, out_acc[f % 4][:, 1, LP - HALF:HALF].rearrange("p (b q) -> p b q", q=DS),
                                        ga[:, 1:NC].unsqueeze(2).to_broadcast([P, DB, DS]), ALU.mult).then_inc(sem("res_free"), 1)
                dve.wait_ge(sem("res_free"), f + 5)
                nc.vector.tensor_tensor(x[:, LP:NT], x[:, LP:NT], rstd[:, 0:LS], ALU.add).then_inc(sem("x_res"), 1)
                dve.wait_ge(sem("x_res"), f + 1)
                dve.wait_ge(sem("x_sum"), f + 1)
                nc.vector.tensor_tensor(xsum, xsum, x, ALU.add).then_inc(sem("x_sum"), 1)
            dve.wait_ge(sem("x_res"), KD)
            ln_dve(1, 3, lambda k: ada_row(N_ADA1 + N_IN + k, S_ADA3 + k, 6))
            mod_copy(0, N_ADA1 + N_IN + 4, 5, 0)
            dve.wait_ge(sem("mod_free"), 7)

            dve.sem_inc(sem("gate_free"), 1)
            dve.sem_inc(sem("h_ready"), 2)

            def hidden(i, n):
                for k in range(n):
                    dve.wait_ge(sem("gate_th"), i * RING + k + 1)
                    th = halves(SQ[:, k % 2, :])
                    nc.vector.scalar_tensor_tensor(out=th, in0=th, scalar=1.0, in1=dense[0], op0=ALU.add, op1=ALU.mult).then_inc(sem("gate_free"), 1)
                    dve.wait_ge(sem("gate_free"), i * RING + k + 2)
                    dve.wait_ge(sem("weights_used"), i * 8 + 2 * S_F1 + 2 * k + 2)
                    nc.vector.scalar_tensor_tensor(out=HT[:, bass.ds(i * RING + k, 1), :].rearrange("p o (h t) -> p (o h) t", h=2), in0=dense[1],
                                                   scalar=0.5, in1=th, op0=ALU.mult, op1=ALU.mult).then_inc(sem("h_ready"), 1)
            full = N_F1 // RING
            with dve.Fori(0, full) as i:
                hidden(i, RING)
            hidden(full, N_F1 - full * RING)

            dve.wait_ge(sem("x_alpha"), 2 * KD)
            dve.wait_ge(sem("weights_used"), 2 * S_F2)
            nc.vector.memset(xsum, 0.0).then_inc(sem("x_sum"), 1)
            with dve.Fori(0, KD // 2) as i:
                for f in range(2):
                    nc.vector.tensor_copy(gares[:, f, :], mod[:, 5, bass.ds(i * 2 + f, 1), :].rearrange("p o c -> p (o c)")).then_inc(sem("gares"), 1)
                    dve.wait_ge(sem("gares"), i * 2 + f + 1)
                    ga = gares[:, f, :]
                    dve.wait_ge(sem("weights_used"), i * 8 + 2 * S_F2 + 4 * (f + 1))
                    dve.wait_ge(sem("x_res"), i * 2 + KD + f)
                    x = X[:, bass.ds(i * 2 + f, 1), :].rearrange("p o t -> p (o t)")
                    for lo, hi in ((0, HALF), (HALF, LP)):
                        nc.vector.scalar_tensor_tensor(out=x[:, lo:hi], in0=dense[f][:, lo // HALF, 0:hi - lo], scalar=ga[:, 0:1], in1=x[:, lo:hi],
                                                       op0=ALU.mult, op1=ALU.add)
                    t = rstd[:, 0:LS].rearrange("p (b q) -> p b q", q=DS)
                    nc.vector.tensor_tensor(t, dense[f][:, 1, LP - HALF:HALF].rearrange("p (b q) -> p b q", q=DS),
                                            ga[:, 1:NC].unsqueeze(2).to_broadcast([P, DB, DS]), ALU.mult).then_inc(sem("res_free"), 1)
                    dve.wait_ge(sem("res_free"), i * 2 + KD + f + 5)
                    nc.vector.tensor_tensor(x[:, LP:NT], x[:, LP:NT], rstd[:, 0:LS], ALU.add).then_inc(sem("x_res"), 1)
                    dve.wait_ge(sem("x_res"), i * 2 + KD + f + 1)
                    dve.wait_ge(sem("x_sum"), i * 2 + KD + 2 + f)
                    nc.vector.tensor_tensor(xsum, xsum, x, ALU.add).then_inc(sem("x_sum"), 1)
            dve.wait_ge(sem("x_res"), 2 * KD)
            ln_dve(2, None)


_OUTS = [(P, KD, NT), (GH, DK, DV), (DB, GH, DK, DV), (LP, KVW), (LS, KVW), (LP, KVW), (LS, KVW), (LP, KVW), (DB, WIN, KVW)]


def kernel(**inputs):
    import numpy as np
    import concourse.bacc as bacc
    from concourse import mybir as mb
    from concourse.bass_utils import run_bass_kernel_spmd

    v = {k: np.asarray(x) for k, x in inputs.items()}

    def rows(m):
        return m.reshape(-1, KD, P).transpose(2, 1, 0)

    def tiles(w, per):
        k, f = w.shape
        return w.reshape(k // P, P, f // (P * per), per * P).transpose(2, 1, 0, 3).reshape(f // (P * per), P, -1)

    def vec(x):
        return x.reshape(-1, P).T

    w_in = v["w_in"][0]
    cut = np.cumsum([256, 256, 512, RANK, 512, 512, KVW, KVW, KVW])
    q_g, k_g, v_g, a_g, r_g, q_n, kc, ks, kw, g_n = np.split(w_in, cut, axis=1)
    q_n = q_n.reshape(D, G, R, HD).transpose(0, 2, 1, 3).reshape(D, -1)
    g_n = g_n.reshape(D, G, R, 3).transpose(0, 2, 1, 3).reshape(D, -1)
    w_main = np.concatenate([q_g, k_g, v_g, r_g, q_n, kc, ks, kw], axis=1)
    w_misc = np.concatenate([a_g, g_n], axis=1)
    w_o = v["w_o"][0]
    w_o = np.concatenate([w_o[:GH * DV], w_o[GH * DV:].reshape(G, R, HD, D).transpose(1, 0, 2, 3).reshape(-1, D)])
    f1 = v["w_ffn_in"][0].reshape(KD, P, 2, KF, P).transpose(3, 1, 0, 2, 4).reshape(KF, P, -1)
    f2 = v["w_ffn_out"][0].reshape(2, KF // 2, P, KD, P).transpose(3, 0, 2, 1, 4).reshape(2 * KD, P, -1)
    ins = {
        "x_t": rows(np.concatenate([v["x_prompt"].reshape(LP, D), v["x_sample"].reshape(LS, D)])),
        "c_t": rows(np.concatenate([v["c_prompt"], v["c_sample"]])),
        "w_ada": tiles(v["w_ada"][0], 2), "b_ada": vec(v["b_ada"][0]).reshape(P, 6, KD),
        "lnv": np.stack([vec(v[n].reshape(-1)) for n in ("ln_in_g", "ln_in_b", "ln1_g", "ln1_b", "ln2_g", "ln2_b")], 1),
        "w_in": tiles(w_main, 2), "w_misc": w_misc.reshape(KD, P, MISC).transpose(1, 0, 2).reshape(P, -1),
        "wa2": v["gla_w_a2"][0], "ba": vec(v["gla_b_a"][0]), "gng": v["gla_norm_g"][0].reshape(P, 1),
        "pe": v["cmp_pe"][0].reshape(2, JP, 2, 2, HD).transpose(2, 4, 3, 0, 1).reshape(P, 2, 2, JP),
        "w1": v["cmp_w1"][0].reshape(2, 2, JP, P, HID).transpose(3, 0, 1, 2, 4),
        "b1": v["cmp_b1"][0].T, "w2": v["cmp_w2"][0].transpose(1, 0, 2),
        "w_o": tiles(w_o, 2), "w_f1": f1, "w_f2": f2,
        "state": v["state_gla"][0].reshape(DB, 2, 2 * DK, DV).transpose(2, 1, 0, 3),
        "ptab": v["page_table"].T,
        "cmp": v["cache_cmp_kv"][0].reshape(-1, SPAN * KVW), "slc": v["cache_slc_kv"][0].reshape(-1, SPAN * KVW),
        "win": v["cache_win_kv"][0].reshape(DB, WIN, KVW),
    }
    nc = bacc.Bacc("TRN2", target_bir_lowering=False, num_devices=1, dynamic_dma_scratch_size=4096)
    arrays, aps = {}, {}
    for name, x in ins.items():
        x = np.ascontiguousarray(x)
        arrays[f"in_{name}_dram"] = x
        aps[name] = nc.dram_tensor(f"in_{name}_dram", x.shape, mb.dt.from_np(x.dtype), kind="ExternalInput").ap()
    outs = [nc.dram_tensor(f"out_{i}_dram", s, F32, kind="ExternalOutput").ap() for i, s in enumerate(_OUTS)]
    build(nc, aps, outs)
    res = run_bass_kernel_spmd(nc, [arrays], core_ids=[0]).results[0]
    y, gp, gs, cp, c_s, slp, sls, wp, ws = (res[f"out_{i}_dram"] for i in range(len(_OUTS)))
    y = y.transpose(2, 1, 0).reshape(NT, D)
    kv = (2, G, HD)
    return (y[:LP].reshape(1, LP, D), y[LP:].reshape(DB, DS, D), gp.reshape(1, 1, GH, DK, DV), gs.reshape(1, DB, GH, DK, DV),
            cp.reshape(1, 1, LP, *kv), c_s.reshape(1, DB, DS, *kv), slp.reshape(1, 1, LP, *kv), sls.reshape(1, DB, DS, *kv),
            wp.reshape(1, 1, LP, *kv), ws.reshape(1, DB, WIN, *kv))
```
